# Optimizing a Trainium2 kernel written in Bass

```python
import jax, jax.numpy as jnp
from jax import lax
import numpy as np
import math

D_MODEL = 1024
BATCH = 1
SEQ = 256
DEPTH = 2

N_META = 16
D_CONV = 512
CONV_A_WIDTH = 3
DN_HEADS = 4
DN_HEAD_DIM = 128
DN_DIM = DN_HEADS * DN_HEAD_DIM
DN_CONV_WIDTH = 4
DN_CHUNK = 64
D_MIX = D_CONV + DN_DIM
IN_DIM = 3 * D_CONV + 4 * DN_DIM + 2 * DN_HEADS
SWA_HEADS = 16
SWA_KV_HEADS = 4
SWA_HEAD_DIM = 64
SWA_WINDOW = 128
SWA_BLOCK = 128
D_FF = 2816
FFN_CONV_WIDTH = 3
EPS = 1e-6
N_EVEN = (DEPTH + 1) // 2
N_ODD = DEPTH // 2


def rms_norm(x, w):
    xf = x.astype(jnp.float32)
    y = xf * lax.rsqrt(jnp.mean(xf * xf, -1, keepdims=True) + EPS)
    return (y * w.astype(jnp.float32)).astype(x.dtype)

def l2_norm(x):
    return x * lax.rsqrt(jnp.sum(x * x, -1, keepdims=True) + EPS)

def causal_dwconv(x, w):
    k = w.shape[0]
    return lax.conv_general_dilated(
        x, w[:, None, :].astype(x.dtype), window_strides=(1,), padding=((k - 1, 0),),
        dimension_numbers=('NWC', 'WIO', 'NWC'), feature_group_count=x.shape[-1])

def gated_delta_rule(q, k, v, beta, g):
    q, k, v, beta, g = (t.astype(jnp.float32) for t in (q, k, v, beta, g))
    b, l, h, dk = q.shape
    dv = v.shape[-1]
    c = DN_CHUNK
    n = l // c

    def chunks(t):
        t = t.reshape((b, n, c, h) + t.shape[3:])
        return jnp.moveaxis(t, 3, 1)

    q, k, v, beta, g = chunks(q), chunks(k), chunks(v), chunks(beta), chunks(g)
    decay = jnp.cumsum(g, -1)
    diff = decay[..., :, None] - decay[..., None, :]
    idx = jnp.arange(c)
    strict = idx[:, None] > idx[None, :]
    incl = idx[:, None] >= idx[None, :]
    dmask = jnp.exp(jnp.where(incl, diff, -jnp.inf))
    kk = jnp.einsum('bhnid,bhnjd->bhnij', k, k)
    a_strict = jnp.where(strict, beta[..., None] * kk * dmask, 0.0)
    t_mat = a_strict + jnp.eye(c, dtype=jnp.float32)
    rhs = jnp.concatenate([v * beta[..., None], k * (beta * jnp.exp(decay))[..., None]], -1)
    sol = lax.linalg.triangular_solve(t_mat, rhs, left_side=True, lower=True, unit_diagonal=True)
    u = sol[..., :dv]
    w = sol[..., dv:]
    qk = jnp.einsum('bhnid,bhnjd->bhnij', q, k) * dmask
    q_dec = q * jnp.exp(decay)[..., None]
    k_dec = k * jnp.exp(decay[..., -1:] - decay)[..., None]
    g_last = jnp.exp(decay[..., -1])

    def step(s, inp):
        u_n, w_n, qk_n, qd_n, kd_n, gl_n = inp
        v_new = u_n - jnp.einsum('bhcd,bhde->bhce', w_n, s)
        o = jnp.einsum('bhcd,bhde->bhce', qd_n, s) + jnp.einsum('bhij,bhje->bhie', qk_n, v_new)
        s = s * gl_n[..., None, None] + jnp.einsum('bhcd,bhce->bhde', kd_n, v_new)
        return s, o

    xs = tuple(jnp.moveaxis(t, 2, 0) for t in (u, w, qk, q_dec, k_dec, g_last))
    s0 = jnp.zeros((b, h, dk, dv), jnp.float32)
    _, o = lax.scan(step, s0, xs)
    return jnp.transpose(o, (1, 0, 3, 2, 4)).reshape(b, l, h, dv)

def even_mixer(h, w_in, conv_a_w, dn_conv_w, a_log, dt_bias, dn_norm_w, w_out):
    b, l, _ = h.shape
    p = h @ w_in
    sizes = [D_CONV, D_CONV, D_CONV, 3 * DN_DIM, DN_DIM, DN_HEADS, DN_HEADS]
    splits = [sum(sizes[:i + 1]) for i in range(len(sizes) - 1)]
    a_gate_in, a_gate_out, a_h, qkv, z, beta_raw, alpha_raw = jnp.split(p, splits, -1)
    y_a = a_gate_out * causal_dwconv(a_gate_in * a_h, conv_a_w)
    qkv = jax.nn.silu(causal_dwconv(qkv, dn_conv_w))
    q, k, v = jnp.split(qkv, 3, -1)
    hd = (b, l, DN_HEADS, DN_HEAD_DIM)
    q = l2_norm(q.reshape(hd).astype(jnp.float32)) * (DN_HEAD_DIM ** -0.5)
    k = l2_norm(k.reshape(hd).astype(jnp.float32))
    v = v.reshape(hd).astype(jnp.float32)
    beta = jax.nn.sigmoid(beta_raw.astype(jnp.float32))
    g = -jnp.exp(a_log.astype(jnp.float32)) * jax.nn.softplus(
        alpha_raw.astype(jnp.float32) + dt_bias.astype(jnp.float32))
    pad = (-N_META) % DN_CHUNK
    padw = lambda t: jnp.pad(t, ((0, 0), (pad, 0)) + ((0, 0),) * (t.ndim - 2))
    o = gated_delta_rule(padw(q), padw(k), padw(v), padw(beta), padw(g))[:, pad:]
    o = rms_norm(o, dn_norm_w) * jax.nn.silu(z.reshape(hd).astype(jnp.float32))
    y_b = o.reshape(b, l, DN_DIM).astype(h.dtype)
    return jnp.concatenate([y_a, y_b], -1) @ w_out

def sink_softmax(logits, sink):
    m = jnp.maximum(jnp.max(logits, -1, keepdims=True), sink)
    e = jnp.exp(logits - m)
    return e / (jnp.sum(e, -1, keepdims=True) + jnp.exp(sink - m))

def swa_mixer(h, wq, wk, wv, q_norm_w, k_norm_w, sinks, wo):
    b, l, _ = h.shape
    kv, grp, d = SWA_KV_HEADS, SWA_HEADS // SWA_KV_HEADS, SWA_HEAD_DIM
    q = rms_norm((h @ wq).reshape(b, l, kv, grp, d), q_norm_w) * (d ** -0.5)
    k = rms_norm((h @ wk).reshape(b, l, kv, d), k_norm_w)
    v = (h @ wv).reshape(b, l, kv, d)
    sink = sinks.astype(jnp.float32).reshape(kv, grp)
    qm, qr = q[:, :N_META], q[:, N_META:]
    km, kr = k[:, :N_META], k[:, N_META:]
    vm, vr = v[:, :N_META], v[:, N_META:]
    sm = jnp.einsum('bikgd,bjkd->bkgij', qm, km).astype(jnp.float32)
    mmask = jnp.tril(jnp.ones((N_META, N_META), bool))
    pm = sink_softmax(jnp.where(mmask, sm, -jnp.inf), sink[None, :, :, None, None])
    om = jnp.einsum('bkgij,bjkd->bikgd', pm.astype(v.dtype), vm).reshape(b, N_META, SWA_HEADS * d)
    s_real = l - N_META
    nb = s_real // SWA_BLOCK
    qb = qr.reshape(b, nb, SWA_BLOCK, kv, grp, d)
    kb = kr.reshape(b, nb, SWA_BLOCK, kv, d)
    vb = vr.reshape(b, nb, SWA_BLOCK, kv, d)
    band = lambda t: jnp.concatenate(
        [jnp.concatenate([jnp.zeros_like(t[:, :1]), t[:, :-1]], 1), t], 2)
    kband, vband = band(kb), band(vb)
    s_meta = jnp.einsum('bnikgd,bjkd->bnkgij', qb, km).astype(jnp.float32)
    s_band = jnp.einsum('bnikgd,bnjkd->bnkgij', qb, kband).astype(jnp.float32)
    i = jnp.arange(SWA_BLOCK)[:, None]
    j = jnp.arange(2 * SWA_BLOCK)[None, :]
    n = jnp.arange(nb)[:, None, None]
    rel = i + SWA_BLOCK - j
    valid = (rel >= 0) & (rel < SWA_WINDOW) & (n * SWA_BLOCK - SWA_BLOCK + j >= 0)
    s_band = jnp.where(valid[None, :, None, None], s_band, -jnp.inf)
    p = sink_softmax(jnp.concatenate([s_meta, s_band], -1), sink[None, None, :, :, None, None])
    p = p.astype(v.dtype)
    orr = (jnp.einsum('bnkgim,bmkd->bnikgd', p[..., :N_META], vm)
           + jnp.einsum('bnkgij,bnjkd->bnikgd', p[..., N_META:], vband))
    orr = orr.reshape(b, s_real, SWA_HEADS * d)
    return jnp.concatenate([om, orr], 1) @ wo

def conv_ffn(h, w_up, conv_w, w_down):
    gate, val = jnp.split(h @ w_up, 2, -1)
    gate = causal_dwconv(gate, conv_w)
    return (jax.nn.silu(gate) * val) @ w_down

def first_inputs(seed: int = 0) -> dict:
    key = jax.random.key(seed)
    ks = jax.random.split(key, 24)
    nrm = lambda k, s, scale: jax.random.normal(k, s, jnp.float32) * scale
    gain = lambda k, s: 1.0 + 0.05 * jax.random.normal(k, s, jnp.float32)
    dt = jnp.exp(jax.random.uniform(ks[7], (N_EVEN, DN_HEADS), jnp.float32, np.log(1e-3), np.log(1e-1)))
    return {
        "x": nrm(ks[0], (BATCH, SEQ, D_MODEL), 1.0),
        "meta_tokens": nrm(ks[1], (N_META, D_MODEL), 1.0),
        "attn_norm_w": gain(ks[2], (DEPTH, D_MODEL)),
        "ffn_norm_w": gain(ks[3], (DEPTH, D_MODEL)),
        "mix_w_in": nrm(ks[4], (N_EVEN, D_MODEL, IN_DIM), D_MODEL ** -0.5),
        "conv_a_w": nrm(ks[5], (N_EVEN, CONV_A_WIDTH, D_CONV), CONV_A_WIDTH ** -0.5),
        "dn_conv_w": nrm(ks[6], (N_EVEN, DN_CONV_WIDTH, 3 * DN_DIM), DN_CONV_WIDTH ** -0.5),
        "dn_a_log": jnp.log(jax.random.uniform(ks[8], (N_EVEN, DN_HEADS), jnp.float32, 1.0, 16.0)),
        "dn_dt_bias": dt + jnp.log(-jnp.expm1(-dt)),
        "dn_norm_w": gain(ks[9], (N_EVEN, DN_HEAD_DIM)),
        "mix_w_out": nrm(ks[10], (N_EVEN, D_MIX, D_MODEL), D_MIX ** -0.5),
        "swa_wq": nrm(ks[11], (N_ODD, D_MODEL, SWA_HEADS * SWA_HEAD_DIM), D_MODEL ** -0.5),
        "swa_wk": nrm(ks[12], (N_ODD, D_MODEL, SWA_KV_HEADS * SWA_HEAD_DIM), D_MODEL ** -0.5),
        "swa_wv": nrm(ks[13], (N_ODD, D_MODEL, SWA_KV_HEADS * SWA_HEAD_DIM), D_MODEL ** -0.5),
        "swa_q_norm_w": gain(ks[14], (N_ODD, SWA_HEAD_DIM)),
        "swa_k_norm_w": gain(ks[15], (N_ODD, SWA_HEAD_DIM)),
        "swa_sinks": nrm(ks[16], (N_ODD, SWA_HEADS), 0.5),
        "swa_wo": nrm(ks[17], (N_ODD, SWA_HEADS * SWA_HEAD_DIM, D_MODEL), (SWA_HEADS * SWA_HEAD_DIM) ** -0.5),
        "ffn_w_up": nrm(ks[18], (DEPTH, D_MODEL, 2 * D_FF), D_MODEL ** -0.5),
        "ffn_conv_w": nrm(ks[19], (DEPTH, FFN_CONV_WIDTH, D_FF), FFN_CONV_WIDTH ** -0.5),
        "ffn_w_down": nrm(ks[20], (DEPTH, D_FF, D_MODEL), D_FF ** -0.5),
    }

def first_block(x, meta_tokens, attn_norm_w, ffn_norm_w, mix_w_in, conv_a_w, dn_conv_w, dn_a_log,
              dn_dt_bias, dn_norm_w, mix_w_out, swa_wq, swa_wk, swa_wv, swa_q_norm_w, swa_k_norm_w,
              swa_sinks, swa_wo, ffn_w_up, ffn_conv_w, ffn_w_down):
    b = x.shape[0]
    meta = jnp.broadcast_to(meta_tokens[None].astype(x.dtype), (b, N_META, D_MODEL))
    h = jnp.concatenate([meta, x], 1)
    for layer in range(DEPTH):
        i = layer // 2
        hn = rms_norm(h, attn_norm_w[layer])
        if layer % 2 == 0:
            mix = even_mixer(hn, mix_w_in[i], conv_a_w[i], dn_conv_w[i], dn_a_log[i],
                             dn_dt_bias[i], dn_norm_w[i], mix_w_out[i])
        else:
            mix = swa_mixer(hn, swa_wq[i], swa_wk[i], swa_wv[i], swa_q_norm_w[i],
                            swa_k_norm_w[i], swa_sinks[i], swa_wo[i])
        h = h + mix.astype(h.dtype)
        ff = conv_ffn(rms_norm(h, ffn_norm_w[layer]), ffn_w_up[layer], ffn_conv_w[layer], ffn_w_down[layer])
        h = h + ff.astype(h.dtype)
    return h[:, N_META:]


N_HEADS = 16
HEAD_DIM = D_MODEL // N_HEADS
D_FF_2 = 4 * D_MODEL
N_MIXERS = 2
N_A_LAYERS = (DEPTH + 1) // 2
N_B_LAYERS = DEPTH // 2
NUM_BUCKETS = 32
MAX_DISTANCE = 128
MOBA_BLOCK = 256
MOBA_TOPK = 3
MOBA_Q_CHUNK = 64
DSA_Q_LORA = 256
DSA_KV_LORA = 256
IDX_HEADS = 8
IDX_DIM = 64
DSA_TOPK_MAX = 256
DSA_Q_CHUNK = 128
DSA_IN_DIM = DSA_Q_LORA + DSA_KV_LORA + IDX_DIM + IDX_HEADS
NEG = -1e30


def rms_norm_2(x, g):
    x32 = x.astype(jnp.float32)
    y = x32 * lax.rsqrt(jnp.mean(x32 * x32, axis=-1, keepdims=True) + EPS)
    return y.astype(x.dtype) * g

def rel_bucket(dist):
    n = jnp.maximum(dist, 0)
    exact = NUM_BUCKETS // 2
    nf = jnp.maximum(n, 1).astype(jnp.float32)
    large = exact + (jnp.log(nf / exact) / math.log(MAX_DISTANCE / exact) * (NUM_BUCKETS - exact)).astype(jnp.int32)
    large = jnp.minimum(large, NUM_BUCKETS - 1)
    return jnp.where(n < exact, n, large)

def moba_attention(h, w_qkv, w_o, bias_table):
    B, S, _ = h.shape
    H, Dh, BLK, QC = N_HEADS, HEAD_DIM, MOBA_BLOCK, MOBA_Q_CHUNK
    q, k, v = jnp.split(h @ w_qkv, 3, axis=-1)
    q = q.reshape(B, S, H, Dh).transpose(0, 2, 1, 3)
    k = k.reshape(B, S, H, Dh).transpose(0, 2, 1, 3)
    v = v.reshape(B, S, H, Dh).transpose(0, 2, 1, 3)
    n_blk = -(-S // BLK)
    pad = ((0, 0), (0, 0), (0, n_blk * BLK - S), (0, 0))
    kb = jnp.pad(k, pad).reshape(B, H, n_blk, BLK, Dh)
    vb = jnp.pad(v, pad).reshape(B, H, n_blk, BLK, Dh)
    k_mean = jnp.mean(kb.astype(jnp.float32), axis=3)
    gate = jnp.einsum('bhsd,bhnd->bhsn', q.astype(jnp.float32), k_mean)
    n_past = jnp.arange(S) // BLK
    past = jnp.arange(n_blk)[None, :] < n_past[:, None]
    gate = jnp.where(past[None, None], gate, NEG)
    k_sel = max(1, min(MOBA_TOPK, n_blk - 1))
    _, sel = lax.top_k(gate, k_sel)
    sel = sel.astype(jnp.int32)

    n_ch = S // QC

    def to_chunks(a):
        a = a.reshape(B, H, n_ch, QC, *a.shape[3:])
        a = jnp.moveaxis(a, 2, 1)
        return a.reshape(B * n_ch, H, QC, *a.shape[4:])

    q_c, sel_c = to_chunks(q), to_chunks(sel)
    b_idx = jnp.repeat(jnp.arange(B, dtype=jnp.int32), n_ch)
    c_idx = jnp.tile(jnp.arange(n_ch, dtype=jnp.int32), B)
    head_ids = jnp.arange(H)
    scale = HEAD_DIM ** -0.5

    def step(args):
        qc, selc, b, c = args
        t = c * QC + jnp.arange(QC, dtype=jnp.int32)
        j_own = (c * QC) // BLK
        kbb = lax.dynamic_index_in_dim(kb, b, 0, keepdims=False)
        vbb = lax.dynamic_index_in_dim(vb, b, 0, keepdims=False)
        k_g = kbb[head_ids[:, None, None], selc]
        v_g = vbb[head_ids[:, None, None], selc]
        k_own = lax.dynamic_index_in_dim(kbb, j_own, 1, keepdims=False)
        v_own = lax.dynamic_index_in_dim(vbb, j_own, 1, keepdims=False)
        qf = qc.astype(jnp.float32)
        l_sel = jnp.einsum('hqd,hqnjd->hqnj', qf, k_g.astype(jnp.float32)) * scale
        pos_sel = selc[..., None] * BLK + jnp.arange(BLK, dtype=jnp.int32)
        b_sel = bias_table[rel_bucket(t[None, :, None, None] - pos_sel), head_ids[:, None, None, None]].astype(jnp.float32)
        slot_ok = jnp.arange(k_sel)[None, :] < (t // BLK)[:, None]
        l_sel = jnp.where(slot_ok[None, :, :, None], l_sel + b_sel, NEG).reshape(H, QC, k_sel * BLK)
        l_own = jnp.einsum('hqd,hkd->hqk', qf, k_own.astype(jnp.float32)) * scale
        d_own = t[:, None] - (j_own * BLK + jnp.arange(BLK, dtype=jnp.int32))[None, :]
        b_own = jnp.moveaxis(bias_table[rel_bucket(d_own)].astype(jnp.float32), -1, 0)
        l_own = jnp.where((d_own >= 0)[None], l_own + b_own, NEG)
        p = jax.nn.softmax(jnp.concatenate([l_sel, l_own], axis=-1), axis=-1)
        p_sel = p[..., :k_sel * BLK].reshape(H, QC, k_sel, BLK)
        p_own = p[..., k_sel * BLK:]
        o = (jnp.einsum('hqnj,hqnjd->hqd', p_sel, v_g.astype(jnp.float32))
             + jnp.einsum('hqk,hkd->hqd', p_own, v_own.astype(jnp.float32)))
        return o.astype(qc.dtype)

    o = lax.map(step, (q_c, sel_c, b_idx, c_idx))
    o = o.reshape(B, n_ch, H, QC, Dh).transpose(0, 1, 3, 2, 4).reshape(B, S, H * Dh)
    return o @ w_o

def dsa_attention(h, w_in, g_q, g_kv, w_uq, w_qi, w_uk, w_uv, w_o, bias_table):
    B, S, _ = h.shape
    H, Dh, QC = N_HEADS, HEAD_DIM, DSA_Q_CHUNK
    proj = h @ w_in
    c_q, c_kv, k_idx, w_idx = jnp.split(proj, [DSA_Q_LORA, DSA_Q_LORA + DSA_KV_LORA, DSA_Q_LORA + DSA_KV_LORA + IDX_DIM], axis=-1)
    c_q = rms_norm_2(c_q, g_q)
    c_kv = rms_norm_2(c_kv, g_kv)
    q_nope = (c_q @ w_uq).reshape(B, S, H, Dh)
    q_idx = (c_q @ w_qi).reshape(B, S, IDX_HEADS, IDX_DIM)
    w_idx = w_idx.astype(jnp.float32) * (IDX_HEADS ** -0.5 * IDX_DIM ** -0.5)
    top_k = min(DSA_TOPK_MAX, S // 4)
    n_ch = S // QC

    def to_chunks(a):
        return jnp.moveaxis(a.reshape(B, n_ch, QC, *a.shape[2:]), 1, 0)

    k_idx32 = k_idx.astype(jnp.float32)
    key_pos = jnp.arange(S, dtype=jnp.int32)
    b_ids = jnp.arange(B)[:, None, None]
    scale = HEAD_DIM ** -0.5

    def step(args):
        qn, qi, wi, c = args
        t = c * QC + jnp.arange(QC, dtype=jnp.int32)
        rel = jax.nn.relu(jnp.einsum('bqhd,bsd->bqhs', qi.astype(jnp.float32), k_idx32))
        score = jnp.einsum('bqh,bqhs->bqs', wi, rel)
        score = jnp.where((key_pos[None, :] <= t[:, None])[None], score, NEG)
        _, idx = lax.top_k(score, top_k)
        valid = idx <= t[None, :, None]
        c_sel = c_kv[b_ids, idx].astype(jnp.float32)
        q_lat = jnp.einsum('bqhd,hdc->bqhc', qn.astype(jnp.float32), w_uk.astype(jnp.float32))
        logits = jnp.einsum('bqhc,bqkc->bhqk', q_lat, c_sel) * scale
        bias = jnp.moveaxis(bias_table[rel_bucket(t[None, :, None] - idx)].astype(jnp.float32), -1, 1)
        logits = jnp.where(valid[:, None], logits + bias, NEG)
        p = jax.nn.softmax(logits, axis=-1)
        o_lat = jnp.einsum('bhqk,bqkc->bqhc', p, c_sel)
        o = jnp.einsum('bqhc,hcd->bqhd', o_lat, w_uv.astype(jnp.float32))
        return o.astype(qn.dtype)

    o = lax.map(step, (to_chunks(q_nope), to_chunks(q_idx), to_chunks(w_idx), jnp.arange(n_ch, dtype=jnp.int32)))
    o = jnp.moveaxis(o, 0, 1).reshape(B, S, H * Dh)
    return o @ w_o

def sq_relu_mlp(h, w_up, w_down):
    return jnp.square(jax.nn.relu(h @ w_up)) @ w_down

def second_inputs(seed: int = 0) -> dict:
    key = jax.random.key(seed)
    ks = jax.random.split(key, 20)
    D, H, Dh = D_MODEL, N_HEADS, HEAD_DIM
    nrm = lambda k, shape, s: jax.random.normal(k, shape, jnp.float32) * s
    gain = lambda k, shape: 1.0 + 0.05 * jax.random.normal(k, shape, jnp.float32)
    return {
        "x": nrm(ks[0], (BATCH, SEQ, D), 1.0),
        "rel_bias": nrm(ks[1], (NUM_BUCKETS, H), 0.2),
        "ln_attn": gain(ks[2], (DEPTH, D)),
        "ln_mlp": gain(ks[3], (DEPTH, D)),
        "moba_w_qkv": nrm(ks[4], (N_A_LAYERS, D, 3 * D), D ** -0.5),
        "moba_w_o": nrm(ks[5], (N_A_LAYERS, D, D), D ** -0.5),
        "dsa_w_in": nrm(ks[6], (N_B_LAYERS, D, DSA_IN_DIM), D ** -0.5),
        "dsa_g_q": gain(ks[7], (N_B_LAYERS, DSA_Q_LORA)),
        "dsa_g_kv": gain(ks[8], (N_B_LAYERS, DSA_KV_LORA)),
        "dsa_w_uq": nrm(ks[9], (N_B_LAYERS, DSA_Q_LORA, H * Dh), DSA_Q_LORA ** -0.5),
        "dsa_w_qi": nrm(ks[10], (N_B_LAYERS, DSA_Q_LORA, IDX_HEADS * IDX_DIM), DSA_Q_LORA ** -0.5),
        "dsa_w_uk": nrm(ks[11], (N_B_LAYERS, H, Dh, DSA_KV_LORA), DSA_KV_LORA ** -0.5),
        "dsa_w_uv": nrm(ks[12], (N_B_LAYERS, H, DSA_KV_LORA, Dh), DSA_KV_LORA ** -0.5),
        "dsa_w_o": nrm(ks[13], (N_B_LAYERS, H * Dh, D), (H * Dh) ** -0.5),
        "mlp_w_up": nrm(ks[14], (DEPTH, D, D_FF_2), D ** -0.5),
        "mlp_w_down": nrm(ks[15], (DEPTH, D_FF_2, D), 0.5 * D_FF_2 ** -0.5),
        "final_norm": gain(ks[16], (D,)),
    }

def second_block(x, rel_bias, ln_attn, ln_mlp, moba_w_qkv, moba_w_o, dsa_w_in, dsa_g_q, dsa_g_kv,
              dsa_w_uq, dsa_w_qi, dsa_w_uk, dsa_w_uv, dsa_w_o, mlp_w_up, mlp_w_down, final_norm):
    for i in range(DEPTH):
        hn = rms_norm_2(x, ln_attn[i])
        j = i // N_MIXERS
        if i % N_MIXERS == 0:
            x = x + moba_attention(hn, moba_w_qkv[j], moba_w_o[j], rel_bias)
        else:
            x = x + dsa_attention(hn, dsa_w_in[j], dsa_g_q[j], dsa_g_kv[j], dsa_w_uq[j], dsa_w_qi[j],
                                  dsa_w_uk[j], dsa_w_uv[j], dsa_w_o[j], rel_bias)
        x = x + sq_relu_mlp(rms_norm_2(x, ln_mlp[i]), mlp_w_up[i], mlp_w_down[i])
    return rms_norm_2(x, final_norm)


def setup_inputs(seed=0):
    out = dict(first_inputs(seed))
    for name, value in second_inputs(seed + 1).items():
        if name != "x":
            out[name + "_2"] = value
    return out


def reference(
    x, meta_tokens, attn_norm_w, ffn_norm_w, mix_w_in, conv_a_w, dn_conv_w, dn_a_log,
    dn_dt_bias, dn_norm_w, mix_w_out, swa_wq, swa_wk, swa_wv, swa_q_norm_w, swa_k_norm_w,
    swa_sinks, swa_wo, ffn_w_up, ffn_conv_w, ffn_w_down, rel_bias_2, ln_attn_2, ln_mlp_2,
    moba_w_qkv_2, moba_w_o_2, dsa_w_in_2, dsa_g_q_2, dsa_g_kv_2, dsa_w_uq_2, dsa_w_qi_2,
    dsa_w_uk_2, dsa_w_uv_2, dsa_w_o_2, mlp_w_up_2, mlp_w_down_2, final_norm_2,
):
    x = first_block(
        x, meta_tokens, attn_norm_w, ffn_norm_w, mix_w_in, conv_a_w, dn_conv_w, dn_a_log,
        dn_dt_bias, dn_norm_w, mix_w_out, swa_wq, swa_wk, swa_wv, swa_q_norm_w, swa_k_norm_w,
        swa_sinks, swa_wo, ffn_w_up, ffn_conv_w, ffn_w_down,
    )
    return second_block(
        x, rel_bias_2, ln_attn_2, ln_mlp_2, moba_w_qkv_2, moba_w_o_2, dsa_w_in_2, dsa_g_q_2,
        dsa_g_kv_2, dsa_w_uq_2, dsa_w_qi_2, dsa_w_uk_2, dsa_w_uv_2, dsa_w_o_2, mlp_w_up_2,
        mlp_w_down_2, final_norm_2,
    )


_drawn_inputs = setup_inputs


def setup_inputs(seed=0):
    import zlib

    import numpy as np

    out = dict(_drawn_inputs(seed))
    spreads = {}
    factors = {'swa_q_norm_w': 5.555,
     'swa_k_norm_w': 5.458,
     'swa_sinks': 8.0,
     'dsa_g_q_2': 3.002,
     'dsa_g_kv_2': 4.969}
    for name, (base, spread) in spreads.items():
        noise = np.random.default_rng([zlib.crc32(name.encode()), seed]).standard_normal(out[name].shape)
        drawn = base * np.exp(spread * noise) if base else spread * noise
        out[name] = __import__('jax').numpy.asarray(drawn.astype(out[name].dtype))
    for name, factor in factors.items():
        out[name] = (out[name] * factor).astype(out[name].dtype)
    return out
```

```python
from contextlib import ExitStack

import numpy as np

import concourse.bass as bass
from concourse import mybir

F32 = mybir.dt.float32
F32R = mybir.dt.float32r
ALU = mybir.AluOpType
ACT = mybir.ActivationFunctionType
AX_X = mybir.AxisListType.X

P = 128
D = 1024
KD = D // P
META = 16
SEQ = 256
T = META + SEQ
DFF = 2816
DFF2 = 4096
GATES = DFF // P
EPS = 1e-6
NEG = -1e30
GONE = -3e38
TOPK = 64
HEADS = 16
HD = 64
BUCKETS = 32
CH = ((0, META), (META, P), (META + P, P))
KEYS = ((META, P), (META + P, P), (0, META))

LINEARS = (
    ("mix_in", 29, KD, 1, 1), ("mix_out", 8, KD, 1, 1),
    ("up0", 2 * GATES, KD, 1, 1), ("down0", 8, GATES, 2, 1),
    ("swa_in", 12, KD, 1, 1), ("swa_out", 8, KD, 1, 1),
    ("up1", 2 * GATES, KD, 1, 1), ("down1", 8, GATES, 2, 1),
    ("moba_in", 24, KD, 1, 1), ("moba_out", 8, KD, 1, 1),
    ("mlp_up0", DFF2 // P, KD, 1, 1), ("mlp_down0", 8, DFF2 // P, 4, 1),
    ("dsa_in", 6, KD, 1, 1), ("dsa_q", 12, 2, 1, 4), ("dsa_kv", 16, 2, 1, 4),
    ("dsa_out", 8, KD, 1, 1),
    ("mlp_up1", DFF2 // P, KD, 1, 1), ("mlp_down1", 8, DFF2 // P, 4, 1),
)
RING = 4
BANKS = 4
AHEAD = 3
SLOT = GATES // 2 * P

PARAMS = (("attn_w", 16), ("ffn_w", 16), ("conv_a", 12), ("dn_conv", 48), ("dn_norm", 1),
          ("q_norm", 1), ("k_norm", 1), ("sinks", 16), ("ffn_conv", 2 * 3 * GATES),
          ("ln_attn", 16), ("ln_mlp", 16), ("g_q", 2), ("g_kv", 2), ("final", 8),
          ("a_log", 1), ("dt_bias", 1), ("rel", HEADS))
VLEN = 3 * P
CONSTS = (("ident", P), ("ones", P), ("levels", 7 * P), ("strict", P), ("incl", P),
          ("head64", 40), ("head128", 15), ("onehot", VLEN), ("swa1", T), ("swa0", META + P),
          ("meta", META), ("causal", 2 * P), ("future", VLEN))


def columns(table):
    at, out = 0, {}
    for name, n in table:
        out[name] = (at, n)
        at += n
    return out, at


PARAM_AT, NPARAM = columns(PARAMS)
CONST_AT, NCONST = columns(CONSTS)


class Linear:

    def __init__(self, name, tiles, chunks, per_tile, per_piece, piece0, tile0):
        self.name, self.tiles, self.chunks = name, tiles, chunks
        self.per_tile, self.per_piece = per_tile, per_piece
        self.piece0, self.tile0 = piece0, tile0
        self.pieces = tiles * per_tile // per_piece
        self.width = chunks * per_piece // per_tile * P


def plan():
    out, piece, tile = {}, 0, 0
    for name, tiles, chunks, per_tile, per_piece in LINEARS:
        out[name] = Linear(name, tiles, chunks, per_tile, per_piece, piece, tile)
        piece += out[name].pieces
        tile += tiles
    return out, piece


LIN, NPIECES = plan()
WIDTHS = [lin.width for lin in LIN.values() for _ in range(lin.pieces)]
IN_UP = 3


def build(nc, x_t, weights, params_d, consts_d, rel_scratch, out_t, last=None, dump=None):
    ctx = ExitStack()
    with ctx:
        sems = {}

        def S(name):
            if name not in sems:
                sems[name] = ctx.enter_context(nc.semaphore(name))
            return sems[name]

        base = (nc.sbuf_base + 31) // 32 * 32
        words = (nc.sbuf_usable_end - base) // 4 // 8 * 8
        ctx.enter_context(nc.sbuf_tensor("slab", [P, words], F32))
        top, where = [0], {}

        def place(at, name, shape, dt=F32):
            n = 1
            for s in shape[1:]:
                n *= s
            assert at + n <= words, (name, at + n, words)
            return nc.alloc_sbuf_tensor_at(name, shape, dt, offset=base + 4 * at), at + (n + 7) // 8 * 8

        def sb(name, shape, dt=F32):
            at = top[0]
            t, top[0] = place(at, name, shape, dt)
            where[t.name] = at
            return t

        raw = sb("raw", [P, RING, SLOT])
        w_hi = sb("w_hi", [P, RING, SLOT], F32R)
        w_lo = sb("w_lo", [P, RING, SLOT], F32R)
        h = sb("h", [P, KD, T])
        x_at = top[0]
        x_hi = sb("x_hi", [P, KD, T], F32R)
        x_lo = sb("x_lo", [P, KD, T], F32R)
        y_hi = sb("y_hi", [P, KD, T], F32R)
        y_lo = sb("y_lo", [P, KD, T], F32R)
        prm = sb("prm", [P, NPARAM])
        cst = sb("cst", [P, NCONST])
        rstd = sb("rstd", [P, T])
        std = sb("std", [P, T])
        sq = sb("sq", [P, T])
        acc = sb("acc", [P, T])
        eps = sb("eps", [P, 1])
        gb = sb("gb", [P, 2, IN_UP + T])
        cb = sb("cb", [P, 2, T])
        sg = sb("sg", [P, 2, T])
        vr = sb("vr", [P, 2, T])
        av = sb("av", [P, 2, T])
        small = sb("small", [P, 64])
        relv = sb("relv", [HEADS, VLEN])
        u_at = top[0]
        u_end = words
        a_hi, at = place(u_at, "a_hi", [P, GATES, T], F32R)
        a_lo, _ = place(at, "a_lo", [P, GATES, T], F32R)
        m_hi, at = place(u_at, "m_hi", [P, DFF2 // P, SEQ], F32R)
        m_lo, _ = place(at, "m_lo", [P, DFF2 // P, SEQ], F32R)

        def U(specs, at):
            out = []
            for name, shape in specs:
                t, at = place(at, name, shape)
                out.append(t)
            assert at <= u_end, (specs[-1][0], at, u_end)
            return out

        def sb_alias(name, shape, over):
            return place(where[over.name], name, shape)[0]

        def C(name, n=P):
            a, w = CONST_AT[name]
            return cst[0:n, a:a + w]

        def prm_col(name, j=0, n=P):
            a = PARAM_AT[name][0] + j
            return prm[0:n, a:a + 1] if isinstance(a, int) else prm[0:n, bass.ds(a, 1)]

        bank = [ctx.enter_context(nc.psum_tensor(f"bank{i}", [P, 512], F32)) for i in range(8)]

        ident = C("ident")

        block = ctx.enter_context(nc.Block())
        landed = [S(f"landed{i}") for i in range(RING)]
        hi_ready = S("hi_ready")
        lo_ready = S("lo_ready")
        piece_used = S("piece_used")
        evac_done = S("evac_done")
        x_hi_ready, x_lo_ready = S("x_hi_ready"), S("x_lo_ready")
        y_hi_ready, y_lo_ready = S("y_hi_ready"), S("y_lo_ready")
        a_ready, a_hi_ready, a_lo_ready = S("a_ready"), S("a_hi_ready"), S("a_lo_ready")
        acc_done, ms_done, std_done, rstd_done = (S("acc_done"), S("ms_done"), S("std_done"),
                                                  S("rstd_done"))
        loaded = S("loaded")
        h_loaded = S("h_loaded")
        eps_set = S("eps_set")
        dve_own, act_own, pool_own = S("dve_own"), S("act_own"), S("pool_own")
        out_done = S("out_done")

        NORMS = {"mix_in": 0, "up0": 1, "swa_in": 2, "up1": 3, "moba_in": 4, "mlp_up0": 5,
                 "dsa_in": 6, "mlp_up1": 7, "final": 8}
        Y0 = {"mix_out": 0, "swa_out": 8, "moba_out": 16, "dsa_q": 24, "dsa_out": 28}
        A0 = {"down0": 0, "down1": GATES, "mlp_down0": 2 * GATES,
              "mlp_down1": 2 * GATES + DFF2 // P}
        PAIR0 = {"up0": 0, "up1": GATES}
        ACT0 = {"up0": 0, "up1": GATES, "mlp_up0": 2 * GATES, "mlp_up1": 2 * GATES + DFF2 // P}
        NORM_W = {"mix_in": ("attn_w", 0), "up0": ("ffn_w", 0), "swa_in": ("attn_w", 8),
                  "up1": ("ffn_w", 8), "moba_in": ("ln_attn", 0), "mlp_up0": ("ln_mlp", 0),
                  "dsa_in": ("ln_attn", 8), "mlp_up1": ("ln_mlp", 8)}
        RESID = {"mix_out": "up0", "down0": "swa_in", "swa_out": "up1", "down1": "moba_in",
                 "moba_out": "mlp_up0", "mlp_down0": "dsa_in", "dsa_out": "mlp_up1",
                 "mlp_down1": "final"}
        ORDER = [name for name, *_ in LINEARS]
        if last is not None:
            ORDER = ORDER[:ORDER.index(last) + 1]
        END_PIECE = LIN[ORDER[-1]].piece0 + LIN[ORDER[-1]].pieces
        SECOND = set(name for name, *_ in LINEARS[8:])

        def cols(name):
            return (META, SEQ) if name in SECOND or name == "down1" else (0, T)

        def inputs(name, c):
            a, n = cols(name)
            if name in NORMS:
                return x_hi[:, c, a:a + n], x_lo[:, c, a:a + n]
            if name in ("down0", "down1"):
                return a_hi[:, c, a:a + n], a_lo[:, c, a:a + n]
            if name in ("mlp_down0", "mlp_down1"):
                return m_hi[:, c, :], m_lo[:, c, :]
            if name == "dsa_kv":
                c += 2
            return y_hi[:, c, a:a + n], y_lo[:, c, a:a + n]

        def at_piece(g, i=0, step=0):
            assert step % RING == 0
            return g % RING, g // RING + 1 + i * (step // RING)

        fin, = U([("fin", [P, KD, SEQ])], u_at)

        def act_round(act, g, i=0, step=RING):
            if g >= END_PIECE:
                return
            slot, turn = at_piece(g, i, step)
            act.wait_ge(landed[slot], 16 * (g // RING + 1) + i * (16 * step // RING))
            if g >= RING:
                act.wait_ge(piece_used, g - RING + 1 + i * step)
            nc.scalar.activation(w_hi[:, slot, 0:WIDTHS[g]], raw[:, slot, 0:WIDTHS[g]],
                                 ACT.Copy).then_inc(hi_ready, 1)

        def dve_rest(dve, g, i=0, step=RING):
            if g >= END_PIECE:
                return
            slot, _ = at_piece(g, i, step)
            dve.wait_ge(hi_ready, g + 1 + i * step)
            nc.vector.tensor_tensor(w_lo[:, slot, 0:WIDTHS[g]], raw[:, slot, 0:WIDTHS[g]],
                                    w_hi[:, slot, 0:WIDTHS[g]].bitcast(F32),
                                    ALU.subtract).then_inc(lo_ready, 1)

        def wait_tile(eng, lin, t, i=0, step=0):
            pieces = (t // lin.per_piece + 1) * lin.per_tile
            eng.wait_ge(piece_used, lin.piece0 + pieces + i * (step * lin.per_tile // lin.per_piece))

        def tile_bank(lin, t):
            return bank[(lin.tile0 + t) % BANKS]

        def pe_tile(pe, lin, t, i=0, step=0, ready=None):
            a, n = cols(lin.name)
            out = tile_bank(lin, t)[:, 0:n]
            if lin.tile0 + t >= BANKS:
                pe.wait_ge(evac_done, lin.tile0 + t - BANKS + 1 + i * step)
            for q in range(lin.per_tile):
                g = lin.piece0 + t // lin.per_piece * lin.per_tile + q
                slot = g % RING
                pe.wait_ge(lo_ready, g + 1 + i * (step * lin.per_tile // lin.per_piece))
                k = lin.chunks // lin.per_tile
                for c in range(k):
                    w0 = (t % lin.per_piece * k + c) * P
                    whi, wlo = w_hi[:, slot, w0:w0 + P], w_lo[:, slot, w0:w0 + P]
                    chunk = q * k + c
                    if ready is not None:
                        ready(chunk)
                    xh, xl = inputs(lin.name, chunk)
                    end = chunk == lin.chunks - 1
                    nc.tensor.matmul(out, whi, xh, start=(chunk == 0), stop=False)
                    nc.tensor.matmul(out, whi, xl, start=False, stop=False)
                    mm = nc.tensor.matmul(out, wlo, xh, start=False, stop=end)
                if t % lin.per_piece == lin.per_piece - 1:
                    mm.then_inc(piece_used, 1)

        def norm_sum(pe, name):
            k = NORMS[name]
            a, n = (META, SEQ) if name in SECOND or name == "final" else (0, T)
            pe.wait_ge(acc_done, k + 1)
            nc.tensor.matmul(bank[4][:, 0:n], C("ones"), acc[:, a:a + n], start=True,
                             stop=True).then_inc(ms_done, 1)

        def pe_linear(pe, name):
            lin = LIN[name]

            def ready(c):
                if name in NORMS:
                    pe.wait_ge(x_lo_ready, 8 * NORMS[name] + c + 1)
                elif name in A0:
                    pe.wait_ge(a_lo_ready, A0[name] + c + 1)
                elif name == "dsa_kv":
                    pe.wait_ge(y_lo_ready, Y0["dsa_q"] + 2 + c + 1)
                else:
                    pe.wait_ge(y_lo_ready, Y0[name] + c + 1)

            for t in range(min(4, lin.tiles)):
                if name == "mix_in" and t == 0:
                    pe.wait_ge(loaded, 32)
                pe_tile(pe, lin, t, ready=ready if t == 0 else None)
                if t == 0 and name in NORMS:
                    norm_sum(pe, name)
            rounds = lin.tiles // 4 - 1
            if lin.per_piece == 1 and rounds > 0:
                with pe.Fori(0, rounds) as i:
                    for t in range(4):
                        pe_tile(pe, lin, 4 + t, i, 4)
                rest = range(4 * (rounds + 1), lin.tiles)
            else:
                rest = range(4, lin.tiles)
            for t in rest:
                pe_tile(pe, lin, t)

        def act_std(act, name):
            k = NORMS[name]
            n = SEQ if name in SECOND or name == "final" else T
            act.wait_ge(ms_done, k + 1)
            nc.scalar.activation(std[:, 0:n], bank[4][:, 0:n], ACT.Sqrt, bias=eps[:, 0:1],
                                 scale=1.0 / D).then_inc(std_done, 1)

        def dve_rstd(dve, name):
            k = NORMS[name]
            n = SEQ if name in SECOND or name == "final" else T
            dve.wait_ge(std_done, k + 1)
            nc.vector.reciprocal(rstd[:, 0:n], std[:, 0:n]).then_inc(rstd_done, 1)
            dve.wait_ge(rstd_done, k + 1)

        def norm_w(name, c):
            p, j = NORM_W[name]
            return prm_col(p, j + c)

        def act_x_hi(act, name, c):
            nc.scalar.activation(x_hi[:, c, :], h[:, c, :], ACT.Copy,
                                 scale=norm_w(name, c)).then_inc(x_hi_ready, 1)

        def dve_x_lo(dve, name, c):
            dve.wait_ge(x_hi_ready, 8 * NORMS[name] + c + 1)
            nc.vector.scalar_tensor_tensor(out=x_lo[:, c, :], in0=h[:, c, :], scalar=norm_w(name, c),
                                           in1=x_hi[:, c, :].bitcast(F32), op0=ALU.mult,
                                           op1=ALU.subtract).then_inc(x_lo_ready, 1)

        pool_count = [0]

        def pool_link(pool, ins):
            pool_count[0] += 1
            ins.then_inc(pool_own, 1)
            pool.wait_ge(pool_own, pool_count[0])

        def pool_squares(pool, c):
            if c == 0:
                ins = nc.gpsimd.tensor_tensor(acc[:], h[:, c, :], h[:, c, :], ALU.mult)
            else:
                pool_link(pool, nc.gpsimd.tensor_tensor(sq[:], h[:, c, :], h[:, c, :], ALU.mult))
                ins = nc.gpsimd.tensor_tensor(acc[:], acc[:], sq[:], ALU.add)
            if c == KD - 1:
                ins.then_inc(acc_done, 1)
            else:
                pool_link(pool, ins)

        dve_count, act_count = [0], [0]

        def dve_link(dve, ins):
            dve_count[0] += 1
            ins.then_inc(dve_own, 1)
            dve.wait_ge(dve_own, dve_count[0])

        def act_link(act, ins):
            act_count[0] += 1
            ins.then_inc(act_own, 1)
            act.wait_ge(act_own, act_count[0])

        def dve_resid(dve, name):
            lin = LIN[name]
            nxt = RESID[name]
            a, n = cols(name)
            for t in range(lin.tiles):
                for q in range(lin.per_tile):
                    dve_rest(dve, lin.piece0 + t * lin.per_tile + q + AHEAD)
                wait_tile(dve, lin, t)
                nc.vector.tensor_tensor(h[:, t, a:a + n], tile_bank(lin, t)[:, 0:n], h[:, t, a:a + n],
                                        ALU.add).then_inc(evac_done, 1)
                if t and nxt != "final":
                    dve_x_lo(dve, nxt, t - 1)
            if nxt != "final":
                dve_x_lo(dve, nxt, lin.tiles - 1)

        def act_resid(act, name):
            lin = LIN[name]
            for t in range(lin.tiles):
                for q in range(lin.per_tile):
                    act_round(act, lin.piece0 + t * lin.per_tile + q + AHEAD)
                act.wait_ge(evac_done, lin.tile0 + t + 1)
                if RESID[name] != "final":
                    act_x_hi(act, RESID[name], t)

        def pool_resid(pool, name):
            lin = LIN[name]
            for t in range(lin.tiles):
                pool.wait_ge(evac_done, lin.tile0 + t + 1)
                pool_squares(pool, t)

        def gated_slots(eng, name, slot_a, slot_b):
            for j in (0, 1):
                slot_a(j, 0)
                slot_b(j, 0)
            with eng.Fori(0, (GATES - 4) // 2) as i:
                for j in (2, 3):
                    slot_a(j, i)
                    slot_b(j, i)
            for j in (GATES - 2, GATES - 1):
                slot_a(j, 0)
                slot_b(j, 0)

        def conv_w(name, tap, j):
            return prm_col("ffn_conv", (0 if name == "up0" else 3 * GATES) + tap * GATES + j)

        def dve_gated(dve, name):
            lin = LIN[name]
            p0 = PAIR0[name]
            a0 = ACT0[name]

            def product(j, i):
                dve.wait_ge(S("silu_done"), p0 + j + 1 + 2 * i)
                dve.wait_ge(evac_done, lin.tile0 + 2 * j + 2 + 4 * i)
                nc.vector.tensor_tensor(av[:, j % 2, :], sg[:, j % 2, :], vr[:, j % 2, :],
                                        ALU.mult).then_inc(a_ready, 1)

            def low(j, i):
                dve.wait_ge(a_hi_ready, a0 + j + 1 + 2 * i)
                nc.vector.tensor_tensor(a_lo[:, j + 2 * i, :], av[:, j % 2, :],
                                        a_hi[:, j + 2 * i, :].bitcast(F32),
                                        ALU.subtract).then_inc(a_lo_ready, 1)

            def slot_a(j, i):
                dve_rest(dve, lin.piece0 + 2 * j + AHEAD, i, 4)
                if j == 0:
                    dve_rstd(dve, name)
                if j:
                    product(j - 1, i)
                wait_tile(dve, lin, 2 * j, i, 4)
                nc.vector.tensor_tensor(gb[:, j % 2, IN_UP:], tile_bank(lin, 2 * j)[:, 0:T], rstd[:],
                                        ALU.mult).then_inc(evac_done, 1)

            def slot_b(j, i):
                g = gb[:, j % 2, :]
                dve_rest(dve, lin.piece0 + 2 * j + 1 + AHEAD, i, 4)
                dve.wait_ge(S("tap_done"), p0 + j + 1 + 2 * i)
                nc.vector.scalar_tensor_tensor(out=cb[:, j % 2, :], in0=g[:, IN_UP - 1:IN_UP - 1 + T],
                                               scalar=conv_w(name, 1, j + 2 * i), in1=cb[:, j % 2, :],
                                               op0=ALU.mult, op1=ALU.add).then_inc(S("tap2_done"), 1)
                wait_tile(dve, lin, 2 * j + 1, i, 4)
                nc.vector.tensor_tensor(vr[:, j % 2, :], tile_bank(lin, 2 * j + 1)[:, 0:T], rstd[:],
                                        ALU.mult).then_inc(evac_done, 1)
                dve.wait_ge(S("tap2_done"), p0 + j + 1 + 2 * i)
                nc.vector.scalar_tensor_tensor(out=cb[:, j % 2, :], in0=g[:, IN_UP - 2:IN_UP - 2 + T],
                                               scalar=conv_w(name, 0, j + 2 * i), in1=cb[:, j % 2, :],
                                               op0=ALU.mult, op1=ALU.add).then_inc(S("conv_done"), 1)
                if j:
                    low(j - 1, i)

            gated_slots(dve, name, slot_a, slot_b)
            product(GATES - 1, 0)
            low(GATES - 1, 0)

        def act_gated(act, name):
            lin = LIN[name]
            p0 = PAIR0[name]
            a0 = ACT0[name]

            def high(j, i):
                act.wait_ge(a_ready, p0 + j + 1 + 2 * i)
                nc.scalar.activation(a_hi[:, j + 2 * i, :], av[:, j % 2, :],
                                     ACT.Copy).then_inc(a_hi_ready, 1)

            def slot_a(j, i):
                act_round(act, lin.piece0 + 2 * j + AHEAD, i, 4)
                if j == 0:
                    act_std(act, name)
                else:
                    silu(j - 1, i)

            def slot_b(j, i):
                act_round(act, lin.piece0 + 2 * j + 1 + AHEAD, i, 4)
                act.wait_ge(evac_done, lin.tile0 + 2 * j + 1 + 4 * i)
                nc.scalar.activation(cb[:, j % 2, :], gb[:, j % 2, IN_UP:], ACT.Copy,
                                     scale=conv_w(name, 2, j + 2 * i)).then_inc(S("tap_done"), 1)
                if j:
                    high(j - 1, i)

            def silu(j, i):
                act.wait_ge(S("conv_done"), p0 + j + 1 + 2 * i)
                nc.scalar.activation(sg[:, j % 2, :], cb[:, j % 2, :],
                                     ACT.Silu).then_inc(S("silu_done"), 1)

            gated_slots(act, name, slot_a, slot_b)
            silu(GATES - 1, 0)
            high(GATES - 1, 0)


        (qkv, zs, expb, decb, betab, a_t, qk_t, dm, bt, bv, braw, ba, g1, g2, g3, l2s, l2r, colsb,
         ecol, negc, dlast, kdc, glast) = U([
            ("qkv", [P, 12, T]), ("zs", [P, 4, T]), ("expb", [P, 4, T]), ("decb", [P, 4, T]),
            ("betab", [P, 4, T]), ("a_t", [P, 3, 512]), ("qk_t", [P, 3, 512]), ("dm", [P, 3, 512]),
            ("bt", [P, 3, 512]), ("bv", [P, 3, 512]), ("braw", [36, T]), ("ba", [36, T]),
            ("g1", [36, T]), ("g2", [36, T]), ("g3", [36, T]), ("l2s", [8, T]), ("l2r", [8, T]),
            ("colsb", [P, 3, 36]), ("ecol", [P, 3, 4]), ("negc", [P, 3, 4]), ("dlast", [P, 3, 4]),
            ("kdc", [P, 3, 4]), ("glast", [P, 3, 4])], u_at)
        squares_at = u_at + 12 * T + 4 * 4 * T
        sqb, _ = place(squares_at, "sqb", [P, 8, T])
        kd, _ = place(squares_at + 2 * 3 * 512, "kd", [P, 3, 512])
        oT, _ = place(u_at + 12 * T + 2 * 4 * T, "oT", [P, 4, T])
        pb, _ = place(u_at + 12 * T + 3 * 4 * T, "pb", [P, 2, 512])
        state, _ = place(squares_at + 3 * 3 * 512, "state", [P, 2, 4, P])
        xm, at = place(x_at, "xm", [P, 3, 512])
        xt, at = place(at, "xt", [P, 3, 512])
        rr, at = place(at, "rr", [P, 512])
        vn, _ = place(at, "vn", [P, 512])
        pb0, _ = place(squares_at + 5 * 3 * 512 + 3 * T, "pb0", [META, 4 * META])
        QKV = 12
        BA = 12
        Z0 = 13
        A0_TILE = 17

        def mix_slots(eng, slot):
            for t in range(4):
                slot(t, 0)
            with eng.Fori(0, QKV // 4 - 1) as i:
                for t in range(4, 8):
                    slot(t, i)

        def dn_w(tap, f):
            return prm_col("dn_conv", tap * QKV + f)

        INV_BANKS = {1: (bank[0], bank[5], bank[6]), 2: (bank[1], bank[7], bank[2]),
                     0: (bank[3], bank[4], bank[4])}
        LEVELS = {0: 4, 1: 7, 2: 7}
        INVERSE = [(level, n) for level in range(1, 8) for n in (1, 2, 0) if level <= LEVELS[n]]
        bt_ready = [S(f"bt_ready{n}") for n in range(3)]
        p_done = [S(f"p_done{n}") for n in range(3)]
        p_ready = [S(f"p_ready{n}") for n in range(3)]
        y_done = [S(f"y_done{n}") for n in range(3)]
        xt_ready = [S(f"xt_ready{n}") for n in range(3)]

        def by_head(ap):
            return ap.rearrange("p (h c) -> p h c", h=4)

        def yt_bank(n):
            c = CH[n][1]
            off = 4 * c if n == 0 else 0
            return INV_BANKS[n][2][:, off:off + 4 * c]

        def dve_mix(dve, name):
            lin = LIN[name]

            def conv(t, i):
                g = gb[:, t % 2, :]
                dve.wait_ge(S("mix_tap3"), t + 1 + 4 * i)
                for tap, done in ((2, S("mix_tap2")), (1, S("mix_tap1")), (0, S("mix_conv"))):
                    nc.vector.scalar_tensor_tensor(
                        out=cb[:, t % 2, :], in0=g[:, tap:tap + T], scalar=dn_w(tap, t + 4 * i),
                        in1=cb[:, t % 2, :], op0=ALU.mult, op1=ALU.add).then_inc(done, 1)
                    if tap:
                        dve.wait_ge(done, t + 1 + 4 * i)

            def slot(t, i):
                dve_rest(dve, lin.piece0 + t + AHEAD, i, 4)
                if t == 0:
                    dve_rstd(dve, name)
                if t:
                    conv(t - 1, i)
                wait_tile(dve, lin, t, i, 4)
                nc.vector.tensor_tensor(gb[:, t % 2, IN_UP:], tile_bank(lin, t)[:, 0:T], rstd[:],
                                        ALU.mult).then_inc(evac_done, 1)

            def plain(t, dst, n=P):
                wait_tile(dve, lin, t)
                nc.vector.tensor_tensor(dst, tile_bank(lin, t)[0:n, 0:T], rstd[0:n, :],
                                        ALU.mult).then_inc(evac_done, 1)

            mix_slots(dve, slot)
            dve_rest(dve, lin.piece0 + BA + AHEAD)
            plain(BA, braw[:, :], 36)
            conv(QKV - 1, 0)
            dve_rest(dve, lin.piece0 + Z0 + AHEAD)
            plain(Z0, zs[:, 0, :])
            dve.wait_ge(S("gates_act"), 1)
            dve_link(dve, nc.vector.tensor_scalar(g3[0:4, :], braw[0:4, :], prm_col("dt_bias", 0, 4), 0.0,
                                                  ALU.add, ALU.max))
            dve_link(dve, nc.vector.tensor_tensor(g3[0:4, :], g3[0:4, :], g2[0:4, :], ALU.add))
            dve_link(dve, nc.vector.tensor_scalar(g3[0:4, :], g3[0:4, :], small[0:4, 0:1], -1.0,
                                                  ALU.mult, ALU.mult))
            dve.wait_ge(S("cleared"), 2)
            for t0, c in CH:
                nc.vector.tensor_tensor_scan(ba[0:4, t0:t0 + c], C("ones", 4)[:, 0:1].to_broadcast([4, c]),
                                             g3[0:4, t0:t0 + c], 0.0, ALU.mult,
                                             ALU.add).then_inc(S("rows_ready"), 1)
            dve_link(dve, nc.vector.tensor_scalar(g1[32:36, :], g1[32:36, :], 1.0, None, ALU.add))
            nc.vector.reciprocal(ba[32:36, :], g1[32:36, :]).then_inc(S("rows_ready"), 1)
            for f in range(1, 4):
                dve_rest(dve, lin.piece0 + Z0 + f + AHEAD)
                plain(Z0 + f, zs[:, f, :])
            for j in range(4):
                t = A0_TILE + 3 * j
                dve_rest(dve, lin.piece0 + t + AHEAD)
                plain(t, vr[:, 0, :])
                dve_rest(dve, lin.piece0 + t + 1 + AHEAD)
                plain(t + 1, vr[:, 1, :])
                if j:
                    y_low(dve, "mix_out", j - 1, av[:, (j - 1) % 2, :])
                dve_rest(dve, lin.piece0 + t + 2 + AHEAD)
                plain(t + 2, sg[:, 0, :])
                dve.wait_ge(S("glu_tap"), j + 1)
                g = gb[:, j % 2, :]
                for tap in (1, 0):
                    dve_link(dve, nc.vector.scalar_tensor_tensor(
                        out=cb[:, j % 2, :], in0=g[:, 1 + tap:1 + tap + T],
                        scalar=prm_col("conv_a", tap * 4 + j), in1=cb[:, j % 2, :],
                        op0=ALU.mult, op1=ALU.add))
                dve.wait_ge(evac_done, lin.tile0 + t + 3)
                nc.vector.tensor_tensor(av[:, j % 2, :], cb[:, j % 2, :], sg[:, 0, :],
                                        ALU.mult).then_inc(S("y_ready"), 1)
            y_low(dve, "mix_out", 3, av[:, 1, :])

            dve.wait_ge(S("cols_ps"), 1)
            nc.vector.tensor_copy(colsb[0:META, 0, :], bank[6][0:META, 0:36]).then_inc(S("cols_ready"), 1)
            nc.vector.tensor_copy(colsb[:, 1:3, :], bank[6][:, 36:108].rearrange(
                "p (n k) -> p n k", n=2)).then_inc(S("cols_ready"), 1)
            for hd in range(4):
                dve.wait_ge(S("bc_done"), 4 + hd + 1)
                nc.vector.tensor_copy(betab[:, hd, :], bank[hd][:, 0:T]).then_inc(S("bc_read"), 1)
            dve.wait_ge(S("l2_std"), 1)
            nc.vector.reciprocal(l2r[:], l2s[:]).then_inc(S("l2_ready"), 1)
            dve.wait_ge(S("cols_ready"), 2)
            dve.wait_ge(S("decb_ready"), 4)
            for n, (t0, c) in enumerate(CH):
                for hd in range(4):
                    ins = nc.vector.tensor_scalar(dm[0:c, n, hd * c:(hd + 1) * c], decb[0:c, hd, t0:t0 + c],
                                                  colsb[0:c, n, hd:hd + 1], 0.0, ALU.subtract, ALU.min)
                ins.then_inc(S("diff_ready"), 1)
                nc.vector.tensor_copy(dlast[:, n, :], decb[:, :, t0 + c - 1]).then_inc(S("dlast_ready"), 1)
            dve.wait_ge(S("dlast_ready"), 3)
            nc.vector.tensor_tensor(kdc[:], dlast[:], colsb[:, :, 0:4], ALU.subtract).then_inc(
                S("dlast_ready"), 1)
            dve.wait_ge(S("exps_ready"), 1)
            nc.vector.scalar_tensor_tensor(out=negc[:], in0=ecol[:], scalar=-1.0, in1=colsb[:, :, 32:36],
                                           op0=ALU.mult, op1=ALU.mult).then_inc(S("negc_ready"), 1)
            for f in range(8):
                dve.wait_ge(S("bc_done"), 8 + f + 1)
                if f == 0:
                    dve.wait_ge(S("mix_silu"), QKV)
                nc.vector.scalar_tensor_tensor(
                    out=qkv[:, f, :], in0=qkv[:, f, :], scalar=P ** -0.5 if f < 4 else 1.0,
                    in1=bank[f % 4][:, 0:T], op0=ALU.mult, op1=ALU.mult).then_inc(S("bc_read"), 1)
            for n, (t0, c) in enumerate(CH):
                w = 4 * c
                dve.wait_ge(S("dm_ready"), n + 1)
                dve.wait_ge(S("gram_done"), 2 * n + 1)
                dve_link(dve, nc.vector.tensor_tensor(a_t[0:c, n, 0:w], bank[n][0:c, 0:w], dm[0:c, n, 0:w],
                                                      ALU.mult))
                a3 = a_t[0:c, n, 0:w].rearrange("p (h c) -> p h c", h=4)
                dve_link(dve, nc.vector.tensor_tensor(a3, a3, betab[0:c, :, t0:t0 + c], ALU.mult))
                nc.vector.tensor_tensor(a3, a3, C("strict", c)[:, 0:c].unsqueeze(1).to_broadcast([c, 4, c]),
                                        ALU.mult).then_inc(S("a_t_ready"), 1)
                dve.wait_ge(S("gram_done"), 2 * n + 2)
                dve_link(dve, nc.vector.tensor_tensor(qk_t[0:c, n, 0:w], bank[5 + n][0:c, 0:w],
                                                      dm[0:c, n, 0:w], ALU.mult))
                q3 = qk_t[0:c, n, 0:w].rearrange("p (h c) -> p h c", h=4)
                nc.vector.tensor_tensor(q3, q3, C("incl", c)[:, 0:c].unsqueeze(1).to_broadcast([c, 4, c]),
                                        ALU.mult).then_inc(S("qk_t_ready"), 1)
            for level, n in INVERSE:
                t0, c = CH[n]
                w = 4 * c
                if level == 1:
                    dve.wait_ge(bt_ready[n], 1)
                    nc.vector.tensor_tensor(by_head(xt[0:c, n, 0:w]),
                                            ident[0:c, 0:c].unsqueeze(1).to_broadcast([c, 4, c]),
                                            by_head(bt[0:c, n, 0:w]), ALU.subtract).then_inc(xt_ready[n], 1)
                    continue
                dve.wait_ge(y_done[n], level - 1)
                if level < LEVELS[n]:
                    nc.vector.tensor_tensor(xm[0:c, n, 0:w], xm[0:c, n, 0:w], INV_BANKS[n][1][0:c, 0:w],
                                            ALU.subtract).then_inc(S("x_ready"), 1)
                nc.vector.tensor_tensor(xt[0:c, n, 0:w], xt[0:c, n, 0:w], yt_bank(n)[0:c, :],
                                        ALU.subtract).then_inc(xt_ready[n], 1)
            dve.wait_ge(S("rows_read"), 6)
            dve.wait_ge(S("negc_ready"), 1)
            for n, (t0, c) in enumerate(CH):
                if n:
                    dve.wait_ge(S("ks_done"), n)
                    for hd in range(4):
                        hs = slice(hd * P, (hd + 1) * P)
                        ins = nc.vector.scalar_tensor_tensor(
                            out=rr[0:c, hs], in0=bank[0][0:c, hs], scalar=negc[0:c, n, hd:hd + 1],
                            in1=bv[0:c, n, hs], op0=ALU.mult, op1=ALU.add)
                    ins.then_inc(S("r_ready"), 1)
                if n < 2:
                    dve.wait_ge(S("su_done"), n + 1)
                    for hd in range(4):
                        hs = slice(hd * P, (hd + 1) * P)
                        if n == 0:
                            ins = nc.vector.tensor_copy(state[:, 0, hd, :], bank[3][:, hs])
                        else:
                            ins = nc.vector.scalar_tensor_tensor(
                                out=state[:, n, hd, :], in0=state[:, n - 1, hd, :], scalar=glast[:, n, hd:hd + 1],
                                in1=bank[3][:, hs], op0=ALU.mult, op1=ALU.add)
                    ins.then_inc(S("state_ready"), 1)
                    dve.wait_ge(S("state_ready"), n + 1)
            dve.wait_ge(S("o_ready"), 3)
            dve.wait_ge(S("z_ready"), 4)
            for hd in range(4):
                nc.vector.scalar_tensor_tensor(out=zs[:, hd, :], in0=oT[:, hd, :], scalar=prm_col("dn_norm"),
                                               in1=zs[:, hd, :], op0=ALU.mult,
                                               op1=ALU.mult).then_inc(S("oz_ready"), 1)
            dve.wait_ge(S("on_std"), 1)
            nc.vector.reciprocal(l2r[0:4, :], l2s[0:4, :]).then_inc(S("on_ready"), 1)
            dve.wait_ge(S("oz_ready"), 4)
            for hd in range(4):
                dve.wait_ge(S("on_bc"), hd + 1)
                nc.vector.tensor_tensor(zs[:, hd, :], zs[:, hd, :], bank[4 + hd][:, 0:T],
                                        ALU.mult).then_inc(S("y_ready"), 1)
            for hd in range(4):
                y_low(dve, "mix_out", 4 + hd, zs[:, hd, :])

        def y_low(dve, name, c, y, a=0, n=T):
            dve.wait_ge(y_hi_ready, Y0[name] + c + 1)
            nc.vector.tensor_tensor(y_lo[:, c, a:a + n], y, y_hi[:, c, a:a + n].bitcast(F32),
                                    ALU.subtract).then_inc(y_lo_ready, 1)

        def act_mix(act, name):
            lin = LIN[name]

            def silu(t, i):
                act.wait_ge(S("mix_conv"), t + 1 + 4 * i)
                nc.scalar.activation(qkv[:, t + 4 * i, :], cb[:, t % 2, :],
                                     ACT.Silu).then_inc(S("mix_silu"), 1)

            def slot(t, i):
                act_round(act, lin.piece0 + t + AHEAD, i, 4)
                if t == 0:
                    act_std(act, name)
                else:
                    tap3(t - 1, i)
                if t > 1:
                    silu(t - 2, i)

            def tap3(t, i):
                act.wait_ge(evac_done, lin.tile0 + t + 1 + 4 * i)
                if t > 1:
                    act.wait_ge(S("mix_silu"), t - 1 + 4 * i)
                nc.scalar.activation(cb[:, t % 2, :], gb[:, t % 2, IN_UP:], ACT.Copy,
                                     scale=dn_w(3, t + 4 * i)).then_inc(S("mix_tap3"), 1)

            mix_slots(act, slot)
            act_round(act, lin.piece0 + BA + AHEAD)
            tap3(QKV - 1, 0)
            silu(QKV - 2, 0)
            silu(QKV - 1, 0)
            act.wait_ge(evac_done, lin.tile0 + BA + 1)
            act_link(act, nc.scalar.activation(g1[0:4, :], braw[0:4, :], ACT.Abs,
                                               bias=prm_col("dt_bias", 0, 4)))
            act_link(act, nc.scalar.activation(g1[0:4, :], g1[0:4, :], ACT.Exp, scale=-1.0))
            nc.scalar.activation(g1[32:36, :], braw[32:36, :], ACT.Exp, scale=-1.0)
            nc.scalar.activation(small[0:4, 0:1], prm_col("a_log", 0, 4), ACT.Exp)
            nc.scalar.activation(g2[0:4, :], g1[0:4, :], ACT.Ln, bias=1.0).then_inc(S("gates_act"), 1)
            for f in range(4):
                act_round(act, lin.piece0 + Z0 + f + AHEAD)
                act.wait_ge(evac_done, lin.tile0 + Z0 + f + 1)
                nc.scalar.activation(zs[:, f, :], zs[:, f, :], ACT.Silu).then_inc(S("z_ready"), 1)
            for j in range(4):
                t = A0_TILE + 3 * j
                act_round(act, lin.piece0 + t + AHEAD)
                if j:
                    y_high(act, "mix_out", j - 1, av[:, (j - 1) % 2, :], j)
                act_round(act, lin.piece0 + t + 1 + AHEAD)
                act_round(act, lin.piece0 + t + 2 + AHEAD)
                act.wait_ge(S("glu_ready"), j + 1)
                nc.scalar.activation(cb[:, j % 2, :], gb[:, j % 2, IN_UP:], ACT.Copy,
                                     scale=prm_col("conv_a", 8 + j)).then_inc(S("glu_tap"), 1)
            y_high(act, "mix_out", 3, av[:, 1, :], 4)

            act.wait_ge(S("l2_sum"), 1)
            nc.scalar.activation(l2s[:], bank[5][0:8, 0:T], ACT.Sqrt, bias=eps[0:8, 0:1],
                                 scale=1.0).then_inc(S("l2_std"), 1)
            for hd in range(4):
                act.wait_ge(S("bc_done"), hd + 1)
                nc.scalar.activation(decb[:, hd, :], bank[hd][:, 0:T], ACT.Copy).then_inc(
                    S("decb_ready"), 1)
                nc.scalar.activation(expb[:, hd, :], bank[hd][:, 0:T], ACT.Exp).then_inc(
                    S("expb_ready"), 1)
            act.wait_ge(S("cols_ready"), 2)
            nc.scalar.activation(ecol[:], colsb[:, :, 0:4], ACT.Exp).then_inc(S("exps_ready"), 1)
            act.wait_ge(S("dlast_ready"), 3)
            nc.scalar.activation(glast[:], dlast[:], ACT.Exp).then_inc(S("exps_ready"), 1)
            act.wait_ge(S("dlast_ready"), 4)
            act_link(act, nc.scalar.activation(kdc[:], kdc[:], ACT.Exp))
            for n, (t0, c) in enumerate(CH):
                act.wait_ge(S("diff_ready"), n + 1)
                nc.scalar.activation(dm[0:c, n, 0:4 * c], dm[0:c, n, 0:4 * c],
                                     ACT.Exp).then_inc(S("dm_ready"), 1)
            act.wait_ge(S("qk_t_ready"), 3)
            for n, (t0, c) in enumerate(CH):
                act.wait_ge(S("rows_done"), 2 * n + 1)
                for hd in range(4):
                    hs = slice(hd * P, (hd + 1) * P)
                    ins = nc.scalar.activation(kd[0:c, n, hs], bank[3][0:c, hs], ACT.Copy,
                                               scale=kdc[0:c, n, hd:hd + 1])
                ins.then_inc(S("rows_read"), 1)
                act.wait_ge(S("rows_done"), 2 * n + 2)
                for hd in range(4):
                    hs = slice(hd * P, (hd + 1) * P)
                    ins = nc.scalar.activation(bv[0:c, n, hs], bank[4][0:c, hs], ACT.Copy,
                                               scale=colsb[0:c, n, 32 + hd:33 + hd])
                ins.then_inc(S("rows_read"), 1)
            for level, n in INVERSE:
                t0, c = CH[n]
                w = 4 * c
                act.wait_ge(p_done[n], level)
                dst = xm[0:c, n, 0:w] if level == 1 else p_of(n)[0:c, 0:w]
                nc.scalar.activation(dst, INV_BANKS[n][0][0:c, 0:w], ACT.Copy).then_inc(p_ready[n], 1)
            for n, (t0, c) in enumerate(CH):
                act.wait_ge(S("vn_done"), n + 1)
                nc.scalar.activation(vn[0:c, :], bank[1][0:c, :], ACT.Copy).then_inc(S("vn_ready"), 1)
                act.wait_ge(S("ot_done"), n + 1)
                nc.scalar.activation(oT[:, :, t0:t0 + c], bank[2][:, 0:4 * c].rearrange(
                    "p (h c) -> p h c", h=4), ACT.Copy).then_inc(S("o_ready"), 1)
            act.wait_ge(S("on_sum"), 1)
            nc.scalar.activation(l2s[0:4, :], bank[5][0:4, 0:T], ACT.Sqrt, bias=eps[0:4, 0:1],
                                 scale=1.0 / P).then_inc(S("on_std"), 1)
            for hd in range(4):
                y_high(act, "mix_out", 4 + hd, zs[:, hd, :], 5 + hd)

        def p_of(n):
            return pb0[:, :] if n == 0 else pb[:, n - 1, :]

        def y_high(act, name, c, y, count, a=0, n=T):
            act.wait_ge(S("y_ready"), count)
            nc.scalar.activation(y_hi[:, c, a:a + n], y, ACT.Copy).then_inc(y_hi_ready, 1)

        def pool_mix(pool, name):
            nc.gpsimd.memset(ba[:], 0.0).then_inc(S("cleared"), 1)
            nc.gpsimd.memset(colsb[:], 0.0).then_inc(S("cleared"), 1)
            for f in range(8):
                pool.wait_ge(S("mix_silu"), f + 1)
                nc.gpsimd.tensor_tensor(sqb[:, f, :], qkv[:, f, :], qkv[:, f, :],
                                        ALU.mult).then_inc(S("sqk_ready"), 1)
            for j in range(4):
                pool.wait_ge(evac_done, LIN[name].tile0 + A0_TILE + 3 * j + 2)
                nc.gpsimd.tensor_tensor(gb[:, j % 2, IN_UP:], vr[:, 0, :], vr[:, 1, :],
                                        ALU.mult).then_inc(S("glu_ready"), 1)
            pool.wait_ge(S("bc_read"), 8)
            pool.wait_ge(S("expb_ready"), 4)
            nc.gpsimd.tensor_tensor(expb[:], qkv[:, 0:4, :], expb[:], ALU.mult).then_inc(S("qd_ready"), 1)
            for level, n in INVERSE:
                t0, c = CH[n]
                w = 4 * c
                if level == 1:
                    pool.wait_ge(S("a_t_ready"), n + 1)
                elif level == 2:
                    pool.wait_ge(xt_ready[n], 1)
                else:
                    pool.wait_ge(p_done[n], level - 1)
                m = C("levels", c)[:, (level - 1) * P:(level - 1) * P + c]
                nc.gpsimd.tensor_tensor(by_head(bt[0:c, n, 0:w]), by_head(a_t[0:c, n, 0:w]),
                                        m.unsqueeze(1).to_broadcast([c, 4, c]),
                                        ALU.mult).then_inc(bt_ready[n], 1)
            pool.wait_ge(S("o_ready"), 3)
            nc.gpsimd.tensor_tensor(qkv[:, 8:12, :], oT[:], oT[:], ALU.mult).then_inc(S("osq_ready"), 1)

        def pe_mix(pe, name):
            pe_linear(pe, name)
            for f in range(8):
                pe.wait_ge(S("sqk_ready"), f + 1)
                mm = nc.tensor.matmul(bank[5][0:8, 0:T], C("head128")[:, 7 - f:15 - f], sqb[:, f, :],
                                      start=(f == 0), stop=(f == 7))
            mm.then_inc(S("l2_sum"), 1)
            pe.wait_ge(S("rows_ready"), 4)
            for n, (t0, c) in enumerate(CH):
                tr = nc.tensor.transpose(bank[6][0:c, n * 36:(n + 1) * 36], ba[0:36, t0:t0 + c],
                                         ident[0:36, 0:36])
            tr.then_inc(S("cols_ps"), 1)
            pe.wait_ge(evac_done, LIN[name].tile0 + LIN[name].tiles)
            for b in range(16):
                if 4 <= b < 8:
                    pe.wait_ge(S("expb_ready"), b - 4 + 1)
                if b >= 8:
                    pe.wait_ge(S("bc_read"), b - 8 + 1)
                    if b == 8:
                        pe.wait_ge(S("l2_ready"), 1)
                rows = 36 if b < 8 else 8
                col = (b, 32 + b - 4, b - 8)[min(b // 4, 2)]
                nc.tensor.matmul(bank[b % 4][:, 0:T], ident[0:rows, col:col + 1].to_broadcast([rows, P]),
                                 (ba if b < 8 else l2r)[0:rows, :], start=True,
                                 stop=True).then_inc(S("bc_done"), 1)
            pe.wait_ge(S("bc_read"), 12)
            for n, (t0, c) in enumerate(CH):
                for x, bk in ((4, bank[n]), (0, bank[5 + n])):
                    for hd in range(4):
                        k_ap = qkv[:, 4 + hd, t0:t0 + c]
                        mm = nc.tensor.matmul(bk[0:c, hd * c:(hd + 1) * c], k_ap,
                                              qkv[:, x + hd, t0:t0 + c], start=True, stop=True)
                    mm.then_inc(S("gram_done"), 1)
            for n, (t0, c) in enumerate(CH):
                for x, bk in ((4, bank[3]), (8, bank[4])):
                    if n:
                        pe.wait_ge(S("rows_read"), 2 * n - (1 if x == 4 else 0))
                    for hd in range(4):
                        tr = nc.tensor.transpose(bk[0:c, hd * P:(hd + 1) * P], qkv[:, x + hd, t0:t0 + c],
                                                 ident)
                    tr.then_inc(S("rows_done"), 1)
            pe.wait_ge(S("qk_t_ready"), 3)
            pe.wait_ge(S("rows_read"), 6)
            for level in range(1, 8):
                for n in (1, 2, 0):
                    if level > LEVELS[n]:
                        continue
                    t0, c = CH[n]
                    pbank = INV_BANKS[n][0]
                    if level == 1:
                        pe.wait_ge(xt_ready[n], 1)
                        for hd in range(4):
                            hs = slice(hd * c, (hd + 1) * c)
                            mm = nc.tensor.transpose(pbank[0:c, hs], xt[0:c, n, hs], ident[0:c, 0:c])
                    else:
                        pe.wait_ge(bt_ready[n], level)
                        if level == 2:
                            pe.wait_ge(p_ready[n], 1)
                        else:
                            pe.wait_ge(xt_ready[n], level - 1)
                        for hd in range(4):
                            hs = slice(hd * c, (hd + 1) * c)
                            mm = nc.tensor.matmul(pbank[0:c, hs], bt[0:c, n, hs], xm[0:c, n, hs],
                                                  start=True, stop=True)
                    mm.then_inc(p_done[n], 1)
                for n in (1, 2, 0):
                    if level == 1 or level > LEVELS[n]:
                        continue
                    t0, c = CH[n]
                    pe.wait_ge(p_ready[n], level)
                    p = p_of(n)
                    for hd in range(4):
                        hs = slice(hd * c, (hd + 1) * c)
                        if level < LEVELS[n]:
                            nc.tensor.matmul(INV_BANKS[n][1][0:c, hs], xt[0:c, n, hs], p[0:c, hs],
                                             start=True, stop=True)
                        mm = nc.tensor.matmul(yt_bank(n)[0:c, hs], p[0:c, hs], xt[0:c, n, hs],
                                              start=True, stop=True)
                    mm.then_inc(y_done[n], 1)
            for n, (t0, c) in enumerate(CH):
                if n:
                    pe.wait_ge(S("state_ready"), n)
                    for hd in range(4):
                        mm = nc.tensor.matmul(bank[0][0:c, hd * P:(hd + 1) * P], qkv[:, 4 + hd, t0:t0 + c],
                                              state[:, n - 1, hd, :], start=True, stop=True)
                    mm.then_inc(S("ks_done"), 1)
                    pe.wait_ge(S("r_ready"), n)
                pe.wait_ge(xt_ready[n], LEVELS[n])
                for hd in range(4):
                    hs = slice(hd * P, (hd + 1) * P)
                    mm = nc.tensor.matmul(bank[1][0:c, hs], xt[0:c, n, hd * c:(hd + 1) * c],
                                          rr[0:c, hs] if n else bv[0:c, n, hs], start=True, stop=True)
                mm.then_inc(S("vn_done"), 1)
                pe.wait_ge(S("vn_ready"), n + 1)
                if n < 2:
                    if n == 0:
                        pe.wait_ge(p_ready[0], LEVELS[0])
                    for hd in range(4):
                        hs = slice(hd * P, (hd + 1) * P)
                        mm = nc.tensor.matmul(bank[3][:, hs], kd[0:c, n, hs], vn[0:c, hs],
                                              start=True, stop=True)
                    mm.then_inc(S("su_done"), 1)
                if n:
                    pe.wait_ge(S("o_ready"), n)
                    pe.wait_ge(S("qd_ready"), 1)
                else:
                    pe.wait_ge(xt_ready[2], LEVELS[2])
                for hd in range(4):
                    out = bank[2][:, hd * c:(hd + 1) * c]
                    if n:
                        nc.tensor.matmul(out, state[:, n - 1, hd, :], expb[:, hd, t0:t0 + c], start=True,
                                         stop=False)
                    mm = nc.tensor.matmul(out, vn[0:c, hd * P:(hd + 1) * P],
                                          qk_t[0:c, n, hd * c:(hd + 1) * c], start=(n == 0), stop=True)
                mm.then_inc(S("ot_done"), 1)
            pe.wait_ge(S("osq_ready"), 1)
            for hd in range(4):
                mm = nc.tensor.matmul(bank[5][0:4, 0:T], C("head128")[:, 7 - hd:11 - hd],
                                      qkv[:, 8 + hd, :], start=(hd == 0), stop=(hd == 3))
            mm.then_inc(S("on_sum"), 1)
            pe.wait_ge(S("on_ready"), 1)
            for hd in range(4):
                nc.tensor.matmul(bank[4 + hd][:, 0:T], ident[0:4, hd:hd + 1].to_broadcast([4, P]),
                                 l2r[0:4, :], start=True, stop=True).then_inc(S("on_bc"), 1)

        def store_rounds(eng, lin, slot, rounds_static=1):
            t = 0
            for t in range(4 * rounds_static):
                slot(t, 0)
            rounds = lin.tiles // 4 - rounds_static
            if rounds > 0:
                with eng.Fori(0, rounds) as i:
                    for t in range(4 * rounds_static, 4 * rounds_static + 4):
                        slot(t, i)
            for t in range(4 * (rounds_static + rounds), lin.tiles):
                slot(t, 0)

        def dve_store(dve, name, dst, scaled=0):
            lin = LIN[name]
            n = cols(name)[1]

            def slot(t, i):
                dve_rest(dve, lin.piece0 + t + AHEAD, i, 4)
                if t == 0:
                    dve_rstd(dve, name)
                wait_tile(dve, lin, t, i, 4)
                if t < scaled:
                    nc.vector.scalar_tensor_tensor(out=dst[:, t + 4 * i, :], in0=tile_bank(lin, t)[:, 0:n],
                                                   scalar=HD ** -0.5, in1=rstd[:, 0:n], op0=ALU.mult,
                                                   op1=ALU.mult).then_inc(evac_done, 1)
                else:
                    nc.vector.tensor_tensor(dst[:, t + 4 * i, :], tile_bank(lin, t)[:, 0:n],
                                            rstd[:, 0:n], ALU.mult).then_inc(evac_done, 1)

            store_rounds(dve, lin, slot, 2 if scaled else 1)

        def act_store(act, name, scaled=0):
            lin = LIN[name]

            def slot(t, i):
                act_round(act, lin.piece0 + t + AHEAD, i, 4)
                if t == 0:
                    act_std(act, name)

            store_rounds(act, lin, slot, 2 if scaled else 1)

        attended = {}

        class Attend:

            def __init__(self, name, y, wa, wb, q, k, v, bias_a, bias_b, cuts_a, cuts_b, tiles):
                self.name, self.y, self.wa, self.wb = name, y, wa, wb
                self.q, self.k, self.v = q, k, v
                self.bias_a, self.bias_b = bias_a, bias_b
                self.cuts_a, self.cuts_b = cuts_a, cuts_b
                self.sm, self.pt, self.st = tiles
                self.sink = name == "swa"
                signals = (("scores", 1), ("max", 2), ("negmax", 1), ("exp", 3 if self.sink else 2),
                           ("den", 1 if self.sink else 0), ("rec", 1), ("p", 2), ("turned", 1),
                           ("pt", 4 if self.sink else 1), ("o", 1))
                self.s = {k: S(f"att_{k}") for k, _ in signals}
                self.before = {k: attended.get(k, 0) for k, _ in signals}
                for k, per_head in signals:
                    attended[k] = self.before[k] + per_head * HEADS

            def wait(self, eng, signal, n):
                eng.wait_ge(self.s[signal], self.before[signal] + n)

        def att_pe(pe, at, before=None):
            s = at.s
            for step in range(HEADS + 3):
                u = step
                if u < HEADS:
                    if u >= 4:
                        at.wait(pe, "max", 2 * (u - 4) + 2)
                    r = slice(HD * (u % 2), HD * (u % 2) + HD)
                    nc.tensor.matmul(bank[u % 4][:, 0:at.wa], at.q(u, r, 1), at.k(u, r, 1),
                                     start=True, stop=True)
                    nc.tensor.matmul(bank[u % 4][:, at.wa:at.wa + at.wb], at.q(u, r, 0), at.k(u, r, 0),
                                     start=True, stop=True).then_inc(s["scores"], 1)
                if before is not None and step == 1:
                    before(pe)
                u = step - 2
                if 0 <= u < HEADS:
                    at.wait(pe, "p", 2 * u + 2)
                    if u:
                        at.wait(pe, "pt", pt_count(at, u))
                    for ba_, cuts, base_ in ((4, at.cuts_a, 0), (5 if at.sink else 4, at.cuts_b,
                                                                0 if at.sink else 2 * P)):
                        for j, (c0, c, _) in enumerate(cuts):
                            tr = nc.tensor.transpose(bank[ba_][0:c, base_ + j * P:base_ + (j + 1) * P],
                                                     at.sm[:, u % 3, c0:c0 + c], ident)
                    tr.then_inc(s["turned"], 1)
                u = step - 3
                if 0 <= u < HEADS:
                    r = slice(HD * (u % 2), HD * (u % 2) + HD)
                    ob = bank[6 + u // 2 % 2]
                    at.wait(pe, "pt", pt_count(at, u + 1))
                    if u % 2 == 0 and u >= 4:
                        pe.wait_ge(y_lo_ready, Y0[at.y] + u // 2 - 1)
                    off = META if at.sink else 0
                    if at.sink:
                        if u == 0:
                            pe.wait_ge(S("meta_pt"), 1)
                        nc.tensor.matmul(ob[r, 0:META], at.v(u, 2, META), ptm[:, META * u:META * (u + 1)],
                                         start=True, stop=True)
                    for cuts, base_, q0 in ((at.cuts_b, 3 * P if at.sink else 2 * P, off),
                                            (at.cuts_a, 0, off + P)):
                        for j, (c0, c, chunk) in enumerate(cuts):
                            mm = nc.tensor.matmul(ob[r, q0:q0 + P], at.v(u, chunk, c),
                                                  at.pt[0:c, u % 2, base_ + j * P:base_ + (j + 1) * P],
                                                  start=(j == 0), stop=(j == len(cuts) - 1))
                    mm.then_inc(s["o"], 1)

        def pt_count(at, heads):
            return heads * (4 if at.sink else 1)

        def att_dve(dve, at, rests=(), extra=None):
            s = at.s
            rests = list(rests)
            for step in range(HEADS + 5):
                u = step
                if u < HEADS:
                    if u >= 3:
                        at.wait(dve, "turned", u - 2)
                    at.wait(dve, "scores", u + 1)
                    if extra is not None:
                        extra(dve, u)
                    for x, (c0, w, bias) in enumerate(((0, at.wa, at.bias_a(u)),
                                                       (at.wa, at.wb, at.bias_b(u)))):
                        nc.vector.tensor_tensor_reduce(
                            out=at.sm[:, u % 3, c0:c0 + w], in0=bank[u % 4][:, c0:c0 + w], in1=bias,
                            scale=1.0, scalar=GONE, op0=ALU.add, op1=ALU.max,
                            accum_out=at.st[:, u, x:x + 1]).then_inc(s["max"], 1)
                    at.wait(dve, "max", 2 * u + 2)
                    sink = prm_col("sinks", u) if at.sink else GONE
                    nc.vector.tensor_scalar(at.st[:, u, 2:4], at.st[:, u, 0:2], sink, -1.0, ALU.max,
                                            ALU.mult).then_inc(s["negmax"], 1)
                u = step - 1
                if 0 <= u < HEADS:
                    at.wait(dve, "exp", (3 if at.sink else 2) * (u + 1))
                    den = at.st[:, u, 4:6]
                    if at.sink:
                        nc.vector.tensor_tensor(den, den, at.st[:, u, 6:8], ALU.add).then_inc(s["den"], 1)
                        at.wait(dve, "den", u + 1)
                    nc.vector.reciprocal(at.st[:, u, 8:10], den).then_inc(s["rec"], 1)
                    at.wait(dve, "rec", u + 1)
                    for x, (c0, w) in enumerate(((0, at.wa), (at.wa, at.wb))):
                        nc.vector.tensor_scalar(at.sm[:, u % 3, c0:c0 + w], at.sm[:, u % 3, c0:c0 + w],
                                                at.st[:, u, 8 + x:9 + x], None,
                                                ALU.mult).then_inc(s["p"], 1)
                u = step - 5
                if u > 0 and u % 2 == 1:
                    o_low(dve, at, u // 2)

        def o_cols(at):
            return (0, T) if at.sink else (META, SEQ)

        def o_low(dve, at, t):
            a, n = o_cols(at)
            c = Y0[at.y] + t
            dve.wait_ge(y_hi_ready, c + 1)
            nc.vector.tensor_tensor(y_lo[:, t, a:a + n], bank[6 + t % 2][:, 0:n],
                                    y_hi[:, t, a:a + n].bitcast(F32), ALU.subtract).then_inc(y_lo_ready, 1)

        def att_act(act, at):
            s = at.s
            a, n = o_cols(at)
            for step in range(HEADS + 4):
                u = step
                if u < HEADS:
                    at.wait(act, "negmax", u + 1)
                    for x, (c0, w) in enumerate(((0, at.wa), (at.wa, at.wb))):
                        nc.scalar.activation(at.sm[:, u % 3, c0:c0 + w], at.sm[:, u % 3, c0:c0 + w],
                                             ACT.Exp, bias=at.st[:, u, 2 + x:3 + x],
                                             accum_out=at.st[:, u, 4 + x:5 + x]).then_inc(s["exp"], 1)
                    if at.sink:
                        nc.scalar.activation(at.st[:, u, 6:8], at.st[:, u, 2:4], ACT.Exp,
                                             bias=prm_col("sinks", u)).then_inc(s["exp"], 1)
                u = step - 2
                if 0 <= u < HEADS:
                    at.wait(act, "turned", u + 1)
                    if at.sink:
                        copies = ((P, 0, 4, 0, 2 * P), (META, 2 * P, 4, 2 * P, P), (P, 3 * P, 5, 0, P),
                                  (META, 4 * P, 5, P, P))
                    else:
                        copies = ((P, 0, 4, 0, 3 * P),)
                    for rows, dst, bk, src, w in copies:
                        nc.scalar.activation(at.pt[0:rows, u % 2, dst:dst + w], bank[bk][0:rows, src:src + w],
                                             ACT.Copy).then_inc(s["pt"], 1)
                u = step - 3
                if u > 0 and u % 2 == 1:
                    o_high(act, at, u // 2)

        def o_high(act, at, t):
            a, n = o_cols(at)
            at.wait(act, "o", 2 * t + 2)
            nc.scalar.activation(y_hi[:, t, a:a + n], bank[6 + t % 2][:, 0:n], ACT.Copy).then_inc(y_hi_ready, 1)

        qs, sqs, vrow, sm_s, pt_s, st_s, sel20, hs20, hr20, smm, ptm, mst = U([
            ("qs", [P, 12, T]), ("sqs", [P, 10, T]), ("vrow", [P, 3, 256]), ("sm_s", [P, 3, 416]),
            ("pt_s", [P, 2, 640]), ("st_s", [P, HEADS, 10]), ("sel20", [20, 20 * HD]), ("hs20", [20, T]),
            ("hr20", [20, T]), ("smm", [META, 256]), ("ptm", [META, 256]), ("mst", [META, 4, HEADS])], u_at)
        swa = Attend(
            "swa", "swa_out", T, META + P,
            lambda u, r, g: qs[r, u // 2, META + P * g:META + P * (g + 1)],
            lambda u, r, g: qs[r, 8 + u // 8, 0:T] if g else qs[r, 8 + u // 8, 0:META + P],
            lambda u, chunk, c: vrow[0:c, chunk, (2 * (u // 8) + u % 2) * HD:(2 * (u // 8) + u % 2) * HD + HD],
            lambda u: C("swa1"), lambda u: C("swa0"),
            ((META, P, 0), (META + P, P, 1), (0, META, 2)),
            ((T + META, P, 0), (T, META, 2)), (sm_s, pt_s, st_s))

        def dve_swa(dve, name):
            sel_ins = nc.vector.tensor_copy(sel20[:].rearrange("p (a b) -> p a b", b=HD),
                                            ident[0:20, 0:20].unsqueeze(2).to_broadcast([20, 20, HD]))
            sel_ins.then_inc(S("sel_ready"), 1)
            nc.vector.tensor_scalar(small[:, 1:2], prm_col("q_norm"), HD ** -0.5, None,
                                    ALU.mult).then_inc(S("qw_ready"), 1)
            dve_store(dve, name, qs)
            dve.wait_ge(S("hs_ready"), 1)
            nc.vector.reciprocal(hr20[:], hs20[:]).then_inc(S("hr_ready"), 1)
            dve.wait_ge(S("qw_ready"), 1)
            dve.wait_ge(evac_done, LIN[name].tile0 + 12)
            for f in range(10):
                dve.wait_ge(S("hn_done"), f + 1)
                nc.vector.scalar_tensor_tensor(
                    out=qs[:, f, :], in0=qs[:, f, :], scalar=small[:, 1:2] if f < 8 else prm_col("k_norm"),
                    in1=bank[f % 4][:, 0:T], op0=ALU.mult, op1=ALU.mult).then_inc(S("qk_ready"), 1)
            m3 = smm[:].rearrange("p (u k) -> p u k", u=HEADS)
            dve.wait_ge(S("meta_scores"), 1)
            halves = smm[:].rearrange("p (t x k) -> p t x k", x=2, k=META)
            for x in range(2):
                dve_link(dve, nc.vector.tensor_tensor(
                    halves[:, :, x, :], bank[7 - x][0:META, 0:P].rearrange("p (t k) -> p t k", k=META),
                    C("meta", META).unsqueeze(1).to_broadcast([META, HEADS // 2, META]), ALU.add))
            dve_link(dve, nc.vector.tensor_reduce(mst[:, 0, :], m3, AX_X, ALU.max))
            sinks = prm[0:META, PARAM_AT["sinks"][0]:PARAM_AT["sinks"][0] + HEADS]
            dve_link(dve, nc.vector.tensor_tensor(mst[:, 0, :], mst[:, 0, :], sinks, ALU.max))
            nc.vector.tensor_tensor(mst[:, 1, :], sinks, mst[:, 0, :], ALU.subtract).then_inc(S("meta_m"), 1)
            nc.vector.tensor_tensor(m3, m3, mst[:, 0, :].unsqueeze(2).to_broadcast([META, HEADS, META]),
                                    ALU.subtract).then_inc(S("meta_m"), 1)
            dve.wait_ge(S("meta_e"), 2)
            dve_link(dve, nc.vector.tensor_reduce(mst[:, 2, :], m3, AX_X, ALU.add))
            dve_link(dve, nc.vector.tensor_tensor(mst[:, 2, :], mst[:, 2, :], mst[:, 1, :], ALU.add))
            dve_link(dve, nc.vector.reciprocal(mst[:, 3, :], mst[:, 2, :]))
            nc.vector.tensor_tensor(m3, m3, mst[:, 3, :].unsqueeze(2).to_broadcast([META, HEADS, META]),
                                    ALU.mult).then_inc(S("meta_p"), 1)
            dve.wait_ge(S("meta_turned"), 1)
            nc.vector.tensor_copy(ptm[:], bank[7][0:META, 256:512]).then_inc(S("meta_pt"), 1)
            att_dve(dve, swa)

        def act_swa(act, name):
            act_store(act, name)
            act.wait_ge(S("hn_sum"), 1)
            nc.scalar.activation(hs20[:], bank[5][0:20, 0:T], ACT.Sqrt, bias=eps[0:20, 0:1],
                                 scale=1.0 / HD).then_inc(S("hs_ready"), 1)
            for j, (t0, c) in enumerate(KEYS):
                act.wait_ge(S("vt_done"), j + 1)
                nc.scalar.activation(vrow[0:c, j, :], bank[5 + (j + 1) % 3][0:c, 0:256],
                                     ACT.Copy).then_inc(S("vrow_ready"), 1)
            act.wait_ge(S("meta_m"), 2)
            nc.scalar.activation(mst[:, 1, :], mst[:, 1, :], ACT.Exp).then_inc(S("meta_e"), 1)
            nc.scalar.activation(smm[:], smm[:], ACT.Exp).then_inc(S("meta_e"), 1)
            att_act(act, swa)

        def pool_swa(pool, name):
            for f in range(10):
                pool.wait_ge(evac_done, LIN[name].tile0 + f + 1)
                nc.gpsimd.tensor_tensor(sqs[:, f, :], qs[:, f, :], qs[:, f, :],
                                        ALU.mult).then_inc(S("sqs_ready"), 1)

        def pe_swa(pe, name):
            pe_linear(pe, name)
            for f in range(10):
                pe.wait_ge(S("sqs_ready"), f + 1)
                mm = nc.tensor.matmul(bank[5][0:20, 0:T], C("head64")[:, 19 - 2 * f:39 - 2 * f],
                                      sqs[:, f, :], start=(f == 0), stop=(f == 9))
            mm.then_inc(S("hn_sum"), 1)
            pe.wait_ge(evac_done, LIN[name].tile0 + 12)
            for j, (t0, c) in enumerate(KEYS):
                if j == 2:
                    pe.wait_ge(S("hs_ready"), 1)
                for f in range(2):
                    tr = nc.tensor.transpose(bank[5 + (j + 1) % 3][0:c, f * P:(f + 1) * P],
                                             qs[:, 10 + f, t0:t0 + c], ident)
                tr.then_inc(S("vt_done"), 1)
            pe.wait_ge(S("sel_ready"), 1)
            pe.wait_ge(S("hr_ready"), 1)
            for f in range(10):
                if f >= 4:
                    pe.wait_ge(S("qk_ready"), f - 3)
                nc.tensor.matmul(bank[f % 4][:, 0:T], sel20[:, f * P:(f + 1) * P], hr20[:], start=True,
                                 stop=True).then_inc(S("hn_done"), 1)
            pe.wait_ge(S("qk_ready"), 10)
            pe.wait_ge(S("vrow_ready"), 3)
            for u in range(HEADS):
                r = slice(HD * (u % 2), HD * (u % 2) + HD)
                t = u // 2
                mm = nc.tensor.matmul(bank[7 - u % 2][0:META, META * t:META * (t + 1)], qs[r, t, 0:META],
                                      qs[r, 8 + u // 8, 0:META], start=True, stop=True)
            mm.then_inc(S("meta_scores"), 1)

            def meta_turn(pe):
                pe.wait_ge(S("meta_p"), 1)
                for u in range(HEADS):
                    tr = nc.tensor.transpose(bank[7][0:META, 256 + META * u:256 + META * (u + 1)],
                                             smm[:, META * u:META * (u + 1)], ident[0:META, 0:META])
                tr.then_inc(S("meta_turned"), 1)

            att_pe(pe, swa, meta_turn)

        qm, vrow_m, bias_m, sm_m, pt_m, st_m = U([
            ("qm", [P, 24, SEQ]), ("vrow_m", [P, 2, D]), ("bias_m", [P, HEADS, 2 * P]),
            ("sm_m", [P, 3, 3 * P]), ("pt_m", [P, 2, 3 * P]), ("st_m", [P, HEADS, 10])], u_at)
        CUTS_A, CUTS_B = ((0, P, 0), (P, P, 1)), ((2 * P, P, 0),)
        moba = Attend(
            "moba", "moba_out", 2 * P, P,
            lambda u, r, g: qm[r, u // 2, P * g:P * (g + 1)],
            lambda u, r, g: qm[r, 8 + u // 2, 0:P * (g + 1)],
            lambda u, chunk, c: vrow_m[:, chunk, u * HD:(u + 1) * HD],
            lambda u: bias_m[:, u, :], lambda u: bias_m[:, u, P:2 * P], CUTS_A, CUTS_B,
            (sm_m, pt_m, st_m))

        def load_bias(act, dst):
            act.dma_start(dst[:], bass.AP(rel_scratch.tensor, P - 1,
                                          [[VLEN - 1, P], [P * VLEN, HEADS], [1, 2 * P]])
                          ).then_inc(S("bias_loaded"), 16)

        def value_rows(pe, src, first, sem):
            for b in range(4):
                for j in range(4):
                    f = 4 * (b % 2) + j
                    tr = nc.tensor.transpose(bank[4 + b][:, j * P:(j + 1) * P],
                                             src[:, first + f, P * (b // 2):P * (b // 2 + 1)], ident)
                tr.then_inc(S(sem), 1)

        def act_value_rows(act, dst, sem, ready):
            for b in range(4):
                act.wait_ge(S(sem), b + 1)
                nc.scalar.activation(dst[:, b // 2, 512 * (b % 2):512 * (b % 2 + 1)], bank[4 + b][:],
                                     ACT.Copy).then_inc(S(ready), 1)

        def dve_moba(dve, name):
            dve_store(dve, name, qm, 8)
            dve.wait_ge(S("bias_loaded"), 16)
            att_dve(dve, moba)

        def act_moba(act, name):
            act.wait_ge(S("rel_stored"), 16)
            load_bias(act, bias_m)
            act_store(act, name, 8)
            act_value_rows(act, vrow_m, "mv_turned", "mv_ready")
            att_act(act, moba)

        def pe_moba(pe, name):
            pe_linear(pe, name)
            pe.wait_ge(evac_done, LIN[name].tile0 + 24)
            value_rows(pe, qm, 16, "mv_turned")
            pe.wait_ge(S("mv_ready"), 4)
            att_pe(pe, moba)

        def mlp_rounds(eng, lin, slot):
            for t in range(4):
                slot(t, 0)
            with eng.Fori(0, lin.tiles // 4 - 1) as i:
                for t in range(4, 8):
                    slot(t, i)

        def dve_mlp(dve, name):
            lin = LIN[name]

            def low(t, i):
                dve.wait_ge(a_hi_ready, ACT0[name] + t + 1 + 4 * i)
                nc.vector.tensor_tensor(m_lo[:, t + 4 * i, :], av[:, t % 2, 0:SEQ],
                                        m_hi[:, t + 4 * i, :].bitcast(F32),
                                        ALU.subtract).then_inc(a_lo_ready, 1)

            def slot(t, i):
                dve_rest(dve, lin.piece0 + t + AHEAD, i, 4)
                if t == 0:
                    dve_rstd(dve, name)
                wait_tile(dve, lin, t, i, 4)
                nc.vector.scalar_tensor_tensor(out=vr[:, t % 2, 0:SEQ], in0=tile_bank(lin, t)[:, 0:SEQ],
                                               scalar=0.0, in1=rstd[:, 0:SEQ], op0=ALU.max,
                                               op1=ALU.mult).then_inc(evac_done, 1)
                if t:
                    low(t - 1, i)

            mlp_rounds(dve, lin, slot)
            low(lin.tiles - 1, 0)

        def act_mlp(act, name):
            lin = LIN[name]

            def slot(t, i):
                act_round(act, lin.piece0 + t + AHEAD, i, 4)
                if t == 0:
                    act_std(act, name)
                else:
                    squares(t - 1, i)

            def squares(t, i):
                act.wait_ge(evac_done, lin.tile0 + t + 1 + 4 * i)
                nc.scalar.activation(av[:, t % 2, 0:SEQ], vr[:, t % 2, 0:SEQ],
                                     ACT.Square).then_inc(S("mlp_sq"), 1)
                nc.scalar.activation(m_hi[:, t + 4 * i, :], vr[:, t % 2, 0:SEQ],
                                     ACT.Square).then_inc(a_hi_ready, 1)

            mlp_rounds(act, lin, slot)
            squares(lin.tiles - 1, 0)

        (ds_, qq, kv, vrow_d, bias_d, sm_d, pt_d, st_d, b2) = U([
            ("ds_", [P, 6, SEQ]), ("qq", [P, 12, SEQ]), ("kv", [P, 16, SEQ]), ("vrow_d", [P, 2, D]),
            ("bias_d", [P, HEADS, 2 * P]), ("sm_d", [P, 3, 3 * P]), ("pt_d", [P, 2, 3 * P]),
            ("st_d", [P, HEADS, 10]), ("b2", [P, 2, 3 * P])], u_at)
        sqd, _ = place(u_at + 18 * SEQ, "sqd", [P, 4, SEQ])
        hs2, after = place(u_at + 18 * SEQ + 4 * SEQ, "hs2", [2, SEQ])
        hr2, _ = place(after, "hr2", [2, SEQ])
        rl, _ = place(u_at + 34 * SEQ + 2 * D + HEADS * 2 * P, "rl", [P, 2, 3 * P])
        score = sb_alias("score", [P, 3 * P], vr)
        pick = sb_alias("pick", [P, 3 * P], av)
        top8 = small[:, 24:40]
        head_w = small[:, 8:24]
        dsa = Attend(
            "dsa", "dsa_out", 2 * P, P,
            lambda u, r, g: qq[r, u // 2, P * g:P * (g + 1)],
            lambda u, r, g: kv[r, u // 2, 0:P * (g + 1)],
            lambda u, chunk, c: vrow_d[:, chunk, u * HD:(u + 1) * HD],
            lambda u: b2[:, u % 2, 0:2 * P], lambda u: b2[:, u % 2, 2 * P:3 * P], CUTS_A, CUTS_B,
            (sm_d, pt_d, st_d))

        def dve_dsa(dve, name):
            lin = LIN[name]
            dve_store(dve, name, ds_)
            dve.wait_ge(S("c_std"), 1)
            nc.vector.reciprocal(hr2[:], hs2[:]).then_inc(S("c_rec"), 1)
            dve.wait_ge(evac_done, lin.tile0 + 6)
            for f in range(4):
                dve.wait_ge(S("c_bc"), f // 2 + 1)
                nc.vector.scalar_tensor_tensor(
                    out=ds_[:, f, :], in0=ds_[:, f, :], scalar=prm_col("g_q" if f < 2 else "g_kv", f % 2),
                    in1=bank[5 + f // 2][:, 0:SEQ], op0=ALU.mult, op1=ALU.mult).then_inc(S("c_ready"), 1)
            for f in range(4):
                dve.wait_ge(y_hi_ready, Y0["dsa_q"] + f + 1)
                nc.vector.tensor_tensor(y_lo[:, f, META:T], ds_[:, f, :],
                                        y_hi[:, f, META:T].bitcast(F32), ALU.subtract).then_inc(y_lo_ready, 1)
            q = LIN["dsa_q"]
            for t in range(12):
                if t % 4 == 0:
                    dve_rest(dve, q.piece0 + t // 4 + AHEAD)
                wait_tile(dve, q, t)
                nc.vector.tensor_scalar(qq[:, t, :], tile_bank(q, t)[:, 0:SEQ],
                                        HD ** -0.5 if t < 8 else 1.0, None,
                                        ALU.mult).then_inc(evac_done, 1)
            dve.wait_ge(S("w_turned"), 1)
            nc.vector.tensor_copy(head_w, bank[4][:, 0:16]).then_inc(S("w_ready"), 1)
            dve.wait_ge(S("w_ready"), 1)
            groups = ((0, 2 * P, 8), (2 * P, P, 0))
            for hd in range(8):
                dve.wait_ge(S("relu_done"), hd + 1)
                for x, (c0, w, w0) in enumerate(groups):
                    prev = (C("causal")[:, 2 * P - w:2 * P] if hd == 0 else score[:, c0:c0 + w])
                    if hd:
                        dve.wait_ge(S("score_done"), 2 * hd - 1 + x)
                    nc.vector.scalar_tensor_tensor(
                        out=score[:, c0:c0 + w], in0=rl[:, hd % 2, c0:c0 + w],
                        scalar=head_w[:, w0 + hd:w0 + hd + 1], in1=prev, op0=ALU.mult,
                        op1=ALU.add).then_inc(S("score_done"), 1)
            kvl = LIN["dsa_kv"]
            rest = [kvl.piece0 + j + AHEAD for j in range(kvl.pieces)]
            for r in range(TOPK // 8):
                if r % 2 == 0:
                    dve_rest(dve, rest[r // 2])
                for x, (c0, w, _) in enumerate(groups):
                    if r == 0:
                        dve.wait_ge(S("score_done"), 15 + x)
                    else:
                        dve.wait_ge(S("taken"), 2 * r - 1 + x)
                    nc.vector.max(top8[:, 8 * x:8 * x + 8], score[:, c0:c0 + w]).then_inc(S("top8"), 1)
                for x, (c0, w, _) in enumerate(groups):
                    dve.wait_ge(S("top8"), 2 * r + 1 + x)
                    nc.vector.match_replace(score[:, c0:c0 + w], top8[:, 8 * x:8 * x + 8],
                                            score[:, c0:c0 + w], GONE).then_inc(S("taken"), 1)
            dve.wait_ge(S("taken"), TOPK // 4)
            nc.vector.tensor_scalar(pick[:], score[:], 0.5 * GONE, NEG, ALU.is_gt,
                                    ALU.mult).then_inc(S("pick_ready"), 1)

            def bias_ready(dve, u):
                dve.wait_ge(S("b2_ready"), 2 * u + 2)

            att_dve(dve, dsa, extra=bias_ready)

        def act_dsa(act, name):
            lin = LIN[name]
            load_bias(act, bias_d)
            act_store(act, name)
            act.wait_ge(S("c_sum"), 1)
            nc.scalar.activation(hs2[:], bank[4][0:2, 0:SEQ], ACT.Sqrt, bias=eps[0:2, 0:1],
                                 scale=1.0 / (2 * P)).then_inc(S("c_std"), 1)
            for f in range(4):
                act.wait_ge(S("c_ready"), f + 1)
                nc.scalar.activation(y_hi[:, f, META:T], ds_[:, f, :], ACT.Copy).then_inc(y_hi_ready, 1)
            q = LIN["dsa_q"]
            for j in range(q.pieces):
                act_round(act, q.piece0 + j + AHEAD)
            for hd in range(8):
                act.wait_ge(S("idx_done"), hd + 1)
                if hd >= 2:
                    act.wait_ge(S("score_done"), 2 * hd - 2)
                nc.scalar.activation(rl[:, hd % 2, :], bank[4 + hd % 4][:, 0:3 * P],
                                     ACT.Relu).then_inc(S("relu_done"), 1)
            kvl = LIN["dsa_kv"]
            act.wait_ge(evac_done, kvl.tile0)
            for t in range(16):
                if t % 4 == 0:
                    act_round(act, kvl.piece0 + t // 4 + AHEAD)
                wait_tile(act, kvl, t)
                nc.scalar.activation(kv[:, t, :], tile_bank(kvl, t)[:, 0:SEQ], ACT.Copy).then_inc(evac_done, 1)
            act_value_rows(act, vrow_d, "dv_turned", "dv_ready")
            att_act(act, dsa)

        def pool_dsa(pool, name):
            lin = LIN[name]
            for f in range(4):
                pool.wait_ge(evac_done, lin.tile0 + f + 1)
                nc.gpsimd.tensor_tensor(sqd[:, f, :], ds_[:, f, :], ds_[:, f, :],
                                        ALU.mult).then_inc(S("sqd_ready"), 1)
            pool.wait_ge(S("pick_ready"), 1)
            pool.wait_ge(S("bias_loaded"), 32)
            for u in range(HEADS):
                if u >= 2:
                    dsa.wait(pool, "max", 2 * (u - 2) + 2)
                nc.gpsimd.tensor_tensor(b2[:, u % 2, 0:2 * P], bias_d[:, u, :], pick[:, 0:2 * P],
                                        ALU.add).then_inc(S("b2_ready"), 1)
                nc.gpsimd.tensor_tensor(b2[:, u % 2, 2 * P:3 * P], bias_d[:, u, P:2 * P],
                                        pick[:, 2 * P:3 * P], ALU.add).then_inc(S("b2_ready"), 1)

        def pe_dsa(pe, name):
            pe_linear(pe, name)
            for f in range(4):
                pe.wait_ge(S("sqd_ready"), f + 1)
                g = f // 2
                mm = nc.tensor.matmul(bank[4][0:2, 0:SEQ], C("head128")[:, 7 - g:9 - g], sqd[:, f, :],
                                      start=(f == 0), stop=(f == 3))
            mm.then_inc(S("c_sum"), 1)
            pe.wait_ge(S("c_rec"), 1)
            for g in range(2):
                nc.tensor.matmul(bank[5 + g][:, 0:SEQ], ident[0:2, g:g + 1].to_broadcast([2, P]), hr2[:],
                                 start=True, stop=True).then_inc(S("c_bc"), 1)
            pe.wait_ge(evac_done, LIN[name].tile0 + 6)
            for g in range(2):
                tr = nc.tensor.transpose(bank[4][:, 8 * g:8 * (g + 1)], ds_[0:8, 5, P * g:P * (g + 1)],
                                         ident[0:8, 0:8])
            tr.then_inc(S("w_turned"), 1)
            pe_linear(pe, "dsa_q")
            pe.wait_ge(evac_done, LIN["dsa_kv"].tile0)
            pe.wait_ge(S("w_ready"), 1)
            pe.wait_ge(S("c_ready"), 4)
            for hd in range(8):
                if hd >= 4:
                    pe.wait_ge(S("relu_done"), hd - 3)
                r = slice(HD * (hd % 2), HD * (hd % 2) + HD)
                bk = bank[4 + hd % 4]
                nc.tensor.matmul(bk[:, 0:2 * P], qq[r, 8 + hd // 2, P:2 * P], ds_[r, 4, 0:2 * P],
                                 start=True, stop=True)
                nc.tensor.matmul(bk[:, 2 * P:3 * P], qq[r, 8 + hd // 2, 0:P], ds_[r, 4, 0:P],
                                 start=True, stop=True).then_inc(S("idx_done"), 1)
            pe_linear(pe, "dsa_kv")
            pe.wait_ge(evac_done, LIN["dsa_kv"].tile0 + 16)
            pe.wait_ge(S("relu_done"), 8)
            value_rows(pe, kv, 8, "dv_turned")
            pe.wait_ge(S("dv_ready"), 4)
            att_pe(pe, dsa)

        def dve_final(dve):
            dve_rstd(dve, "final")
            for c in range(KD):
                nc.vector.scalar_tensor_tensor(out=fin[:, c, :], in0=h[:, c, META:T],
                                               scalar=prm_col("final", c), in1=rstd[:, 0:SEQ],
                                               op0=ALU.mult, op1=ALU.mult).then_inc(S("final_ready"), 1)

        SECTIONS = {"act": {}, "dve": {}, "pe": {}, "pool": {}}
        for nm in ORDER:
            if nm == "mix_in":
                fns = (act_mix, dve_mix, pe_mix, pool_mix)
            elif nm in PAIR0:
                fns = (act_gated, dve_gated, pe_linear, None)
            elif nm in RESID:
                fns = (act_resid, dve_resid, pe_linear, pool_resid)
            elif nm == "swa_in":
                fns = (act_swa, dve_swa, pe_swa, pool_swa)
            elif nm == "moba_in":
                fns = (act_moba, dve_moba, pe_moba, None)
            elif nm in ("mlp_up0", "mlp_up1"):
                fns = (act_mlp, dve_mlp, pe_linear, None)
            elif nm == "dsa_in":
                fns = (act_dsa, dve_dsa, pe_dsa, pool_dsa)
            else:
                fns = (None, None, None, None)
            for e, fn in zip(("act", "dve", "pe", "pool"), fns):
                SECTIONS[e][nm] = fn or (lambda eng, name: None)

        def dump_at(sp):
            sp.wait_ge(S("rel_stored"), 16)
            if last in RESID:
                sp.wait_ge(evac_done, LIN[last].tile0 + LIN[last].tiles)
                sp.dma_start(dump.rearrange("p (a b) -> p a b", a=KD)[:, :, :], h[:]).then_inc(out_done, 16)
                sp.wait_ge(out_done, 16)

        @block.sync
        def _(sp):
            def load(lin, g, i=0):
                slot, turn = at_piece(g, i, RING)
                if g >= RING:
                    sp.wait_ge(lo_ready, g - RING + 1 + i * RING)
                sp.dma_start(raw[:, slot, 0:lin.width],
                             weights[lin.name][g - lin.piece0 + i * RING]).then_inc(landed[slot], 16)

            for name in ORDER:
                if name == "mix_out":
                    sp.wait_ge(S("rel_ready"), 1)
                    sp.dma_start(rel_scratch, relv[:].unsqueeze(1).to_broadcast([HEADS, P, VLEN])
                                 ).then_inc(S("rel_stored"), 16)
                lin = LIN[name]
                g = lin.piece0
                if lin is LIN["mix_in"]:
                    for _ in range(RING):
                        load(lin, g)
                        g += 1
                    sp.dma_start(cst[:], consts_d).then_inc(loaded, 16)
                rounds = (lin.piece0 + lin.pieces - g) // RING
                if rounds > 1:
                    with sp.Fori(0, rounds) as i:
                        for k in range(RING):
                            load(lin, g + k, i)
                    g += rounds * RING
                while g < lin.piece0 + lin.pieces:
                    load(lin, g)
                    g += 1

            if last is None:
                for c in range(KD):
                    sp.wait_ge(S("final_ready"), c + 1)
                    sp.dma_start(out_t[c], fin[:, c, :]).then_inc(out_done, 16)
                sp.wait_ge(out_done, 16 * KD)
            else:
                dump_at(sp)

        @block.scalar
        def _(act):
            for c in range(KD):
                if c == 0:
                    act.dma_start(prm[:], params_d).then_inc(loaded, 16)
                act.dma_start(h[:, c, :], x_t[c]).then_inc(h_loaded, 16)
            for g in range(AHEAD):
                act_round(act, g)
            act.wait_ge(loaded, 32)
            act.wait_ge(h_loaded, 16 * KD)
            for c in range(KD):
                act_x_hi(act, "mix_in", c)
            for name in ORDER:
                SECTIONS["act"][name](act, name)
            if last is None:
                act_std(act, "final")

        @block.vector
        def _(dve):
            nc.vector.memset(eps[:], EPS).then_inc(eps_set, 1)
            nc.vector.memset(gb[:], 0.0).then_inc(eps_set, 1)
            for g in range(AHEAD):
                dve_rest(dve, g)
            dve.wait_ge(loaded, 32)
            dve.wait_ge(h_loaded, 16 * KD)
            for c in range(KD):
                dve_x_lo(dve, "mix_in", c)
            dve.wait_ge(S("rel_done"), 1)
            nc.vector.tensor_tensor(relv[:], bank[7][0:HEADS, 0:VLEN], C("future", HEADS),
                                    ALU.add).then_inc(S("rel_ready"), 1)
            dve.wait_ge(eps_set, 2)
            for name in ORDER:
                SECTIONS["dve"][name](dve, name)
            if last is None:
                dve_final(dve)

        @block.tensor
        def _(pe):
            pe.wait_ge(loaded, 32)
            nc.tensor.matmul(bank[7][0:HEADS, 0:VLEN],
                             prm[0:BUCKETS, PARAM_AT["rel"][0]:PARAM_AT["rel"][0] + HEADS],
                             C("onehot", BUCKETS), start=True, stop=True).then_inc(S("rel_done"), 1)
            for name in ORDER:
                SECTIONS["pe"][name](pe, name)
            if last is None:
                norm_sum(pe, "final")

        @block.gpsimd
        def _(pool):
            pool.wait_ge(h_loaded, 16 * KD)
            for c in range(KD):
                pool_squares(pool, c)
            for name in ORDER:
                SECTIONS["pool"][name](pool, name)


def rel_bucket(dist):
    exact = BUCKETS // 2
    nf = np.maximum(dist, 1).astype(np.float32)
    ratio = np.log(nf / np.float32(exact)) / np.float32(np.log(P / exact))
    large = exact + (ratio * np.float32(BUCKETS - exact)).astype(np.int32)
    return np.where(dist < exact, dist, np.minimum(large, BUCKETS - 1))


def constants():
    out = np.zeros((P, NCONST), np.float32)

    def put(name, value):
        a, n = CONST_AT[name]
        out[:value.shape[0], a:a + n] = value.reshape(value.shape[0], n)

    i, j = np.arange(P)[:, None], np.arange(P)[None, :]
    put("ident", (i == j).astype(np.float32))
    put("ones", np.ones((P, P), np.float32))
    levels = np.zeros((P, 7, P), np.float32)
    for level in range(7):
        b = 1 << level
        levels[:, level] = (i // (2 * b) == j // (2 * b)) & (i // b % 2 == 0) & (j // b % 2 == 1)
    put("levels", levels)
    put("strict", (j > i).astype(np.float32))
    put("incl", (j >= i).astype(np.float32))
    c = np.arange(40)[None, :]
    put("head64", (c == 19 + i // HD).astype(np.float32))
    put("head128", np.broadcast_to(np.arange(15)[None, :] == 7, (P, 15)).astype(np.float32))
    dist = 2 * P - 1 - np.arange(VLEN)
    hot = (rel_bucket(np.maximum(dist, 0))[None, :] == np.arange(BUCKETS)[:, None]) & (dist >= 0)[None, :]
    put("onehot", hot.astype(np.float32))
    put("future", np.broadcast_to(np.where(dist < 0, NEG, 0.0)[None, :], (HEADS, VLEN)))
    for name, q0, n in (("swa1", META + P, T), ("swa0", META, META + P)):
        rel = q0 + np.arange(P)[:, None] - np.arange(n)[None, :]
        keep = (np.arange(n)[None, :] < META) | ((rel >= 0) & (rel < P))
        put(name, np.where(keep, 0.0, NEG))
    m = np.arange(META)
    put("meta", np.where(m[:, None] >= m[None, :], 0.0, NEG))
    put("causal", np.where(np.arange(2 * P)[None, :] <= P + np.arange(P)[:, None], 0.0, NEG))
    return out


def blocks(w, name):
    lin = LIN[name]
    t = w.reshape(lin.chunks, P, lin.tiles, P).transpose(2, 1, 0, 3)
    if lin.per_tile > 1:
        k = lin.chunks // lin.per_tile
        t = t.reshape(lin.tiles, P, lin.per_tile, k, P).transpose(0, 2, 1, 3, 4)
    if lin.per_piece > 1:
        t = t.reshape(lin.tiles // lin.per_piece, lin.per_piece, P, lin.chunks, P).transpose(0, 2, 1, 3, 4)
    return np.ascontiguousarray(t.reshape(lin.pieces, P, lin.width))


def by_column(v):
    v = v.reshape(-1, P)
    return v.T


SWA_ORDER = [h for t in range(8) for h in (t // 4 * 8 + t % 4, t // 4 * 8 + 4 + t % 4)]


def lay_out(a):
    w = a["mix_w_in"][0]
    sizes = [512, 512, 512, 1536, 512, 4, 4]
    at = [sum(sizes[:i]) for i in range(len(sizes) + 1)]
    gate_in, gate_out, a_h, qkv_w, z_w, beta_w, alpha_w = (w[:, at[i]:at[i + 1]] for i in range(7))
    rates = np.zeros((D, P), np.float32)
    rates[:, 0:4] = alpha_w
    rates[:, 32:36] = beta_w
    parts = [qkv_w, rates, z_w]
    for j in range(4):
        s = slice(j * P, (j + 1) * P)
        parts += [gate_in[:, s], a_h[:, s], gate_out[:, s]]
    mats = {"mix_in": np.concatenate(parts, 1), "mix_out": a["mix_w_out"][0]}
    for n in range(2):
        up = a["ffn_w_up"][n].reshape(D, 2, GATES, P).transpose(0, 2, 1, 3)
        mats[f"up{n}"] = up.reshape(D, 2 * DFF)
        mats[f"down{n}"] = a["ffn_w_down"][n]
        mats[f"mlp_up{n}"] = a["mlp_w_up_2"][n]
        mats[f"mlp_down{n}"] = a["mlp_w_down_2"][n]
    wq = a["swa_wq"][0].reshape(D, HEADS, HD)[:, SWA_ORDER].reshape(D, D)
    mats["swa_in"] = np.concatenate([wq, a["swa_wk"][0], a["swa_wv"][0]], 1)
    mats["swa_out"] = a["swa_wo"][0].reshape(HEADS, HD, D)[SWA_ORDER].reshape(D, D)
    mats["moba_in"] = a["moba_w_qkv_2"][0]
    mats["moba_out"] = a["moba_w_o_2"][0]
    w = a["dsa_w_in_2"][0]
    heads_w = np.zeros((D, P), np.float32)
    heads_w[:, 0:8] = w[:, 576:584]
    mats["dsa_in"] = np.concatenate([w[:, 0:512], w[:, 512:576], w[:, 512:576], heads_w], 1)
    mats["dsa_q"] = np.concatenate([a["dsa_w_uq_2"][0], a["dsa_w_qi_2"][0]], 1)
    uk = a["dsa_w_uk_2"][0].transpose(2, 0, 1).reshape(2 * P, D)
    uv = a["dsa_w_uv_2"][0].transpose(1, 0, 2).reshape(2 * P, D)
    mats["dsa_kv"] = np.concatenate([uk, uv], 1)
    mats["dsa_out"] = a["dsa_w_o_2"][0]
    weights = {name: blocks(mats[name], name) for name in LIN}

    prm = np.zeros((P, NPARAM), np.float32)

    def put(name, value):
        at, n = PARAM_AT[name]
        prm[:value.shape[0], at:at + n] = value.reshape(value.shape[0], n)

    put("attn_w", by_column(a["attn_norm_w"]))
    put("ffn_w", by_column(a["ffn_norm_w"]))
    put("conv_a", by_column(a["conv_a_w"]))
    put("dn_conv", by_column(a["dn_conv_w"]))
    put("dn_norm", by_column(a["dn_norm_w"]))
    put("q_norm", np.concatenate([a["swa_q_norm_w"][0], a["swa_q_norm_w"][0]])[:, None])
    put("k_norm", np.concatenate([a["swa_k_norm_w"][0], a["swa_k_norm_w"][0]])[:, None])
    put("sinks", np.broadcast_to(a["swa_sinks"][0][SWA_ORDER][None, :], (P, HEADS)))
    put("ffn_conv", by_column(a["ffn_conv_w"]))
    put("ln_attn", by_column(a["ln_attn_2"]))
    put("ln_mlp", by_column(a["ln_mlp_2"]))
    put("g_q", by_column(a["dsa_g_q_2"]))
    put("g_kv", by_column(a["dsa_g_kv_2"]))
    put("final", by_column(a["final_norm_2"]))
    put("a_log", a["dn_a_log"][0][:, None])
    put("dt_bias", a["dn_dt_bias"][0][:, None])
    put("rel", a["rel_bias_2"])
    h0 = np.concatenate([a["meta_tokens"], a["x"][0]], 0)
    x_t = np.ascontiguousarray(h0.T).reshape(KD, P, T)
    return x_t, weights, prm


def kernel(_last=None, **inputs):
    import concourse.bacc as bacc
    from concourse.bass_utils import run_bass_kernel_spmd

    a = {k: np.asarray(v) for k, v in inputs.items()}
    x_t, weights, prm = lay_out(a)
    nc = bacc.Bacc("TRN2", target_bir_lowering=False, num_devices=1)
    arrays = {"x_t": x_t, "prm": prm, "cst": constants()}
    arrays.update({f"w_{k}": v for k, v in weights.items()})
    ap = {k: nc.dram_tensor(k, v.shape, F32, kind="ExternalInput").ap() for k, v in arrays.items()}
    rel = nc.dram_tensor("rel_scratch", (HEADS, P, VLEN), F32, kind="Internal").ap()
    out = nc.dram_tensor("out", (KD, P, SEQ), F32, kind="ExternalOutput").ap()
    dump = None
    if _last is not None:
        dump = nc.dram_tensor("dump", (P, KD * T), F32, kind="ExternalOutput").ap()
    build(nc, ap["x_t"], {k: ap[f"w_{k}"] for k in weights}, ap["prm"], ap["cst"], rel, out, _last, dump)
    r = run_bass_kernel_spmd(nc, [arrays], core_ids=[0])
    if _last is not None:
        return r.results[0]["dump"]
    return r.results[0]["out"].reshape(D, SEQ).T[None]
```

```python
from contextlib import ExitStack

import numpy as np

import concourse.bass as bass
from concourse import mybir

F32 = mybir.dt.float32
F32R = mybir.dt.float32r
ALU = mybir.AluOpType
ACT = mybir.ActivationFunctionType
AX_X = mybir.AxisListType.X

P = 128
D = 1024
KD = D // P
META = 16
SEQ = 256
T = META + SEQ
DFF = 2816
DFF2 = 4096
GATES = DFF // P
EPS = 1e-6
NEG = -1e30
GONE = -3e38
TOPK = 64
HEADS = 16
HD = 64
BUCKETS = 32
CH = ((0, META), (META, P), (META + P, P))
KEYS = ((META, P), (META + P, P), (0, META))

LINEARS = (
    ("mix_in", 29, KD, 1, 1), ("mix_out", 8, KD, 1, 1),
    ("up0", 2 * GATES, KD, 1, 1), ("down0", 8, GATES, 2, 1),
    ("swa_in", 12, KD, 1, 1), ("swa_out", 8, KD, 1, 1),
    ("up1", 2 * GATES, KD, 1, 1), ("down1", 8, GATES, 2, 1),
    ("moba_in", 24, KD, 1, 1), ("moba_out", 8, KD, 1, 1),
    ("mlp_up0", DFF2 // P, KD, 1, 1), ("mlp_down0", 8, DFF2 // P, 4, 1),
    ("dsa_in", 6, KD, 1, 1), ("dsa_q", 12, 2, 1, 4), ("dsa_kv", 16, 2, 1, 4),
    ("dsa_out", 8, KD, 1, 1),
    ("mlp_up1", DFF2 // P, KD, 1, 1), ("mlp_down1", 8, DFF2 // P, 4, 1),
)
RING = 4
BANKS = 4
AHEAD = 3
SLOT = GATES // 2 * P

PARAMS = (("attn_w", 16), ("ffn_w", 16), ("conv_a", 12), ("dn_conv", 48), ("dn_norm", 1),
          ("q_norm", 1), ("k_norm", 1), ("sinks", 16), ("ffn_conv", 2 * 3 * GATES),
          ("ln_attn", 16), ("ln_mlp", 16), ("g_q", 2), ("g_kv", 2), ("final", 8),
          ("a_log", 1), ("dt_bias", 1), ("rel", HEADS))
VLEN = 3 * P
CONSTS = (("ident", P), ("ones", P), ("levels", 7 * P), ("strict", P), ("incl", P),
          ("head64", 40), ("head128", 15), ("onehot", VLEN), ("swa1", T), ("swa0", META + P),
          ("meta", META), ("causal", 2 * P), ("future", VLEN))


def columns(table):
    at, out = 0, {}
    for name, n in table:
        out[name] = (at, n)
        at += n
    return out, at


PARAM_AT, NPARAM = columns(PARAMS)
CONST_AT, NCONST = columns(CONSTS)


class Linear:

    def __init__(self, name, tiles, chunks, per_tile, per_piece, piece0, tile0):
        self.name, self.tiles, self.chunks = name, tiles, chunks
        self.per_tile, self.per_piece = per_tile, per_piece
        self.piece0, self.tile0 = piece0, tile0
        self.pieces = tiles * per_tile // per_piece
        self.width = chunks * per_piece // per_tile * P


def plan():
    out, piece, tile = {}, 0, 0
    for name, tiles, chunks, per_tile, per_piece in LINEARS:
        out[name] = Linear(name, tiles, chunks, per_tile, per_piece, piece, tile)
        piece += out[name].pieces
        tile += tiles
    return out, piece


LIN, NPIECES = plan()
WIDTHS = [lin.width for lin in LIN.values() for _ in range(lin.pieces)]
IN_UP = 3


def build(nc, x_t, weights, params_d, consts_d, rel_scratch, out_t):
    ctx = ExitStack()
    with ctx:
        sems = {}

        def S(name):
            if name not in sems:
                sems[name] = ctx.enter_context(nc.semaphore(name))
            return sems[name]

        base = (nc.sbuf_base + 31) // 32 * 32
        words = (nc.sbuf_usable_end - base) // 4 // 8 * 8
        ctx.enter_context(nc.sbuf_tensor("slab", [P, words], F32))
        top, where = [0], {}

        def place(at, name, shape, dt=F32):
            n = 1
            for s in shape[1:]:
                n *= s
            assert at + n <= words, (name, at + n, words)
            return nc.alloc_sbuf_tensor_at(name, shape, dt, offset=base + 4 * at), at + (n + 7) // 8 * 8

        def sb(name, shape, dt=F32):
            at = top[0]
            t, top[0] = place(at, name, shape, dt)
            where[t.name] = at
            return t

        raw = sb("raw", [P, RING, SLOT])
        w_hi = sb("w_hi", [P, RING, SLOT], F32R)
        w_lo = sb("w_lo", [P, RING, SLOT], F32R)
        h = sb("h", [P, KD, T])
        x_hi = sb("x_hi", [P, KD, T], F32R)
        x_lo = sb("x_lo", [P, KD, T], F32R)
        y_hi = sb("y_hi", [P, KD, T], F32R)
        y_lo = sb("y_lo", [P, KD, T], F32R)
        prm = sb("prm", [P, NPARAM])
        cst = sb("cst", [P, NCONST])
        rstd = sb("rstd", [P, T])
        std = sb("std", [P, T])
        sq = sb("sq", [P, T])
        acc = sb("acc", [P, T])
        eps = sb("eps", [P, 1])
        gb = sb("gb", [P, 2, IN_UP + T])
        cb = sb("cb", [P, 2, T])
        sg = sb("sg", [P, 2, T])
        vr = sb("vr", [P, 2, T])
        av = sb("av", [P, 2, T])
        small = sb("small", [P, 64])
        relv = sb("relv", [HEADS, VLEN])
        u_at = top[0]
        u_end = words
        a_hi, at = place(u_at, "a_hi", [P, GATES, T], F32R)
        a_lo, _ = place(at, "a_lo", [P, GATES, T], F32R)
        m_hi, at = place(u_at, "m_hi", [P, DFF2 // P, SEQ], F32R)
        m_lo, _ = place(at, "m_lo", [P, DFF2 // P, SEQ], F32R)

        def U(specs, at):
            out = []
            for name, shape in specs:
                t, at = place(at, name, shape)
                out.append(t)
            assert at <= u_end, (specs[-1][0], at, u_end)
            return out

        def sb_alias(name, shape, over):
            return place(where[over.name], name, shape)[0]

        def C(name, n=P):
            a, w = CONST_AT[name]
            return cst[0:n, a:a + w]

        def prm_col(name, j=0, n=P):
            a = PARAM_AT[name][0] + j
            return prm[0:n, a:a + 1] if isinstance(a, int) else prm[0:n, bass.ds(a, 1)]

        bank = [ctx.enter_context(nc.psum_tensor(f"bank{i}", [P, 512], F32)) for i in range(8)]

        ident = C("ident")

        block = ctx.enter_context(nc.Block())
        landed = [S(f"landed{i}") for i in range(RING)]
        hi_ready = S("hi_ready")
        lo_ready = S("lo_ready")
        piece_used = S("piece_used")
        evac_done = S("evac_done")
        x_hi_ready, x_lo_ready = S("x_hi_ready"), S("x_lo_ready")
        y_hi_ready, y_lo_ready = S("y_hi_ready"), S("y_lo_ready")
        a_ready, a_hi_ready, a_lo_ready = S("a_ready"), S("a_hi_ready"), S("a_lo_ready")
        acc_done, ms_done, std_done, rstd_done = (S("acc_done"), S("ms_done"), S("std_done"),
                                                  S("rstd_done"))
        loaded = S("loaded")
        h_loaded = [S(f"h_loaded{i}") for i in range(KD // 2)]
        eps_set = S("eps_set")
        dve_own, act_own, pool_own = S("dve_own"), S("act_own"), S("pool_own")
        out_done = S("out_done")

        NORMS = {"mix_in": 0, "up0": 1, "swa_in": 2, "up1": 3, "moba_in": 4, "mlp_up0": 5,
                 "dsa_in": 6, "mlp_up1": 7, "final": 8}
        Y0 = {"mix_out": 0, "swa_out": 8, "moba_out": 16, "dsa_q": 24, "dsa_out": 28}
        A0 = {"down0": 0, "down1": GATES, "mlp_down0": 2 * GATES,
              "mlp_down1": 2 * GATES + DFF2 // P}
        PAIR0 = {"up0": 0, "up1": GATES}
        ACT0 = {"up0": 0, "up1": GATES, "mlp_up0": 2 * GATES, "mlp_up1": 2 * GATES + DFF2 // P}
        NORM_W = {"mix_in": ("attn_w", 0), "up0": ("ffn_w", 0), "swa_in": ("attn_w", 8),
                  "up1": ("ffn_w", 8), "moba_in": ("ln_attn", 0), "mlp_up0": ("ln_mlp", 0),
                  "dsa_in": ("ln_attn", 8), "mlp_up1": ("ln_mlp", 8)}
        RESID = {"mix_out": "up0", "down0": "swa_in", "swa_out": "up1", "down1": "moba_in",
                 "moba_out": "mlp_up0", "mlp_down0": "dsa_in", "dsa_out": "mlp_up1",
                 "mlp_down1": "final"}
        ORDER = [name for name, *_ in LINEARS]
        END_PIECE = LIN[ORDER[-1]].piece0 + LIN[ORDER[-1]].pieces
        SECOND = set(name for name, *_ in LINEARS[8:])

        def cols(name):
            return (META, SEQ) if name in SECOND or name == "down1" else (0, T)

        def inputs(name, c):
            a, n = cols(name)
            if name in NORMS:
                return x_hi[:, c, a:a + n], x_lo[:, c, a:a + n]
            if name in ("down0", "down1"):
                return a_hi[:, c, a:a + n], a_lo[:, c, a:a + n]
            if name in ("mlp_down0", "mlp_down1"):
                return m_hi[:, c, :], m_lo[:, c, :]
            if name == "dsa_kv":
                c += 2
            return y_hi[:, c, a:a + n], y_lo[:, c, a:a + n]

        def at_piece(g, i=0, step=0):
            assert step % RING == 0
            return g % RING, g // RING + 1 + i * (step // RING)

        fin, = U([("fin", [P, KD, SEQ])], u_at)

        def act_round(act, g, i=0, step=RING):
            if g >= END_PIECE:
                return
            slot, turn = at_piece(g, i, step)
            act.wait_ge(landed[slot], 16 * (g // RING + 1) + i * (16 * step // RING))
            if g >= RING:
                act.wait_ge(piece_used, g - RING + 1 + i * step)
            nc.scalar.activation(w_hi[:, slot, 0:WIDTHS[g]], raw[:, slot, 0:WIDTHS[g]],
                                 ACT.Copy).then_inc(hi_ready, 1)

        def dve_rest(dve, g, i=0, step=RING):
            if g >= END_PIECE:
                return
            slot, _ = at_piece(g, i, step)
            dve.wait_ge(hi_ready, g + 1 + i * step)
            nc.vector.tensor_tensor(w_lo[:, slot, 0:WIDTHS[g]], raw[:, slot, 0:WIDTHS[g]],
                                    w_hi[:, slot, 0:WIDTHS[g]].bitcast(F32),
                                    ALU.subtract).then_inc(lo_ready, 1)

        def wait_tile(eng, lin, t, i=0, step=0):
            pieces = (t // lin.per_piece + 1) * lin.per_tile
            eng.wait_ge(piece_used, lin.piece0 + pieces + i * (step * lin.per_tile // lin.per_piece))

        def tile_bank(lin, t):
            if lin is LIN["mix_in"] and t >= A0_TILE:
                return bank[BANKS - 1]
            return bank[(lin.tile0 + t) % BANKS]

        def pe_tile(pe, lin, t, i=0, step=0, ready=None):
            a, n = cols(lin.name)
            out = tile_bank(lin, t)[:, 0:n]
            if lin.tile0 + t >= BANKS:
                pe.wait_ge(evac_done, lin.tile0 + t - BANKS + 1 + i * step)
            for q in range(lin.per_tile):
                g = lin.piece0 + t // lin.per_piece * lin.per_tile + q
                slot = g % RING
                pe.wait_ge(lo_ready, g + 1 + i * (step * lin.per_tile // lin.per_piece))
                k = lin.chunks // lin.per_tile
                for c in range(k):
                    w0 = (t % lin.per_piece * k + c) * P
                    whi, wlo = w_hi[:, slot, w0:w0 + P], w_lo[:, slot, w0:w0 + P]
                    chunk = q * k + c
                    if ready is not None:
                        ready(chunk)
                    xh, xl = inputs(lin.name, chunk)
                    end = chunk == lin.chunks - 1
                    nc.tensor.matmul(out, whi, xh, start=(chunk == 0), stop=False)
                    nc.tensor.matmul(out, whi, xl, start=False, stop=False)
                    mm = nc.tensor.matmul(out, wlo, xh, start=False, stop=end)
                if t % lin.per_piece == lin.per_piece - 1:
                    mm.then_inc(piece_used, 1)

        def norm_sum(pe, name):
            k = NORMS[name]
            a, n = (META, SEQ) if name in SECOND or name == "final" else (0, T)
            pe.wait_ge(acc_done, k + 1)
            nc.tensor.matmul(bank[4][:, 0:n], C("ones"), acc[:, a:a + n], start=True,
                             stop=True).then_inc(ms_done, 1)

        def pe_linear(pe, name, tiles=None):
            lin = LIN[name]
            tiles = tiles or lin.tiles

            def ready(c):
                if name in NORMS:
                    pe.wait_ge(x_lo_ready, 8 * NORMS[name] + c + 1)
                elif name in A0:
                    pe.wait_ge(a_lo_ready, A0[name] + c + 1)
                elif name == "dsa_kv":
                    pe.wait_ge(y_lo_ready, Y0["dsa_q"] + 2 + c + 1)
                else:
                    pe.wait_ge(y_lo_ready, Y0[name] + c + 1)

            for t in range(min(4, tiles)):
                pe_tile(pe, lin, t, ready=ready if t == 0 else None)
                if name == "mix_in" and t == 2:
                    pe.wait_ge(loaded, 16)
                    nc.tensor.matmul(bank[7][0:HEADS, 0:VLEN],
                                     prm[0:BUCKETS, PARAM_AT["rel"][0]:PARAM_AT["rel"][0] + HEADS],
                                     C("onehot", BUCKETS), start=True, stop=True).then_inc(S("rel_done"), 1)
                if t == (2 if name == "mix_in" else 0) and name in NORMS:
                    norm_sum(pe, name)
            rounds = tiles // 4 - 1
            if lin.per_piece == 1 and rounds > 0:
                with pe.Fori(0, rounds) as i:
                    for t in range(4):
                        pe_tile(pe, lin, 4 + t, i, 4)
                rest = range(4 * (rounds + 1), tiles)
            else:
                rest = range(4, tiles)
            for t in rest:
                pe_tile(pe, lin, t)

        def act_std(act, name):
            k = NORMS[name]
            n = SEQ if name in SECOND or name == "final" else T
            act.wait_ge(ms_done, k + 1)
            nc.scalar.activation(std[:, 0:n], bank[4][:, 0:n], ACT.Sqrt, bias=eps[:, 0:1],
                                 scale=1.0 / D).then_inc(std_done, 1)

        def dve_rstd(dve, name):
            k = NORMS[name]
            n = SEQ if name in SECOND or name == "final" else T
            dve.wait_ge(std_done, k + 1)
            nc.vector.reciprocal(rstd[:, 0:n], std[:, 0:n]).then_inc(rstd_done, 1)
            dve.wait_ge(rstd_done, k + 1)

        def norm_w(name, c):
            p, j = NORM_W[name]
            return prm_col(p, j + c)

        def act_x_hi(act, name, c):
            nc.scalar.activation(x_hi[:, c, :], h[:, c, :], ACT.Copy,
                                 scale=norm_w(name, c)).then_inc(x_hi_ready, 1)

        def dve_x_lo(dve, name, c):
            dve.wait_ge(x_hi_ready, 8 * NORMS[name] + c + 1)
            nc.vector.scalar_tensor_tensor(out=x_lo[:, c, :], in0=h[:, c, :], scalar=norm_w(name, c),
                                           in1=x_hi[:, c, :].bitcast(F32), op0=ALU.mult,
                                           op1=ALU.subtract).then_inc(x_lo_ready, 1)

        pool_count = [0]

        def pool_link(pool, ins):
            pool_count[0] += 1
            ins.then_inc(pool_own, 1)
            pool.wait_ge(pool_own, pool_count[0])

        def pool_squares(pool, c):
            if c == 0:
                ins = nc.gpsimd.tensor_tensor(acc[:], h[:, c, :], h[:, c, :], ALU.mult)
            else:
                pool_link(pool, nc.gpsimd.tensor_tensor(sq[:], h[:, c, :], h[:, c, :], ALU.mult))
                ins = nc.gpsimd.tensor_tensor(acc[:], acc[:], sq[:], ALU.add)
            if c == KD - 1:
                ins.then_inc(acc_done, 1)
            else:
                pool_link(pool, ins)

        dve_count, act_count = [0], [0]

        def dve_link(dve, ins):
            dve_count[0] += 1
            ins.then_inc(dve_own, 1)
            dve.wait_ge(dve_own, dve_count[0])

        def act_link(act, ins):
            act_count[0] += 1
            ins.then_inc(act_own, 1)
            act.wait_ge(act_own, act_count[0])

        def dve_resid(dve, name):
            lin = LIN[name]
            nxt = RESID[name]
            a, n = cols(name)
            for t in range(lin.tiles):
                for q in range(lin.per_tile):
                    dve_rest(dve, lin.piece0 + t * lin.per_tile + q + AHEAD)
                wait_tile(dve, lin, t)
                nc.vector.tensor_tensor(h[:, t, a:a + n], tile_bank(lin, t)[:, 0:n], h[:, t, a:a + n],
                                        ALU.add).then_inc(evac_done, 1)
                if t and nxt != "final":
                    dve_x_lo(dve, nxt, t - 1)
            if nxt != "final":
                dve_x_lo(dve, nxt, lin.tiles - 1)

        def act_resid(act, name):
            lin = LIN[name]
            for t in range(lin.tiles):
                for q in range(lin.per_tile):
                    act_round(act, lin.piece0 + t * lin.per_tile + q + AHEAD)
                act.wait_ge(evac_done, lin.tile0 + t + 1)
                if RESID[name] != "final":
                    act_x_hi(act, RESID[name], t)

        def pool_resid(pool, name):
            lin = LIN[name]
            for t in range(lin.tiles):
                pool.wait_ge(evac_done, lin.tile0 + t + 1)
                pool_squares(pool, t)

        def gated_slots(eng, name, slot_a, slot_b):
            for j in (0, 1):
                slot_a(j, 0)
                slot_b(j, 0)
            with eng.Fori(0, (GATES - 4) // 2) as i:
                for j in (2, 3):
                    slot_a(j, i)
                    slot_b(j, i)
            for j in (GATES - 2, GATES - 1):
                slot_a(j, 0)
                slot_b(j, 0)

        def conv_w(name, tap, j):
            return prm_col("ffn_conv", (0 if name == "up0" else 3 * GATES) + tap * GATES + j)

        def dve_gated(dve, name):
            lin = LIN[name]
            p0 = PAIR0[name]
            a0 = ACT0[name]

            def product(j, i):
                dve.wait_ge(S("silu_done"), p0 + j + 1 + 2 * i)
                dve.wait_ge(evac_done, lin.tile0 + 2 * j + 2 + 4 * i)
                nc.vector.tensor_tensor(av[:, j % 2, :], sg[:, j % 2, :], vr[:, j % 2, :],
                                        ALU.mult).then_inc(a_ready, 1)

            def low(j, i):
                dve.wait_ge(a_hi_ready, a0 + j + 1 + 2 * i)
                nc.vector.tensor_tensor(a_lo[:, j + 2 * i, :], av[:, j % 2, :],
                                        a_hi[:, j + 2 * i, :].bitcast(F32),
                                        ALU.subtract).then_inc(a_lo_ready, 1)

            def slot_a(j, i):
                dve_rest(dve, lin.piece0 + 2 * j + AHEAD, i, 4)
                if j == 0:
                    dve_rstd(dve, name)
                if j:
                    product(j - 1, i)
                wait_tile(dve, lin, 2 * j, i, 4)
                nc.vector.tensor_tensor(gb[:, j % 2, IN_UP:], tile_bank(lin, 2 * j)[:, 0:T], rstd[:],
                                        ALU.mult).then_inc(evac_done, 1)

            def slot_b(j, i):
                g = gb[:, j % 2, :]
                dve_rest(dve, lin.piece0 + 2 * j + 1 + AHEAD, i, 4)
                dve.wait_ge(S("tap_done"), p0 + j + 1 + 2 * i)
                nc.vector.scalar_tensor_tensor(out=cb[:, j % 2, :], in0=g[:, IN_UP - 1:IN_UP - 1 + T],
                                               scalar=conv_w(name, 1, j + 2 * i), in1=cb[:, j % 2, :],
                                               op0=ALU.mult, op1=ALU.add).then_inc(S("tap2_done"), 1)
                wait_tile(dve, lin, 2 * j + 1, i, 4)
                nc.vector.tensor_tensor(vr[:, j % 2, :], tile_bank(lin, 2 * j + 1)[:, 0:T], rstd[:],
                                        ALU.mult).then_inc(evac_done, 1)
                dve.wait_ge(S("tap2_done"), p0 + j + 1 + 2 * i)
                nc.vector.scalar_tensor_tensor(out=cb[:, j % 2, :], in0=g[:, IN_UP - 2:IN_UP - 2 + T],
                                               scalar=conv_w(name, 0, j + 2 * i), in1=cb[:, j % 2, :],
                                               op0=ALU.mult, op1=ALU.add).then_inc(S("conv_done"), 1)
                if j:
                    low(j - 1, i)

            gated_slots(dve, name, slot_a, slot_b)
            product(GATES - 1, 0)
            low(GATES - 1, 0)

        def act_gated(act, name):
            lin = LIN[name]
            p0 = PAIR0[name]
            a0 = ACT0[name]

            def high(j, i):
                act.wait_ge(a_ready, p0 + j + 1 + 2 * i)
                nc.scalar.activation(a_hi[:, j + 2 * i, :], av[:, j % 2, :],
                                     ACT.Copy).then_inc(a_hi_ready, 1)

            def slot_a(j, i):
                act_round(act, lin.piece0 + 2 * j + AHEAD, i, 4)
                if j == 0:
                    act_std(act, name)
                else:
                    silu(j - 1, i)

            def slot_b(j, i):
                act_round(act, lin.piece0 + 2 * j + 1 + AHEAD, i, 4)
                act.wait_ge(evac_done, lin.tile0 + 2 * j + 1 + 4 * i)
                nc.scalar.activation(cb[:, j % 2, :], gb[:, j % 2, IN_UP:], ACT.Copy,
                                     scale=conv_w(name, 2, j + 2 * i)).then_inc(S("tap_done"), 1)
                if j:
                    high(j - 1, i)

            def silu(j, i):
                act.wait_ge(S("conv_done"), p0 + j + 1 + 2 * i)
                nc.scalar.activation(sg[:, j % 2, :], cb[:, j % 2, :],
                                     ACT.Silu).then_inc(S("silu_done"), 1)

            gated_slots(act, name, slot_a, slot_b)
            silu(GATES - 1, 0)
            high(GATES - 1, 0)


        (qkv, zs, expb, decb, betab, a_t, qk_t, dm, bt, bv, braw, ba, g1, g2, g3, l2s, l2r, colsb,
         ecol, negc, dlast, kdc, glast) = U([
            ("qkv", [P, 12, T]), ("zs", [P, 4, T]), ("expb", [P, 4, T]), ("decb", [P, 4, T]),
            ("betab", [P, 4, T]), ("a_t", [P, 3, 512]), ("qk_t", [P, 3, 512]), ("dm", [P, 3, 512]),
            ("bt", [P, 3, 512]), ("bv", [P, 3, 512]), ("braw", [36, T]), ("ba", [36, T]),
            ("g1", [36, T]), ("g2", [36, T]), ("g3", [36, T]), ("l2s", [8, T]), ("l2r", [8, T]),
            ("colsb", [P, 3, 36]), ("ecol", [P, 3, 4]), ("negc", [P, 3, 4]), ("dlast", [P, 3, 4]),
            ("kdc", [P, 3, 4]), ("glast", [P, 3, 4])], u_at)
        squares_at = u_at + 12 * T + 4 * 4 * T
        sqb, _ = place(squares_at, "sqb", [P, 8, T])
        kd, _ = place(squares_at + 2 * 3 * 512, "kd", [P, 3, 512])
        oT = place(where[y_hi.name] + 4 * T, "oT", [P, 4, T])[0]
        pb, _ = place(u_at + 12 * T + 3 * 4 * T, "pb", [P, 2, 512])
        state, _ = place(squares_at + 3 * 3 * 512, "state", [P, 2, 4, P])
        xm, _ = place(u_at + 8 * T, "xm", [P, 2, 512])
        xt, _ = place(u_at + 12 * T + 2 * 4 * T, "xt", [P, 2, 512])
        rr, at = place(where[y_lo.name] + 4 * T, "rr", [P, 512])
        vn, _ = place(at, "vn", [P, 512])
        gates_at = squares_at + 5 * 3 * 512 + 2 * T
        xm0, _ = place(gates_at, "xm0", [META, 4 * META])
        pb0, _ = place(gates_at + T, "pb0", [META, 4 * META])
        xt0, _ = place(gates_at + 2 * T, "xt0", [META, 4 * META])
        QKV = 12
        BA = 12
        Z0 = 13
        A0_TILE = 17

        def mix_slots(eng, slot):
            for t in range(4):
                slot(t, 0)
            with eng.Fori(0, QKV // 4 - 1) as i:
                for t in range(4, 8):
                    slot(t, i)

        def dn_w(tap, f):
            return prm_col("dn_conv", tap * QKV + f)

        INV_BANKS = {1: (bank[0][:, :], bank[5][:, :], bank[6][:, :]),
                     2: (bank[1][:, :], bank[7][:, :], bank[2][:, :]),
                     0: tuple(bank[4][:, 4 * META * i:4 * META * (i + 1)] for i in range(3))}
        BC = (bank[0], bank[1], bank[2], bank[7])
        ROWS = [(x, n) for x in (8, 4) for n in range(3)]
        SIDE0 = 13
        SIDES = 16
        LEVELS = {0: 4, 1: 7, 2: 7}
        INVERSE = [(level, n) for level in range(1, 8) for n in (1, 2, 0) if level <= LEVELS[n]]
        bt_ready = [S(f"bt_ready{n}") for n in range(3)]
        p_done = [S(f"p_done{n}") for n in range(3)]
        p_ready = [S(f"p_ready{n}") for n in range(3)]
        y_done = [S(f"y_done{n}") for n in range(3)]
        xt_ready = [S(f"xt_ready{n}") for n in range(3)]

        def by_head(ap):
            return ap.rearrange("p (h c) -> p h c", h=4)

        def yt_bank(n):
            return INV_BANKS[n][2][:, 0:4 * CH[n][1]]

        def half(ap, level, odd):
            return ap.rearrange("p (g x b) -> p g x b", x=2, b=1 << (level - 1))[:, :, odd, :]

        def xm_of(n):
            return xm0[:, :] if n == 0 else xm[:, n - 1, :]

        def xt_of(n):
            return xt0[:, :] if n == 0 else xt[:, n - 1, :]

        def dve_mix(dve, name):
            lin = LIN[name]

            def conv(t, i, *between):
                g = gb[:, t % 2, :]
                dve.wait_ge(S("mix_tap3"), t + 1 + 4 * i)
                taps = ((2, S("mix_tap2")), (1, S("mix_tap1")), (0, S("mix_conv")))
                for (tap, done), other in zip(taps, between):
                    nc.vector.scalar_tensor_tensor(
                        out=cb[:, t % 2, :], in0=g[:, tap:tap + T], scalar=dn_w(tap, t + 4 * i),
                        in1=cb[:, t % 2, :], op0=ALU.mult, op1=ALU.add).then_inc(done, 1)
                    other()
                    if tap:
                        dve.wait_ge(done, t + 1 + 4 * i)

            def slot(t, i):
                def read_out():
                    wait_tile(dve, lin, t, i, 4)
                    nc.vector.tensor_tensor(gb[:, t % 2, IN_UP:], tile_bank(lin, t)[:, 0:T], rstd[:],
                                            ALU.mult).then_inc(evac_done, 1)

                dve_rest(dve, lin.piece0 + t + AHEAD, i, 4)
                if t == 0:
                    dve_rstd(dve, name)
                    read_out()
                else:
                    conv(t - 1, i, nothing, read_out, nothing)

            def nothing():
                pass

            def plain(t, dst, n=P):
                wait_tile(dve, lin, t)
                nc.vector.tensor_tensor(dst, tile_bank(lin, t)[0:n, 0:T], rstd[0:n, :],
                                        ALU.mult).then_inc(evac_done, 1)

            def side(k):
                t = SIDE0 + k
                j, part = (k - 4) // 3, (k - 4) % 3
                if k < 4:
                    plain(t, zs[:, k, :])
                else:
                    plain(t, (vr[:, 0, :], vr[:, 1, :], sg[:, 0, :])[part])
                dve_rest(dve, lin.piece0 + t + AHEAD)
                if k < 4:
                    return
                if part == 1 and j:
                    y_low(dve, "mix_out", j - 1, av[:, (j - 1) % 2, :])
                if part == 2:
                    dve.wait_ge(S("glu_tap"), j + 1)
                    g = gb[:, j % 2, :]
                    for tap in (1, 0):
                        dve_link(dve, nc.vector.scalar_tensor_tensor(
                            out=cb[:, j % 2, :], in0=g[:, 1 + tap:1 + tap + T],
                            scalar=prm_col("conv_a", tap * 4 + j), in1=cb[:, j % 2, :],
                            op0=ALU.mult, op1=ALU.add))
                    dve.wait_ge(evac_done, lin.tile0 + t + 1)
                    nc.vector.tensor_tensor(av[:, j % 2, :], cb[:, j % 2, :], sg[:, 0, :],
                                            ALU.mult).then_inc(S("y_ready"), 1)
                if k == SIDES - 1:
                    y_low(dve, "mix_out", 3, av[:, 1, :])

            mix_slots(dve, slot)
            dve.wait_ge(S("rel_done"), 1)
            nc.vector.tensor_tensor(relv[:], bank[7][0:HEADS, 0:VLEN], C("future", HEADS),
                                    ALU.add).then_inc(S("rel_ready"), 1)
            dve_rest(dve, lin.piece0 + BA + AHEAD)
            conv(QKV - 1, 0, nothing, lambda: plain(BA, braw[:, :], 36), nothing)
            for k in range(4):
                side(k)
            dve.wait_ge(S("gates_act"), 1)
            dve_link(dve, nc.vector.tensor_scalar(g3[0:4, :], braw[0:4, :], prm_col("dt_bias", 0, 4), 0.0,
                                                  ALU.add, ALU.max))
            dve_link(dve, nc.vector.tensor_tensor(g3[0:4, :], g3[0:4, :], g2[0:4, :], ALU.add))
            dve_link(dve, nc.vector.tensor_scalar(g3[0:4, :], g3[0:4, :], small[0:4, 0:1], -1.0,
                                                  ALU.mult, ALU.mult))
            dve.wait_ge(S("cleared"), 2)
            for t0, c in CH:
                nc.vector.tensor_tensor_scan(ba[0:4, t0:t0 + c], C("ones", 4)[:, 0:1].to_broadcast([4, c]),
                                             g3[0:4, t0:t0 + c], 0.0, ALU.mult,
                                             ALU.add).then_inc(S("rows_ready"), 1)
            dve_link(dve, nc.vector.tensor_scalar(g1[32:36, :], g1[32:36, :], 1.0, None, ALU.add))
            nc.vector.reciprocal(ba[32:36, :], g1[32:36, :]).then_inc(S("rows_ready"), 1)

            side(4)
            dve.wait_ge(S("cols_ps"), 1)
            nc.vector.tensor_copy(colsb[0:META, 0, :], bank[6][0:META, 0:36]).then_inc(S("cols_ready"), 1)
            nc.vector.tensor_copy(colsb[:, 1:3, :], bank[6][:, 36:108].rearrange(
                "p (n k) -> p n k", n=2)).then_inc(S("cols_ready"), 1)
            for hd in range(4):
                dve.wait_ge(S("bc_done"), 4 + hd + 1)
                nc.vector.tensor_copy(betab[:, hd, :], BC[hd][:, 0:T]).then_inc(S("bc_read"), 1)
            dve.wait_ge(S("l2_std"), 1)
            nc.vector.reciprocal(l2r[:], l2s[:]).then_inc(S("l2_ready"), 1)
            side(5)
            for f in range(8):
                dve.wait_ge(S("bc_done"), 8 + f + 1)
                if f == 0:
                    dve.wait_ge(S("mix_silu"), QKV)
                nc.vector.scalar_tensor_tensor(
                    out=qkv[:, f, :], in0=qkv[:, f, :], scalar=P ** -0.5 if f < 4 else 1.0,
                    in1=BC[f % 4][:, 0:T], op0=ALU.mult, op1=ALU.mult).then_inc(S("bc_read"), 1)
            dve.wait_ge(S("cols_ready"), 2)
            dve.wait_ge(S("decb_ready"), 4)
            for n, (t0, c) in enumerate(CH):
                for hd in range(4):
                    ins = nc.vector.tensor_scalar(dm[0:c, n, hd * c:(hd + 1) * c], decb[0:c, hd, t0:t0 + c],
                                                  colsb[0:c, n, hd:hd + 1], 0.0, ALU.subtract, ALU.min)
                ins.then_inc(S("diff_ready"), 1)
                nc.vector.tensor_copy(dlast[:, n, :], decb[:, :, t0 + c - 1]).then_inc(S("dlast_ready"), 1)
            dve.wait_ge(S("dlast_ready"), 3)
            nc.vector.tensor_tensor(kdc[:], dlast[:], colsb[:, :, 0:4], ALU.subtract).then_inc(
                S("dlast_ready"), 1)
            dve.wait_ge(S("exps_ready"), 1)
            nc.vector.scalar_tensor_tensor(out=negc[:], in0=ecol[:], scalar=-1.0, in1=colsb[:, :, 32:36],
                                           op0=ALU.mult, op1=ALU.mult).then_inc(S("negc_ready"), 1)
            side(6)
            for n, (t0, c) in enumerate(CH):
                w = 4 * c
                dve.wait_ge(S("dm_ready"), n + 1)
                dve.wait_ge(S("gram_done"), 2 * n + 1)
                dve_link(dve, nc.vector.tensor_tensor(a_t[0:c, n, 0:w], bank[n][0:c, 0:w], dm[0:c, n, 0:w],
                                                      ALU.mult))
                a3 = a_t[0:c, n, 0:w].rearrange("p (h c) -> p h c", h=4)
                dve_link(dve, nc.vector.tensor_tensor(a3, a3, betab[0:c, :, t0:t0 + c], ALU.mult))
                nc.vector.tensor_tensor(a3, a3, C("strict", c)[:, 0:c].unsqueeze(1).to_broadcast([c, 4, c]),
                                        ALU.mult).then_inc(S("a_t_ready"), 1)
                dve.wait_ge(S("gram_done"), 2 * n + 2)
                dve_link(dve, nc.vector.tensor_tensor(qk_t[0:c, n, 0:w], bank[5 + n][0:c, 0:w],
                                                      dm[0:c, n, 0:w], ALU.mult))
                q3 = qk_t[0:c, n, 0:w].rearrange("p (h c) -> p h c", h=4)
                nc.vector.tensor_tensor(q3, q3, C("incl", c)[:, 0:c].unsqueeze(1).to_broadcast([c, 4, c]),
                                        ALU.mult).then_inc(S("qk_t_ready"), 1)
            side(7)
            for level, n in INVERSE:
                t0, c = CH[n]
                w = 4 * c
                if n == 1 and 2 <= level <= 6:
                    side(7 + level)
                if level == 1:
                    dve.wait_ge(bt_ready[n], 1)
                    nc.vector.tensor_tensor(by_head(xt_of(n)[0:c, 0:w]),
                                            ident[0:c, 0:c].unsqueeze(1).to_broadcast([c, 4, c]),
                                            by_head(bt[0:c, n, 0:w]), ALU.subtract).then_inc(xt_ready[n], 1)
                    if n == 0:
                        side(8)
                    continue
                dve.wait_ge(y_done[n], level - 1)
                if level < LEVELS[n]:
                    x = half(xm_of(n)[0:c, 0:w], level, 0)
                    nc.vector.tensor_tensor(x, x, half(INV_BANKS[n][1][0:c, 0:w], level, 0),
                                            ALU.subtract).then_inc(S("x_ready"), 1)
                x = half(xt_of(n)[0:c, 0:w], level, 1)
                nc.vector.tensor_tensor(x, x, half(yt_bank(n)[0:c, :], level, 1),
                                        ALU.subtract).then_inc(xt_ready[n], 1)
            dve.wait_ge(S("rows_read"), 6)
            dve.wait_ge(S("negc_ready"), 1)
            for n, (t0, c) in enumerate(CH):
                if n:
                    dve.wait_ge(S("ks_done"), n)
                    for hd in range(4):
                        hs = slice(hd * P, (hd + 1) * P)
                        ins = nc.vector.scalar_tensor_tensor(
                            out=rr[0:c, hs], in0=bank[0][0:c, hs], scalar=negc[0:c, n, hd:hd + 1],
                            in1=bv[0:c, n, hs], op0=ALU.mult, op1=ALU.add)
                    ins.then_inc(S("r_ready"), 1)
                if n < 2:
                    dve.wait_ge(S("su_done"), n + 1)
                    for hd in range(4):
                        hs = slice(hd * P, (hd + 1) * P)
                        if n == 0:
                            ins = nc.vector.tensor_copy(state[:, 0, hd, :], bank[4][:, hs])
                        else:
                            ins = nc.vector.scalar_tensor_tensor(
                                out=state[:, n, hd, :], in0=state[:, n - 1, hd, :], scalar=glast[:, n, hd:hd + 1],
                                in1=bank[4][:, hs], op0=ALU.mult, op1=ALU.add)
                    ins.then_inc(S("state_ready"), 1)
                    dve.wait_ge(S("state_ready"), n + 1)
            dve.wait_ge(S("o_ready"), 3)
            dve.wait_ge(S("z_ready"), 4)
            for hd in range(4):
                nc.vector.scalar_tensor_tensor(out=zs[:, hd, :], in0=oT[:, hd, :], scalar=prm_col("dn_norm"),
                                               in1=zs[:, hd, :], op0=ALU.mult,
                                               op1=ALU.mult).then_inc(S("oz_ready"), 1)
            side(14)
            dve.wait_ge(S("on_std"), 1)
            nc.vector.reciprocal(l2r[0:4, :], l2s[0:4, :]).then_inc(S("on_ready"), 1)
            side(15)
            dve.wait_ge(S("oz_ready"), 4)
            for hd in range(4):
                dve.wait_ge(S("on_bc"), hd + 1)
                nc.vector.tensor_tensor(zs[:, hd, :], zs[:, hd, :], bank[4 + hd][:, 0:T],
                                        ALU.mult).then_inc(S("y_ready"), 1)
            for hd in range(4):
                y_low(dve, "mix_out", 4 + hd, zs[:, hd, :])

        def y_low(dve, name, c, y, a=0, n=T):
            dve.wait_ge(y_hi_ready, Y0[name] + c + 1)
            nc.vector.tensor_tensor(y_lo[:, c, a:a + n], y, y_hi[:, c, a:a + n].bitcast(F32),
                                    ALU.subtract).then_inc(y_lo_ready, 1)

        def act_mix(act, name):
            lin = LIN[name]

            def silu(t, i):
                act.wait_ge(S("mix_conv"), t + 1 + 4 * i)
                nc.scalar.activation(qkv[:, t + 4 * i, :], cb[:, t % 2, :],
                                     ACT.Silu).then_inc(S("mix_silu"), 1)

            def slot(t, i):
                act_round(act, lin.piece0 + t + AHEAD, i, 4)
                if t == 0:
                    act_std(act, name)
                else:
                    tap3(t - 1, i)
                if t > 1:
                    silu(t - 2, i)

            def tap3(t, i):
                act.wait_ge(evac_done, lin.tile0 + t + 1 + 4 * i)
                if t > 1:
                    act.wait_ge(S("mix_silu"), t - 1 + 4 * i)
                nc.scalar.activation(cb[:, t % 2, :], gb[:, t % 2, IN_UP:], ACT.Copy,
                                     scale=dn_w(3, t + 4 * i)).then_inc(S("mix_tap3"), 1)

            def side(k):
                t = SIDE0 + k
                j, part = (k - 4) // 3, (k - 4) % 3
                act_round(act, lin.piece0 + t + AHEAD)
                if k < 4:
                    act.wait_ge(evac_done, lin.tile0 + t + 1)
                    nc.scalar.activation(zs[:, k, :], zs[:, k, :], ACT.Silu).then_inc(S("z_ready"), 1)
                elif part == 0 and j:
                    y_high(act, "mix_out", j - 1, av[:, (j - 1) % 2, :], j)
                elif part == 2:
                    act.wait_ge(S("glu_ready"), j + 1)
                    nc.scalar.activation(cb[:, j % 2, :], gb[:, j % 2, IN_UP:], ACT.Copy,
                                         scale=prm_col("conv_a", 8 + j)).then_inc(S("glu_tap"), 1)
                if k == SIDES - 1:
                    y_high(act, "mix_out", 3, av[:, 1, :], 4)

            mix_slots(act, slot)
            act_round(act, lin.piece0 + BA + AHEAD)
            tap3(QKV - 1, 0)
            silu(QKV - 2, 0)
            silu(QKV - 1, 0)
            for k in range(2):
                side(k)
            act.wait_ge(evac_done, lin.tile0 + BA + 1)
            act_link(act, nc.scalar.activation(g1[0:4, :], braw[0:4, :], ACT.Abs,
                                               bias=prm_col("dt_bias", 0, 4)))
            act_link(act, nc.scalar.activation(g1[0:4, :], g1[0:4, :], ACT.Exp, scale=-1.0))
            nc.scalar.activation(g1[32:36, :], braw[32:36, :], ACT.Exp, scale=-1.0)
            nc.scalar.activation(small[0:4, 0:1], prm_col("a_log", 0, 4), ACT.Exp)
            nc.scalar.activation(g2[0:4, :], g1[0:4, :], ACT.Ln, bias=1.0).then_inc(S("gates_act"), 1)
            for k in range(2, 4):
                side(k)
            act.wait_ge(S("l2_sum"), 1)
            nc.scalar.activation(l2s[:], bank[5][0:8, 0:T], ACT.Sqrt, bias=eps[0:8, 0:1],
                                 scale=1.0).then_inc(S("l2_std"), 1)
            side(4)
            for hd in range(4):
                act.wait_ge(S("bc_done"), hd + 1)
                nc.scalar.activation(decb[:, hd, :], BC[hd][:, 0:T], ACT.Copy).then_inc(
                    S("decb_ready"), 1)
                nc.scalar.activation(expb[:, hd, :], BC[hd][:, 0:T], ACT.Exp).then_inc(
                    S("expb_ready"), 1)
            side(5)
            act.wait_ge(S("cols_ready"), 2)
            nc.scalar.activation(ecol[:], colsb[:, :, 0:4], ACT.Exp).then_inc(S("exps_ready"), 1)
            act.wait_ge(S("dlast_ready"), 3)
            nc.scalar.activation(glast[:], dlast[:], ACT.Exp).then_inc(S("exps_ready"), 1)
            act.wait_ge(S("dlast_ready"), 4)
            act_link(act, nc.scalar.activation(kdc[:], kdc[:], ACT.Exp))
            for n, (t0, c) in enumerate(CH):
                act.wait_ge(S("diff_ready"), n + 1)
                nc.scalar.activation(dm[0:c, n, 0:4 * c], dm[0:c, n, 0:4 * c],
                                     ACT.Exp).then_inc(S("dm_ready"), 1)
            side(6)
            for i, (x, n) in enumerate(ROWS):
                c = CH[n][1]
                if i == 3:
                    act.wait_ge(S("qk_t_ready"), 3)
                    side(7)
                act.wait_ge(S("rows_done"), i + 1)
                for hd in range(4):
                    hs = slice(hd * P, (hd + 1) * P)
                    ins = nc.scalar.activation(
                        (bv if x == 8 else kd)[0:c, n, hs], bank[4 - 4 * (i % 2)][0:c, hs], ACT.Copy,
                        scale=colsb[0:c, n, 32 + hd:33 + hd] if x == 8 else kdc[0:c, n, hd:hd + 1])
                ins.then_inc(S("rows_read"), 1)
            for level, n in INVERSE:
                t0, c = CH[n]
                w = 4 * c
                act.wait_ge(p_done[n], level)
                dst = xm_of(n)[0:c, 0:w] if level == 1 else p_of(n)[0:c, 0:w]
                nc.scalar.activation(dst, INV_BANKS[n][0][0:c, 0:w], ACT.Copy).then_inc(p_ready[n], 1)
                if level <= 6 and n == (0 if level <= LEVELS[0] else 2):
                    side(7 + level)
            for n, (t0, c) in enumerate(CH):
                act.wait_ge(S("vn_done"), n + 1)
                nc.scalar.activation(vn[0:c, :], bank[1][0:c, :], ACT.Copy).then_inc(S("vn_ready"), 1)
                act.wait_ge(S("ot_done"), n + 1)
                nc.scalar.activation(oT[:, :, t0:t0 + c], bank[2][:, 0:4 * c].rearrange(
                    "p (h c) -> p h c", h=4), ACT.Copy).then_inc(S("o_ready"), 1)
                if n == 2:
                    side(14)
            act.wait_ge(S("on_sum"), 1)
            nc.scalar.activation(l2s[0:4, :], bank[5][0:4, 0:T], ACT.Sqrt, bias=eps[0:4, 0:1],
                                 scale=1.0 / P).then_inc(S("on_std"), 1)
            side(15)
            for hd in range(4):
                y_high(act, "mix_out", 4 + hd, zs[:, hd, :], 5 + hd)

        def p_of(n):
            return pb0[:, :] if n == 0 else pb[:, n - 1, :]

        def y_high(act, name, c, y, count, a=0, n=T):
            act.wait_ge(S("y_ready"), count)
            nc.scalar.activation(y_hi[:, c, a:a + n], y, ACT.Copy).then_inc(y_hi_ready, 1)

        def pool_mix(pool, name):
            nc.gpsimd.memset(ba[:], 0.0).then_inc(S("cleared"), 1)
            nc.gpsimd.memset(colsb[:], 0.0).then_inc(S("cleared"), 1)
            for f in range(8):
                pool.wait_ge(S("mix_silu"), f + 1)
                nc.gpsimd.tensor_tensor(sqb[:, f, :], qkv[:, f, :], qkv[:, f, :],
                                        ALU.mult).then_inc(S("sqk_ready"), 1)

            def glu(j):
                pool.wait_ge(evac_done, LIN[name].tile0 + A0_TILE + 3 * j + 2)
                nc.gpsimd.tensor_tensor(gb[:, j % 2, IN_UP:], vr[:, 0, :], vr[:, 1, :],
                                        ALU.mult).then_inc(S("glu_ready"), 1)

            glu(0)
            pool.wait_ge(S("bc_read"), 8)
            pool.wait_ge(S("expb_ready"), 4)
            nc.gpsimd.tensor_tensor(expb[:], qkv[:, 0:4, :], expb[:], ALU.mult).then_inc(S("qd_ready"), 1)
            for level, n in INVERSE:
                t0, c = CH[n]
                w = 4 * c
                if level == 1:
                    pool.wait_ge(S("a_t_ready"), n + 1)
                elif level == 2:
                    pool.wait_ge(xt_ready[n], 1)
                else:
                    pool.wait_ge(p_done[n], level - 1)
                m = C("levels", c)[:, (level - 1) * P:(level - 1) * P + c]
                nc.gpsimd.tensor_tensor(by_head(bt[0:c, n, 0:w]), by_head(a_t[0:c, n, 0:w]),
                                        m.unsqueeze(1).to_broadcast([c, 4, c]),
                                        ALU.mult).then_inc(bt_ready[n], 1)
                if (level, n) in ((2, 0), (5, 2)):
                    glu(1 + (2, 5).index(level))
            pool.wait_ge(S("o_ready"), 3)
            nc.gpsimd.tensor_tensor(qkv[:, 8:12, :], oT[:], oT[:], ALU.mult).then_inc(S("osq_ready"), 1)
            glu(3)

        def pe_mix(pe, name):
            lin = LIN[name]
            pe_linear(pe, name, SIDE0)

            def side(k):
                if k >= 4:
                    pe.wait_ge(evac_done, lin.tile0 + SIDE0 + k)
                pe_tile(pe, lin, SIDE0 + k)

            for k in range(4):
                side(k)
            for f in range(8):
                pe.wait_ge(S("sqk_ready"), f + 1)
                mm = nc.tensor.matmul(bank[5][0:8, 0:T], C("head128")[:, 7 - f:15 - f], sqb[:, f, :],
                                      start=(f == 0), stop=(f == 7))
            mm.then_inc(S("l2_sum"), 1)
            side(4)
            pe.wait_ge(S("rows_ready"), 4)
            for n, (t0, c) in enumerate(CH):
                tr = nc.tensor.transpose(bank[6][0:c, n * 36:(n + 1) * 36], ba[0:36, t0:t0 + c],
                                         ident[0:36, 0:36])
            tr.then_inc(S("cols_ps"), 1)
            for b in range(16):
                if b == 8:
                    side(5)
                if 4 <= b < 8:
                    pe.wait_ge(S("expb_ready"), b - 4 + 1)
                if b >= 8:
                    pe.wait_ge(S("bc_read"), b - 8 + 1)
                    if b == 8:
                        pe.wait_ge(S("l2_ready"), 1)
                rows = 36 if b < 8 else 8
                col = (b, 32 + b - 4, b - 8)[min(b // 4, 2)]
                nc.tensor.matmul(BC[b % 4][:, 0:T], ident[0:rows, col:col + 1].to_broadcast([rows, P]),
                                 (ba if b < 8 else l2r)[0:rows, :], start=True,
                                 stop=True).then_inc(S("bc_done"), 1)
            side(6)
            pe.wait_ge(S("bc_read"), 12)
            for n, (t0, c) in enumerate(CH):
                for x, bk in ((4, bank[n]), (0, bank[5 + n])):
                    for hd in range(4):
                        k_ap = qkv[:, 4 + hd, t0:t0 + c]
                        mm = nc.tensor.matmul(bk[0:c, hd * c:(hd + 1) * c], k_ap,
                                              qkv[:, x + hd, t0:t0 + c], start=True, stop=True)
                    mm.then_inc(S("gram_done"), 1)
            side(7)
            pe.wait_ge(S("a_t_ready"), 1)
            for i, (x, n) in enumerate(ROWS):
                t0, c = CH[n]
                if i >= 2:
                    pe.wait_ge(S("rows_read"), i - 1)
                for hd in range(4):
                    tr = nc.tensor.transpose(bank[4 - 4 * (i % 2)][0:c, hd * P:(hd + 1) * P],
                                             qkv[:, x + hd, t0:t0 + c], ident)
                tr.then_inc(S("rows_done"), 1)
            side(8)
            pe.wait_ge(S("qk_t_ready"), 3)
            pe.wait_ge(S("rows_read"), 6)
            for level in range(1, 8):
                for n in (1, 2, 0):
                    if level > LEVELS[n]:
                        continue
                    t0, c = CH[n]
                    pbank = INV_BANKS[n][0]
                    if level == 1:
                        pe.wait_ge(xt_ready[n], 1)
                        for hd in range(4):
                            hs = slice(hd * c, (hd + 1) * c)
                            mm = nc.tensor.transpose(pbank[0:c, hs], xt_of(n)[0:c, hs], ident[0:c, 0:c])
                    else:
                        pe.wait_ge(bt_ready[n], level)
                        if level == 2:
                            pe.wait_ge(p_ready[n], 1)
                        else:
                            pe.wait_ge(xt_ready[n], level - 1)
                        for hd in range(4):
                            hs = slice(hd * c, (hd + 1) * c)
                            mm = nc.tensor.matmul(pbank[0:c, hs], bt[0:c, n, hs], xm_of(n)[0:c, hs],
                                                  start=True, stop=True)
                    mm.then_inc(p_done[n], 1)
                if level <= 5:
                    side(8 + level)
                for n in (1, 2, 0):
                    if level == 1 or level > LEVELS[n]:
                        continue
                    t0, c = CH[n]
                    pe.wait_ge(p_ready[n], level)
                    p = p_of(n)
                    for hd in range(4):
                        hs = slice(hd * c, (hd + 1) * c)
                        if level < LEVELS[n]:
                            nc.tensor.matmul(half(INV_BANKS[n][1][0:c, hs], level, 0), xt_of(n)[0:c, hs],
                                             half(p[0:c, hs], level, 0), start=True, stop=True)
                        mm = nc.tensor.matmul(half(yt_bank(n)[0:c, hs], level, 1), p[0:c, hs],
                                              half(xt_of(n)[0:c, hs], level, 1), start=True, stop=True)
                    mm.then_inc(y_done[n], 1)
            for n, (t0, c) in enumerate(CH):
                if n:
                    pe.wait_ge(S("state_ready"), n)
                    for hd in range(4):
                        mm = nc.tensor.matmul(bank[0][0:c, hd * P:(hd + 1) * P], qkv[:, 4 + hd, t0:t0 + c],
                                              state[:, n - 1, hd, :], start=True, stop=True)
                    mm.then_inc(S("ks_done"), 1)
                    pe.wait_ge(S("r_ready"), n)
                pe.wait_ge(xt_ready[n], LEVELS[n])
                for hd in range(4):
                    hs = slice(hd * P, (hd + 1) * P)
                    mm = nc.tensor.matmul(bank[1][0:c, hs], xt_of(n)[0:c, hd * c:(hd + 1) * c],
                                          rr[0:c, hs] if n else bv[0:c, n, hs], start=True, stop=True)
                mm.then_inc(S("vn_done"), 1)
                pe.wait_ge(S("vn_ready"), n + 1)
                if n < 2:
                    if n == 0:
                        pe.wait_ge(p_ready[0], LEVELS[0])
                    for hd in range(4):
                        hs = slice(hd * P, (hd + 1) * P)
                        mm = nc.tensor.matmul(bank[4][:, hs], kd[0:c, n, hs], vn[0:c, hs],
                                              start=True, stop=True)
                    mm.then_inc(S("su_done"), 1)
                if n:
                    pe.wait_ge(S("o_ready"), n)
                    pe.wait_ge(S("qd_ready"), 1)
                else:
                    pe.wait_ge(xt_ready[2], LEVELS[2])
                for hd in range(4):
                    out = bank[2][:, hd * c:(hd + 1) * c]
                    if n:
                        nc.tensor.matmul(out, state[:, n - 1, hd, :], expb[:, hd, t0:t0 + c], start=True,
                                         stop=False)
                    mm = nc.tensor.matmul(out, vn[0:c, hd * P:(hd + 1) * P],
                                          qk_t[0:c, n, hd * c:(hd + 1) * c], start=(n == 0), stop=True)
                mm.then_inc(S("ot_done"), 1)
            side(14)
            pe.wait_ge(S("osq_ready"), 1)
            for hd in range(4):
                mm = nc.tensor.matmul(bank[5][0:4, 0:T], C("head128")[:, 7 - hd:11 - hd],
                                      qkv[:, 8 + hd, :], start=(hd == 0), stop=(hd == 3))
            mm.then_inc(S("on_sum"), 1)
            side(15)
            pe.wait_ge(S("on_ready"), 1)
            for hd in range(4):
                nc.tensor.matmul(bank[4 + hd][:, 0:T], ident[0:4, hd:hd + 1].to_broadcast([4, P]),
                                 l2r[0:4, :], start=True, stop=True).then_inc(S("on_bc"), 1)

        def store_rounds(eng, lin, slot):
            for t in range(4):
                slot(t, 0)
            rounds = lin.tiles // 4 - 1
            if rounds > 0:
                with eng.Fori(0, rounds) as i:
                    for t in range(4, 8):
                        slot(t, i)
            for t in range(4 * (rounds + 1), lin.tiles):
                slot(t, 0)

        def dve_store(dve, name, dst):
            lin = LIN[name]
            n = cols(name)[1]

            def slot(t, i):
                dve_rest(dve, lin.piece0 + t + AHEAD, i, 4)
                if t == 0:
                    dve_rstd(dve, name)
                wait_tile(dve, lin, t, i, 4)
                nc.vector.tensor_tensor(dst[:, t + 4 * i, :], tile_bank(lin, t)[:, 0:n],
                                        rstd[:, 0:n], ALU.mult).then_inc(evac_done, 1)

            store_rounds(dve, lin, slot)

        def act_store(act, name):
            lin = LIN[name]

            def slot(t, i):
                act_round(act, lin.piece0 + t + AHEAD, i, 4)
                if t == 0:
                    act_std(act, name)

            store_rounds(act, lin, slot)

        VALUE_STEPS = ((0, P, 0, 0, 2 * P), (1, P, 2 * P, P, P), (2, META, 3 * P, 0, 2 * P))
        attended = {}

        class Attend:

            def __init__(self, name, y, wa, wb, q, k, v, bias_a, bias_b, turns, tiles,
                         sides=None):
                self.name, self.y, self.wa, self.wb = name, y, wa, wb
                self.q, self.k, self.v = q, k, v
                self.bias_a, self.bias_b = bias_a, bias_b
                self.turns = turns
                self.sm, self.pt, self.st = tiles
                self.sink = name == "swa"
                self.sides = sides or {}
                self.score_banks = (bank[5], bank[7]) if sides else tuple(bank[0:4])
                self.out_banks = (bank[6],) if sides else (bank[6], bank[7])
                signals = (("scores", 1), ("max", 2), ("negmax", 1), ("exp", 3 if self.sink else 2),
                           ("den", 1 if self.sink else 0), ("rec", 1), ("p", 2), ("turned", 1),
                           ("pt", 2 if self.sink else 1), ("o", 1))
                self.s = {k: S(f"att_{k}") for k, _ in signals}
                self.before = {k: attended.get(k, 0) for k, _ in signals}
                for k, per_head in signals:
                    attended[k] = self.before[k] + per_head * HEADS

            def wait(self, eng, signal, n):
                eng.wait_ge(self.s[signal], self.before[signal] + n)

            def score_bank(self, u):
                return self.score_banks[u % len(self.score_banks)]

            def out_bank(self, t):
                return self.out_banks[t % len(self.out_banks)]

        def att_pe(pe, at, before=None, tile=None, rows=None):
            s = at.s
            nb, no = len(at.score_banks), len(at.out_banks)

            def turn(u):
                if not 0 <= u < HEADS:
                    return
                at.wait(pe, "p", 2 * u + 2)
                if u:
                    at.wait(pe, "pt", pt_count(at, u))
                for b, dst, keys, c0 in at.turns:
                    tr = nc.tensor.transpose(bank[b][0:keys, dst:dst + P],
                                             at.sm[:, u % 3, c0:c0 + keys], ident)
                tr.then_inc(s["turned"], 1)

            def values(u):
                if not 0 <= u < HEADS:
                    return
                r = slice(HD * (u % 2), HD * (u % 2) + HD)
                ob = at.out_bank(u // 2)
                at.wait(pe, "pt", pt_count(at, u + 1))
                if u % 2 == 0 and u >= 2 * no:
                    pe.wait_ge(y_lo_ready, Y0[at.y] + u // 2 + 1 - no)
                if rows is not None:
                    pe.wait_ge(S("mv_ready"), min(u // 2 + 1 + u % 2, HEADS // 2))
                off = META if at.sink else 0
                if at.sink:
                    if u == 0:
                        pe.wait_ge(S("meta_pt"), 1)
                    nc.tensor.matmul(ob[r, 0:META], at.v(u, 2, META), ptm[:, META * u:META * (u + 1)],
                                     start=True, stop=True)
                last_chunk = 2 if at.sink else 1
                for chunk, keys, src, q0, w in VALUE_STEPS[:last_chunk + 1]:
                    mm = nc.tensor.matmul(ob[r, off + q0:off + q0 + w], at.v(u, chunk, keys),
                                          at.pt[0:keys, u % 2, src:src + w], start=(chunk == 0),
                                          stop=(chunk == last_chunk))
                mm.then_inc(s["o"], 1)

            def scores(heads):
                for u in heads:
                    if u >= nb:
                        at.wait(pe, "max", 2 * (u - nb) + 2)
                    if at.sides and u % 2 == 0:
                        pe.wait_ge(evac_done, LIN["moba_in"].tile0 + 3 * (u // 2) + 2)
                for g, c0, w in ((1, 0, at.wa), (0, at.wa, at.wb)):
                    for u in heads:
                        r = slice(HD * (u % 2), HD * (u % 2) + HD)
                        mm = nc.tensor.matmul(at.score_bank(u)[:, c0:c0 + w], at.q(u, r, g), at.k(u, r, g),
                                              start=True, stop=True)
                        if g == 0:
                            mm.then_inc(s["scores"], 1)

            if not at.sides:
                scores((0, 1))
            for step in range(HEADS + 3):
                if at.sides and step < HEADS:
                    scores((step,))
                elif not at.sides and step % 2 == 1 and step + 1 < HEADS:
                    scores((step + 1, step + 2))
                sides = list(at.sides.get(step, ()))
                if sides:
                    tile(sides.pop(0))
                if rows is not None and step % 2 == 1:
                    values(step - 3)
                    if step < HEADS:
                        rows(step // 2)
                    turn(step - 2)
                    continue
                turn(step - 2)
                if before is not None and step == 2:
                    before(pe)
                for t in sides:
                    tile(t)
                values(step - 3)

        def pt_count(at, heads):
            return heads * (2 if at.sink else 1)

        def att_dve(dve, at, extra=None, tile=None, after=None):
            s = at.s
            for step in range(HEADS + 5):
                u = step
                if u < HEADS:
                    if u >= 3:
                        at.wait(dve, "turned", u - 2)
                    at.wait(dve, "scores", u + 1)
                    if extra is not None:
                        extra(dve, u)
                    for x, (c0, w, bias) in enumerate(((0, at.wa, at.bias_a(u)),
                                                       (at.wa, at.wb, at.bias_b(u)))):
                        nc.vector.tensor_tensor_reduce(
                            out=at.sm[:, u % 3, c0:c0 + w], in0=at.score_bank(u)[:, c0:c0 + w], in1=bias,
                            scale=1.0, scalar=GONE, op0=ALU.add, op1=ALU.max,
                            accum_out=at.st[:, u, x:x + 1]).then_inc(s["max"], 1)
                    at.wait(dve, "max", 2 * u + 2)
                    sink = prm_col("sinks", u) if at.sink else GONE
                    nc.vector.tensor_scalar(at.st[:, u, 2:4], at.st[:, u, 0:2], sink, -1.0, ALU.max,
                                            ALU.mult).then_inc(s["negmax"], 1)
                u = step - 1
                if 0 <= u < HEADS:
                    at.wait(dve, "exp", (3 if at.sink else 2) * (u + 1))
                    den = at.st[:, u, 4:6]
                    if at.sink:
                        nc.vector.tensor_tensor(den, den, at.st[:, u, 6:8], ALU.add).then_inc(s["den"], 1)
                        at.wait(dve, "den", u + 1)
                    nc.vector.reciprocal(at.st[:, u, 8:10], den).then_inc(s["rec"], 1)
                    at.wait(dve, "rec", u + 1)
                    for x, (c0, w) in enumerate(((0, at.wa), (at.wa, at.wb))):
                        nc.vector.tensor_scalar(at.sm[:, u % 3, c0:c0 + w], at.sm[:, u % 3, c0:c0 + w],
                                                at.st[:, u, 8 + x:9 + x], None,
                                                ALU.mult).then_inc(s["p"], 1)
                u = step - (4 if at.sides else 5)
                if u > 0 and u % 2 == 1:
                    o_low(dve, at, u // 2)
                for t in at.sides.get(step, ()):
                    tile(t)
                if after is not None and step == 1:
                    after()

        def o_cols(at):
            return (0, T) if at.sink else (META, SEQ)

        def o_low(dve, at, t):
            a, n = o_cols(at)
            c = Y0[at.y] + t
            dve.wait_ge(y_hi_ready, c + 1)
            nc.vector.tensor_tensor(y_lo[:, t, a:a + n], at.out_bank(t)[:, 0:n],
                                    y_hi[:, t, a:a + n].bitcast(F32), ALU.subtract).then_inc(y_lo_ready, 1)

        def att_act(act, at, tile=None, rows=None, after=None):
            s = at.s
            a, n = o_cols(at)
            for step in range(HEADS + 4 + (1 if at.sides else 0)):
                sides = list(at.sides.get(step, ()))
                u = step - 4
                if at.sides and u > 0 and u % 2 == 1:
                    o_high(act, at, u // 2)
                u = step
                if u < HEADS:
                    at.wait(act, "negmax", u + 1)
                    for x, (c0, w) in enumerate(((0, at.wa), (at.wa, at.wb))):
                        nc.scalar.activation(at.sm[:, u % 3, c0:c0 + w], at.sm[:, u % 3, c0:c0 + w],
                                             ACT.Exp, bias=at.st[:, u, 2 + x:3 + x],
                                             accum_out=at.st[:, u, 4 + x:5 + x]).then_inc(s["exp"], 1)
                    if at.sink:
                        nc.scalar.activation(at.st[:, u, 6:8], at.st[:, u, 2:4], ACT.Exp,
                                             bias=prm_col("sinks", u)).then_inc(s["exp"], 1)
                if sides:
                    tile(sides.pop(0))
                if rows is not None and u % 2 == 1 and u < HEADS:
                    rows(u // 2)
                u = step - 2
                if 0 <= u < HEADS:
                    at.wait(act, "turned", u + 1)
                    if at.sink:
                        copies = ((P, 0, 4, 0, 3 * P), (META, 3 * P, 5, 0, 2 * P))
                    else:
                        copies = ((P, 0, 4, 0, 3 * P),)
                    for keys, dst, bk, src, w in copies:
                        nc.scalar.activation(at.pt[0:keys, u % 2, dst:dst + w], bank[bk][0:keys, src:src + w],
                                             ACT.Copy).then_inc(s["pt"], 1)
                for t in sides:
                    tile(t)
                u = step - 3
                if not at.sides and u > 0 and u % 2 == 1:
                    o_high(act, at, u // 2)
                if after is not None and step == 1:
                    after()

        def o_high(act, at, t):
            a, n = o_cols(at)
            at.wait(act, "o", 2 * t + 2)
            nc.scalar.activation(y_hi[:, t, a:a + n], at.out_bank(t)[:, 0:n], ACT.Copy).then_inc(y_hi_ready, 1)

        qs, sqs, vrow, sm_s, pt_s, st_s, hs20, hr20, smm, ptm, mst = U([
            ("qs", [P, 12, T]), ("sqs", [P, 10, T]), ("vrow", [P, 3, 256]), ("sm_s", [P, 3, 416]),
            ("pt_s", [P, 2, 640]), ("st_s", [P, HEADS, 10]), ("hs20", [20, T]),
            ("hr20", [20, T]), ("smm", [META, 256]), ("ptm", [META, 256]), ("mst", [META, 4, HEADS])], u_at)
        split_at = u_at + 22 * T + 3 * 256 + 3 * 416 + 2 * 640 + HEADS * 10 + 2 * T + 2 * 256 + 4 * HEADS
        sel_r, split_at = place(split_at, "sel_r", [20, 20 * HD], F32R)
        hr_hi, split_at = place(split_at, "hr_hi", [20, T], F32R)
        hr_lo, _ = place(split_at, "hr_lo", [20, T], F32R)
        swa = Attend(
            "swa", "swa_out", T, META + P,
            lambda u, r, g: qs[r, u // 2, META + P * g:META + P * (g + 1)],
            lambda u, r, g: qs[r, 8 + u // 8, 0:T] if g else qs[r, 8 + u // 8, 0:META + P],
            lambda u, chunk, c: vrow[0:c, chunk, (2 * (u // 8) + u % 2) * HD:(2 * (u // 8) + u % 2) * HD + HD],
            lambda u: C("swa1"), lambda u: C("swa0"),
            ((4, 0, P, T + META), (4, P, P, META), (4, 2 * P, P, META + P), (5, 0, META, T),
             (5, P, META, 0)), (sm_s, pt_s, st_s))

        def dve_swa(dve, name):
            nc.vector.tensor_copy(sel_r[:].rearrange("p (a b) -> p a b", b=HD),
                                  ident[0:20, 0:20].unsqueeze(2).to_broadcast([20, 20, HD])
                                  ).then_inc(S("sel_ready"), 1)
            nc.vector.tensor_scalar(small[:, 1:2], prm_col("q_norm"), HD ** -0.5, None,
                                    ALU.mult).then_inc(S("qw_ready"), 1)
            dve_store(dve, name, qs)
            dve.wait_ge(S("hs_ready"), 1)
            dve_link(dve, nc.vector.reciprocal(hr20[:], hs20[:]))
            dve_link(dve, nc.vector.tensor_copy(hr_hi[:], hr20[:]))
            nc.vector.tensor_tensor(hr_lo[:], hr20[:], hr_hi[:].bitcast(F32),
                                    ALU.subtract).then_inc(S("hr_ready"), 1)
            dve.wait_ge(S("qw_ready"), 1)
            dve.wait_ge(evac_done, LIN[name].tile0 + 12)
            for f in range(10):
                dve.wait_ge(S("hn_done"), f + 1)
                nc.vector.scalar_tensor_tensor(
                    out=qs[:, f, :], in0=qs[:, f, :], scalar=small[:, 1:2] if f < 8 else prm_col("k_norm"),
                    in1=bank[f % 4][:, 0:T], op0=ALU.mult, op1=ALU.mult).then_inc(S("qk_ready"), 1)
            def meta_queries():
                m3 = smm[:].rearrange("p (u k) -> p u k", u=HEADS)
                dve.wait_ge(S("meta_scores"), 1)
                halves = smm[:].rearrange("p (t x k) -> p t x k", x=2, k=META)
                for x in range(2):
                    dve_link(dve, nc.vector.tensor_tensor(
                        halves[:, :, x, :], bank[7 - x][0:META, 0:P].rearrange("p (t k) -> p t k", k=META),
                        C("meta", META).unsqueeze(1).to_broadcast([META, HEADS // 2, META]), ALU.add))
                dve_link(dve, nc.vector.tensor_reduce(mst[:, 0, :], m3, AX_X, ALU.max))
                sinks = prm[0:META, PARAM_AT["sinks"][0]:PARAM_AT["sinks"][0] + HEADS]
                dve_link(dve, nc.vector.tensor_tensor(mst[:, 0, :], mst[:, 0, :], sinks, ALU.max))
                nc.vector.tensor_tensor(mst[:, 1, :], sinks, mst[:, 0, :], ALU.subtract).then_inc(S("meta_m"), 1)
                nc.vector.tensor_tensor(m3, m3, mst[:, 0, :].unsqueeze(2).to_broadcast([META, HEADS, META]),
                                        ALU.subtract).then_inc(S("meta_m"), 1)
                dve.wait_ge(S("meta_e"), 2)
                dve_link(dve, nc.vector.tensor_reduce(mst[:, 2, :], m3, AX_X, ALU.add))
                dve_link(dve, nc.vector.tensor_tensor(mst[:, 2, :], mst[:, 2, :], mst[:, 1, :], ALU.add))
                dve_link(dve, nc.vector.reciprocal(mst[:, 3, :], mst[:, 2, :]))
                nc.vector.tensor_tensor(m3, m3, mst[:, 3, :].unsqueeze(2).to_broadcast([META, HEADS, META]),
                                        ALU.mult).then_inc(S("meta_p"), 1)
                dve.wait_ge(S("meta_turned"), 1)
                nc.vector.tensor_copy(ptm[:], bank[7][0:META, 256:512]).then_inc(S("meta_pt"), 1)

            att_dve(dve, swa, after=meta_queries)

        def act_swa(act, name):
            act_store(act, name)
            act.wait_ge(S("hn_sum"), 1)
            nc.scalar.activation(hs20[:], bank[5][0:20, 0:T], ACT.Sqrt, bias=eps[0:20, 0:1],
                                 scale=1.0 / HD).then_inc(S("hs_ready"), 1)
            for j, (t0, c) in enumerate(KEYS):
                act.wait_ge(S("vt_done"), j + 1)
                nc.scalar.activation(vrow[0:c, j, :], bank[5 + (j + 1) % 3][0:c, 0:256],
                                     ACT.Copy).then_inc(S("vrow_ready"), 1)

            def meta_exps():
                act.wait_ge(S("meta_m"), 2)
                nc.scalar.activation(mst[:, 1, :], mst[:, 1, :], ACT.Exp).then_inc(S("meta_e"), 1)
                nc.scalar.activation(smm[:], smm[:], ACT.Exp).then_inc(S("meta_e"), 1)

            att_act(act, swa, after=meta_exps)

        def pool_swa(pool, name):
            for f in range(10):
                pool.wait_ge(evac_done, LIN[name].tile0 + f + 1)
                nc.gpsimd.tensor_tensor(sqs[:, f, :], qs[:, f, :], qs[:, f, :],
                                        ALU.mult).then_inc(S("sqs_ready"), 1)

        def pe_swa(pe, name):
            pe_linear(pe, name, 11)
            for f in range(10):
                pe.wait_ge(S("sqs_ready"), f + 1)
                mm = nc.tensor.matmul(bank[5][0:20, 0:T], C("head64")[:, 19 - 2 * f:39 - 2 * f],
                                      sqs[:, f, :], start=(f == 0), stop=(f == 9))
            mm.then_inc(S("hn_sum"), 1)
            pe_tile(pe, LIN[name], 11)
            pe.wait_ge(evac_done, LIN[name].tile0 + 12)
            for j, (t0, c) in enumerate(KEYS):
                if j == 2:
                    pe.wait_ge(S("hs_ready"), 1)
                for f in range(2):
                    tr = nc.tensor.transpose(bank[5 + (j + 1) % 3][0:c, f * P:(f + 1) * P],
                                             qs[:, 10 + f, t0:t0 + c], ident)
                tr.then_inc(S("vt_done"), 1)
            pe.wait_ge(S("sel_ready"), 1)
            pe.wait_ge(S("hr_ready"), 1)
            for f in range(10):
                if f >= 4:
                    pe.wait_ge(S("qk_ready"), f - 3)
                sel = sel_r[:, f * P:(f + 1) * P]
                nc.tensor.matmul(bank[f % 4][:, 0:T], sel, hr_hi[:], start=True, stop=False)
                nc.tensor.matmul(bank[f % 4][:, 0:T], sel, hr_lo[:], start=False,
                                 stop=True).then_inc(S("hn_done"), 1)
            pe.wait_ge(S("qk_ready"), 10)
            pe.wait_ge(S("vrow_ready"), 3)
            for u in range(HEADS):
                r = slice(HD * (u % 2), HD * (u % 2) + HD)
                t = u // 2
                mm = nc.tensor.matmul(bank[7 - u % 2][0:META, META * t:META * (t + 1)], qs[r, t, 0:META],
                                      qs[r, 8 + u // 8, 0:META], start=True, stop=True)
            mm.then_inc(S("meta_scores"), 1)

            def meta_turn(pe):
                pe.wait_ge(S("meta_p"), 1)
                for u in range(HEADS):
                    tr = nc.tensor.transpose(bank[7][0:META, 256 + META * u:256 + META * (u + 1)],
                                             smm[:, META * u:META * (u + 1)], ident[0:META, 0:META])
                tr.then_inc(S("meta_turned"), 1)

            att_pe(pe, swa, meta_turn)

        qm, vrow_m, bias_m, sm_m, pt_m, st_m = U([
            ("qm", [P, 24, SEQ]), ("vrow_m", [P, 2, D]), ("bias_m", [P, HEADS, 2 * P]),
            ("sm_m", [P, 3, 3 * P]), ("pt_m", [P, 2, 3 * P]), ("st_m", [P, HEADS, 10])], u_at)
        CAUSAL_TURNS = ((4, 0, P, 2 * P), (4, P, P, 0), (4, 2 * P, P, P))
        MOBA_SIDES = {}
        for pair in range(1, HEADS // 2):
            MOBA_SIDES[2 * pair - 2] = (3 * pair, 3 * pair + 1)
            MOBA_SIDES[2 * pair - 1] = (3 * pair + 2,)
        moba = Attend(
            "moba", "moba_out", 2 * P, P,
            lambda u, r, g: qm[r, u // 2, P * g:P * (g + 1)],
            lambda u, r, g: qm[r, 8 + u // 2, 0:P * (g + 1)],
            lambda u, chunk, c: vrow_m[:, chunk, u * HD:(u + 1) * HD],
            lambda u: bias_m[:, u, :], lambda u: bias_m[:, u, P:2 * P], CAUSAL_TURNS,
            (sm_m, pt_m, st_m), MOBA_SIDES)

        def load_bias(act, dst):
            act.dma_start(dst[:], bass.AP(rel_scratch.tensor, P - 1,
                                          [[VLEN - 1, P], [P * VLEN, HEADS], [1, 2 * P]])
                          ).then_inc(S("bias_loaded"), 16)

        def value_rows(pe, src, first, sem):
            for b in range(4):
                for j in range(4):
                    f = 4 * (b % 2) + j
                    tr = nc.tensor.transpose(bank[4 + b][:, j * P:(j + 1) * P],
                                             src[:, first + f, P * (b // 2):P * (b // 2 + 1)], ident)
                tr.then_inc(S(sem), 1)

        def act_value_rows(act, dst, sem, ready):
            for b in range(4):
                act.wait_ge(S(sem), b + 1)
                nc.scalar.activation(dst[:, b // 2, 512 * (b % 2):512 * (b % 2 + 1)], bank[4 + b][:],
                                     ACT.Copy).then_inc(S(ready), 1)

        def dve_moba(dve, name):
            lin = LIN[name]

            def tile(t):
                wait_tile(dve, lin, t)
                dst, n = qm[:, 8 * (t % 3) + t // 3, :], SEQ
                if t % 3 == 0:
                    nc.vector.scalar_tensor_tensor(out=dst, in0=tile_bank(lin, t)[:, 0:n],
                                                   scalar=HD ** -0.5, in1=rstd[:, 0:n], op0=ALU.mult,
                                                   op1=ALU.mult).then_inc(evac_done, 1)
                else:
                    nc.vector.tensor_tensor(dst, tile_bank(lin, t)[:, 0:n], rstd[:, 0:n],
                                            ALU.mult).then_inc(evac_done, 1)
                dve_rest(dve, lin.piece0 + t + AHEAD)

            dve_rstd(dve, name)
            for t in range(3):
                tile(t)
            dve.wait_ge(S("bias_loaded"), 16)
            att_dve(dve, moba, tile=tile)

        def act_moba(act, name):
            act.wait_ge(S("rel_stored"), 16)
            load_bias(act, bias_m)
            lin = LIN[name]

            def tile(t):
                act_round(act, lin.piece0 + t + AHEAD)

            def rows(pair):
                act.wait_ge(S("mv_turned"), pair + 1)
                nc.scalar.activation(vrow_m[:, :, pair * P:(pair + 1) * P],
                                     bank[6][:, SEQ:2 * SEQ].rearrange("p (c k) -> p c k", c=2),
                                     ACT.Copy).then_inc(S("mv_ready"), 1)

            tile(0)
            act_std(act, name)
            tile(1)
            tile(2)
            att_act(act, moba, tile, rows)

        def pe_moba(pe, name):
            lin = LIN[name]

            def rows(pair):
                pe.wait_ge(evac_done, lin.tile0 + 3 * pair + 3)
                if pair >= 1:
                    pe.wait_ge(S("mv_ready"), pair)
                if pair >= 2:
                    pe.wait_ge(y_lo_ready, Y0["moba_out"] + pair - 1)
                for c in range(2):
                    tr = nc.tensor.transpose(bank[6][:, SEQ + c * P:SEQ + (c + 1) * P],
                                             qm[:, 16 + pair, c * P:(c + 1) * P], ident)
                tr.then_inc(S("mv_turned"), 1)

            pe_linear(pe, name, 3)
            att_pe(pe, moba, tile=lambda t: pe_tile(pe, lin, t), rows=rows)

        def mlp_rounds(eng, lin, slot):
            for t in range(4):
                slot(t, 0)
            with eng.Fori(0, lin.tiles // 4 - 1) as i:
                for t in range(4, 8):
                    slot(t, i)

        def dve_mlp(dve, name):
            lin = LIN[name]

            def low(t, i):
                dve.wait_ge(a_hi_ready, ACT0[name] + t + 1 + 4 * i)
                nc.vector.tensor_tensor(m_lo[:, t + 4 * i, :], av[:, t % 2, 0:SEQ],
                                        m_hi[:, t + 4 * i, :].bitcast(F32),
                                        ALU.subtract).then_inc(a_lo_ready, 1)

            def slot(t, i):
                dve_rest(dve, lin.piece0 + t + AHEAD, i, 4)
                if t == 0:
                    dve_rstd(dve, name)
                wait_tile(dve, lin, t, i, 4)
                nc.vector.scalar_tensor_tensor(out=vr[:, t % 2, 0:SEQ], in0=tile_bank(lin, t)[:, 0:SEQ],
                                               scalar=0.0, in1=rstd[:, 0:SEQ], op0=ALU.max,
                                               op1=ALU.mult).then_inc(evac_done, 1)
                if t:
                    low(t - 1, i)

            mlp_rounds(dve, lin, slot)
            low(lin.tiles - 1, 0)

        def act_mlp(act, name):
            lin = LIN[name]

            def slot(t, i):
                act_round(act, lin.piece0 + t + AHEAD, i, 4)
                if t == 0:
                    act_std(act, name)
                else:
                    squares(t - 1, i)

            def squares(t, i):
                act.wait_ge(evac_done, lin.tile0 + t + 1 + 4 * i)
                nc.scalar.activation(av[:, t % 2, 0:SEQ], vr[:, t % 2, 0:SEQ],
                                     ACT.Square).then_inc(S("mlp_sq"), 1)
                nc.scalar.activation(m_hi[:, t + 4 * i, :], vr[:, t % 2, 0:SEQ],
                                     ACT.Square).then_inc(a_hi_ready, 1)

            mlp_rounds(act, lin, slot)
            squares(lin.tiles - 1, 0)

        (ds_, qq, kv, vrow_d, bias_d, sm_d, pt_d, st_d, b2) = U([
            ("ds_", [P, 6, SEQ]), ("qq", [P, 12, SEQ]), ("kv", [P, 16, SEQ]), ("vrow_d", [P, 2, D]),
            ("bias_d", [P, HEADS, 2 * P]), ("sm_d", [P, 3, 3 * P]), ("pt_d", [P, 2, 3 * P]),
            ("st_d", [P, HEADS, 10]), ("b2", [P, 2, 3 * P])], u_at)
        sqd, _ = place(u_at + 18 * SEQ, "sqd", [P, 4, SEQ])
        hs2, after = place(u_at + 18 * SEQ + 4 * SEQ, "hs2", [2, SEQ])
        hr2, _ = place(after, "hr2", [2, SEQ])
        rl, _ = place(u_at + 34 * SEQ + 2 * D + HEADS * 2 * P, "rl", [P, 2, 3 * P])
        score = sb_alias("score", [P, 3 * P], vr)
        pick = sb_alias("pick", [P, 3 * P], av)
        top8 = small[:, 24:40]
        head_w = small[:, 8:24]
        dsa = Attend(
            "dsa", "dsa_out", 2 * P, P,
            lambda u, r, g: qq[r, u // 2, P * g:P * (g + 1)],
            lambda u, r, g: kv[r, u // 2, 0:P * (g + 1)],
            lambda u, chunk, c: vrow_d[:, chunk, u * HD:(u + 1) * HD],
            lambda u: b2[:, u % 2, 0:2 * P], lambda u: b2[:, u % 2, 2 * P:3 * P], CAUSAL_TURNS,
            (sm_d, pt_d, st_d))

        def dve_dsa(dve, name):
            lin = LIN[name]
            dve_store(dve, name, ds_)
            dve.wait_ge(S("c_std"), 1)
            nc.vector.reciprocal(hr2[:], hs2[:]).then_inc(S("c_rec"), 1)
            dve.wait_ge(evac_done, lin.tile0 + 6)
            for f in range(4):
                dve.wait_ge(S("c_bc"), f // 2 + 1)
                nc.vector.scalar_tensor_tensor(
                    out=ds_[:, f, :], in0=ds_[:, f, :], scalar=prm_col("g_q" if f < 2 else "g_kv", f % 2),
                    in1=bank[5 + f // 2][:, 0:SEQ], op0=ALU.mult, op1=ALU.mult).then_inc(S("c_ready"), 1)
            for f in range(4):
                dve.wait_ge(y_hi_ready, Y0["dsa_q"] + f + 1)
                nc.vector.tensor_tensor(y_lo[:, f, META:T], ds_[:, f, :],
                                        y_hi[:, f, META:T].bitcast(F32), ALU.subtract).then_inc(y_lo_ready, 1)
            q = LIN["dsa_q"]
            for t in range(12):
                if t % 4 == 0:
                    dve_rest(dve, q.piece0 + t // 4 + AHEAD)
                wait_tile(dve, q, t)
                nc.vector.tensor_scalar(qq[:, t, :], tile_bank(q, t)[:, 0:SEQ],
                                        HD ** -0.5 if t < 8 else 1.0, None,
                                        ALU.mult).then_inc(evac_done, 1)
            dve.wait_ge(S("w_turned"), 1)
            nc.vector.tensor_copy(head_w, bank[4][:, 0:16]).then_inc(S("w_ready"), 1)
            dve.wait_ge(S("w_ready"), 1)
            groups = ((0, 2 * P, 8), (2 * P, P, 0))
            for hd in range(8):
                dve.wait_ge(S("relu_done"), hd + 1)
                for x, (c0, w, w0) in enumerate(groups):
                    prev = (C("causal")[:, 2 * P - w:2 * P] if hd == 0 else score[:, c0:c0 + w])
                    if hd:
                        dve.wait_ge(S("score_done"), 2 * hd - 1 + x)
                    nc.vector.scalar_tensor_tensor(
                        out=score[:, c0:c0 + w], in0=rl[:, hd % 2, c0:c0 + w],
                        scalar=head_w[:, w0 + hd:w0 + hd + 1], in1=prev, op0=ALU.mult,
                        op1=ALU.add).then_inc(S("score_done"), 1)
            kvl = LIN["dsa_kv"]
            rest = [kvl.piece0 + j + AHEAD for j in range(kvl.pieces)]
            for r in range(TOPK // 8):
                if r % 2 == 0:
                    dve_rest(dve, rest[r // 2])
                for x, (c0, w, _) in enumerate(groups):
                    if r == 0:
                        dve.wait_ge(S("score_done"), 15 + x)
                    else:
                        dve.wait_ge(S("taken"), 2 * r - 1 + x)
                    nc.vector.max(top8[:, 8 * x:8 * x + 8], score[:, c0:c0 + w]).then_inc(S("top8"), 1)
                for x, (c0, w, _) in enumerate(groups):
                    dve.wait_ge(S("top8"), 2 * r + 1 + x)
                    nc.vector.match_replace(score[:, c0:c0 + w], top8[:, 8 * x:8 * x + 8],
                                            score[:, c0:c0 + w], GONE).then_inc(S("taken"), 1)
            dve.wait_ge(S("taken"), TOPK // 4)
            nc.vector.tensor_scalar(pick[:], score[:], 0.5 * GONE, NEG, ALU.is_gt,
                                    ALU.mult).then_inc(S("pick_ready"), 1)

            def bias_ready(dve, u):
                dve.wait_ge(S("b2_ready"), 2 * u + 2)

            att_dve(dve, dsa, extra=bias_ready)

        def act_dsa(act, name):
            lin = LIN[name]
            load_bias(act, bias_d)
            act_store(act, name)
            act.wait_ge(S("c_sum"), 1)
            nc.scalar.activation(hs2[:], bank[4][0:2, 0:SEQ], ACT.Sqrt, bias=eps[0:2, 0:1],
                                 scale=1.0 / (2 * P)).then_inc(S("c_std"), 1)
            for f in range(4):
                act.wait_ge(S("c_ready"), f + 1)
                nc.scalar.activation(y_hi[:, f, META:T], ds_[:, f, :], ACT.Copy).then_inc(y_hi_ready, 1)
            q = LIN["dsa_q"]
            for j in range(q.pieces):
                act_round(act, q.piece0 + j + AHEAD)
            for hd in range(8):
                act.wait_ge(S("idx_done"), hd + 1)
                if hd >= 2:
                    act.wait_ge(S("score_done"), 2 * hd - 2)
                nc.scalar.activation(rl[:, hd % 2, :], bank[4 + hd % 4][:, 0:3 * P],
                                     ACT.Relu).then_inc(S("relu_done"), 1)
            kvl = LIN["dsa_kv"]
            act.wait_ge(evac_done, kvl.tile0)
            for t in range(16):
                if t % 4 == 0:
                    act_round(act, kvl.piece0 + t // 4 + AHEAD)
                wait_tile(act, kvl, t)
                nc.scalar.activation(kv[:, t, :], tile_bank(kvl, t)[:, 0:SEQ], ACT.Copy).then_inc(evac_done, 1)
            act_value_rows(act, vrow_d, "dv_turned", "dv_ready")
            att_act(act, dsa)

        def pool_dsa(pool, name):
            lin = LIN[name]
            for f in range(4):
                pool.wait_ge(evac_done, lin.tile0 + f + 1)
                nc.gpsimd.tensor_tensor(sqd[:, f, :], ds_[:, f, :], ds_[:, f, :],
                                        ALU.mult).then_inc(S("sqd_ready"), 1)
            pool.wait_ge(S("pick_ready"), 1)
            pool.wait_ge(S("bias_loaded"), 32)
            for u in range(HEADS):
                if u >= 2:
                    dsa.wait(pool, "max", 2 * (u - 2) + 2)
                nc.gpsimd.tensor_tensor(b2[:, u % 2, 0:2 * P], bias_d[:, u, :], pick[:, 0:2 * P],
                                        ALU.add).then_inc(S("b2_ready"), 1)
                nc.gpsimd.tensor_tensor(b2[:, u % 2, 2 * P:3 * P], bias_d[:, u, P:2 * P],
                                        pick[:, 2 * P:3 * P], ALU.add).then_inc(S("b2_ready"), 1)

        def pe_dsa(pe, name):
            pe_linear(pe, name, 5)
            for f in range(4):
                pe.wait_ge(S("sqd_ready"), f + 1)
                g = f // 2
                mm = nc.tensor.matmul(bank[4][0:2, 0:SEQ], C("head128")[:, 7 - g:9 - g], sqd[:, f, :],
                                      start=(f == 0), stop=(f == 3))
            mm.then_inc(S("c_sum"), 1)
            pe_tile(pe, LIN[name], 5)
            pe.wait_ge(S("c_rec"), 1)
            for g in range(2):
                nc.tensor.matmul(bank[5 + g][:, 0:SEQ], ident[0:2, g:g + 1].to_broadcast([2, P]), hr2[:],
                                 start=True, stop=True).then_inc(S("c_bc"), 1)
            pe.wait_ge(evac_done, LIN[name].tile0 + 6)
            for g in range(2):
                tr = nc.tensor.transpose(bank[4][:, 8 * g:8 * (g + 1)], ds_[0:8, 5, P * g:P * (g + 1)],
                                         ident[0:8, 0:8])
            tr.then_inc(S("w_turned"), 1)
            pe_linear(pe, "dsa_q")
            pe.wait_ge(evac_done, LIN["dsa_kv"].tile0)
            pe.wait_ge(S("w_ready"), 1)
            pe.wait_ge(S("c_ready"), 4)
            for hd in range(8):
                if hd >= 4:
                    pe.wait_ge(S("relu_done"), hd - 3)
                r = slice(HD * (hd % 2), HD * (hd % 2) + HD)
                bk = bank[4 + hd % 4]
                nc.tensor.matmul(bk[:, 0:2 * P], qq[r, 8 + hd // 2, P:2 * P], ds_[r, 4, 0:2 * P],
                                 start=True, stop=True)
                nc.tensor.matmul(bk[:, 2 * P:3 * P], qq[r, 8 + hd // 2, 0:P], ds_[r, 4, 0:P],
                                 start=True, stop=True).then_inc(S("idx_done"), 1)
            pe_linear(pe, "dsa_kv")
            pe.wait_ge(evac_done, LIN["dsa_kv"].tile0 + 16)
            pe.wait_ge(S("relu_done"), 8)
            value_rows(pe, kv, 8, "dv_turned")
            pe.wait_ge(S("dv_ready"), 4)
            att_pe(pe, dsa)

        def dve_final(dve):
            dve_rstd(dve, "final")
            for c in range(KD):
                nc.vector.scalar_tensor_tensor(out=fin[:, c, :], in0=h[:, c, META:T],
                                               scalar=prm_col("final", c), in1=rstd[:, 0:SEQ],
                                               op0=ALU.mult, op1=ALU.mult).then_inc(S("final_ready"), 1)

        SECTIONS = {"act": {}, "dve": {}, "pe": {}, "pool": {}}
        for nm in ORDER:
            if nm == "mix_in":
                fns = (act_mix, dve_mix, pe_mix, pool_mix)
            elif nm in PAIR0:
                fns = (act_gated, dve_gated, pe_linear, None)
            elif nm in RESID:
                fns = (act_resid, dve_resid, pe_linear, pool_resid)
            elif nm == "swa_in":
                fns = (act_swa, dve_swa, pe_swa, pool_swa)
            elif nm == "moba_in":
                fns = (act_moba, dve_moba, pe_moba, None)
            elif nm in ("mlp_up0", "mlp_up1"):
                fns = (act_mlp, dve_mlp, pe_linear, None)
            elif nm == "dsa_in":
                fns = (act_dsa, dve_dsa, pe_dsa, pool_dsa)
            else:
                fns = (None, None, None, None)
            for e, fn in zip(("act", "dve", "pe", "pool"), fns):
                SECTIONS[e][nm] = fn or (lambda eng, name: None)

        @block.sync
        def _(sp):
            def load(lin, g, i=0):
                slot, turn = at_piece(g, i, RING)
                if g >= RING:
                    sp.wait_ge(lo_ready, g - RING + 1 + i * RING)
                sp.dma_start(raw[:, slot, 0:lin.width],
                             weights[lin.name][g - lin.piece0 + i * RING]).then_inc(landed[slot], 16)

            for name in ORDER:
                if name == "mix_out":
                    sp.wait_ge(S("rel_ready"), 1)
                    sp.dma_start(rel_scratch, relv[:].unsqueeze(1).to_broadcast([HEADS, P, VLEN])
                                 ).then_inc(S("rel_stored"), 16)
                lin = LIN[name]
                g = lin.piece0
                if lin is LIN["mix_in"]:
                    load(lin, g)
                    for c in range(0, KD, 2):
                        sp.dma_start(h[:, c:c + 2, :], x_t[c:c + 2].rearrange("c p t -> p c t")
                                     ).then_inc(h_loaded[c // 2], 16)
                    load(lin, g + 1)
                    load(lin, g + 2)
                    sp.dma_start(cst[:], consts_d).then_inc(loaded, 16)
                    load(lin, g + 3)
                    g += RING
                rounds = (lin.piece0 + lin.pieces - g) // RING
                if rounds > 1:
                    with sp.Fori(0, rounds) as i:
                        for k in range(RING):
                            load(lin, g + k, i)
                    g += rounds * RING
                while g < lin.piece0 + lin.pieces:
                    load(lin, g)
                    g += 1

            for c in range(KD):
                sp.wait_ge(S("final_ready"), c + 1)
                sp.dma_start(out_t[c], fin[:, c, :]).then_inc(out_done, 16)
            sp.wait_ge(out_done, 16 * KD)

        @block.scalar
        def _(act):
            act.dma_start(prm[:], params_d).then_inc(S("prm_loaded"), 16)
            act_round(act, 0)
            act.wait_ge(S("prm_loaded"), 16)
            for c in range(KD):
                act.wait_ge(h_loaded[c // 2], 16)
                act_x_hi(act, "mix_in", c)
            for g in range(1, AHEAD):
                act_round(act, g)
            for name in ORDER:
                SECTIONS["act"][name](act, name)
            act_std(act, "final")

        @block.vector
        def _(dve):
            nc.vector.memset(eps[:], EPS).then_inc(eps_set, 1)
            nc.vector.memset(gb[:], 0.0).then_inc(eps_set, 1)
            dve_rest(dve, 0)
            dve.wait_ge(S("prm_loaded"), 16)
            for c in range(KD):
                dve.wait_ge(h_loaded[c // 2], 16)
                dve_x_lo(dve, "mix_in", c)
            for g in range(1, AHEAD):
                dve_rest(dve, g)
            dve.wait_ge(eps_set, 2)
            for name in ORDER:
                SECTIONS["dve"][name](dve, name)
            dve_final(dve)

        @block.tensor
        def _(pe):
            for name in ORDER:
                SECTIONS["pe"][name](pe, name)
            norm_sum(pe, "final")

        @block.gpsimd
        def _(pool):
            for c in range(KD):
                pool.wait_ge(h_loaded[c // 2], 16)
                pool_squares(pool, c)
            for name in ORDER:
                SECTIONS["pool"][name](pool, name)


def rel_bucket(dist):
    exact = BUCKETS // 2
    nf = np.maximum(dist, 1).astype(np.float32)
    ratio = np.log(nf / np.float32(exact)) / np.float32(np.log(P / exact))
    large = exact + (ratio * np.float32(BUCKETS - exact)).astype(np.int32)
    return np.where(dist < exact, dist, np.minimum(large, BUCKETS - 1))


def constants():
    out = np.zeros((P, NCONST), np.float32)

    def put(name, value):
        a, n = CONST_AT[name]
        out[:value.shape[0], a:a + n] = value.reshape(value.shape[0], n)

    i, j = np.arange(P)[:, None], np.arange(P)[None, :]
    put("ident", (i == j).astype(np.float32))
    put("ones", np.ones((P, P), np.float32))
    levels = np.zeros((P, 7, P), np.float32)
    for level in range(7):
        b = 1 << level
        levels[:, level] = (i // (2 * b) == j // (2 * b)) & (i // b % 2 == 0) & (j // b % 2 == 1)
    put("levels", levels)
    put("strict", (j > i).astype(np.float32))
    put("incl", (j >= i).astype(np.float32))
    c = np.arange(40)[None, :]
    put("head64", (c == 19 + i // HD).astype(np.float32))
    put("head128", np.broadcast_to(np.arange(15)[None, :] == 7, (P, 15)).astype(np.float32))
    dist = 2 * P - 1 - np.arange(VLEN)
    hot = (rel_bucket(np.maximum(dist, 0))[None, :] == np.arange(BUCKETS)[:, None]) & (dist >= 0)[None, :]
    put("onehot", hot.astype(np.float32))
    put("future", np.broadcast_to(np.where(dist < 0, NEG, 0.0)[None, :], (HEADS, VLEN)))
    for name, q0, n in (("swa1", META + P, T), ("swa0", META, META + P)):
        rel = q0 + np.arange(P)[:, None] - np.arange(n)[None, :]
        keep = (np.arange(n)[None, :] < META) | ((rel >= 0) & (rel < P))
        put(name, np.where(keep, 0.0, NEG))
    m = np.arange(META)
    put("meta", np.where(m[:, None] >= m[None, :], 0.0, NEG))
    put("causal", np.where(np.arange(2 * P)[None, :] <= P + np.arange(P)[:, None], 0.0, NEG))
    return out


def blocks(w, name):
    lin = LIN[name]
    t = w.reshape(lin.chunks, P, lin.tiles, P).transpose(2, 1, 0, 3)
    if lin.per_tile > 1:
        k = lin.chunks // lin.per_tile
        t = t.reshape(lin.tiles, P, lin.per_tile, k, P).transpose(0, 2, 1, 3, 4)
    if lin.per_piece > 1:
        t = t.reshape(lin.tiles // lin.per_piece, lin.per_piece, P, lin.chunks, P).transpose(0, 2, 1, 3, 4)
    return np.ascontiguousarray(t.reshape(lin.pieces, P, lin.width))


def by_column(v):
    v = v.reshape(-1, P)
    return v.T


SWA_ORDER = [h for t in range(8) for h in (t // 4 * 8 + t % 4, t // 4 * 8 + 4 + t % 4)]


def lay_out(a):
    w = a["mix_w_in"][0]
    sizes = [512, 512, 512, 1536, 512, 4, 4]
    at = [sum(sizes[:i]) for i in range(len(sizes) + 1)]
    gate_in, gate_out, a_h, qkv_w, z_w, beta_w, alpha_w = (w[:, at[i]:at[i + 1]] for i in range(7))
    rates = np.zeros((D, P), np.float32)
    rates[:, 0:4] = alpha_w
    rates[:, 32:36] = beta_w
    parts = [qkv_w, rates, z_w]
    for j in range(4):
        s = slice(j * P, (j + 1) * P)
        parts += [gate_in[:, s], a_h[:, s], gate_out[:, s]]
    mats = {"mix_in": np.concatenate(parts, 1), "mix_out": a["mix_w_out"][0]}
    for n in range(2):
        up = a["ffn_w_up"][n].reshape(D, 2, GATES, P).transpose(0, 2, 1, 3)
        mats[f"up{n}"] = up.reshape(D, 2 * DFF)
        mats[f"down{n}"] = a["ffn_w_down"][n]
        mats[f"mlp_up{n}"] = a["mlp_w_up_2"][n]
        mats[f"mlp_down{n}"] = a["mlp_w_down_2"][n]
    wq = a["swa_wq"][0].reshape(D, HEADS, HD)[:, SWA_ORDER].reshape(D, D)
    mats["swa_in"] = np.concatenate([wq, a["swa_wk"][0], a["swa_wv"][0]], 1)
    mats["swa_out"] = a["swa_wo"][0].reshape(HEADS, HD, D)[SWA_ORDER].reshape(D, D)
    qkv_w = a["moba_w_qkv_2"][0].reshape(D, 3, KD, P).transpose(0, 2, 1, 3)
    mats["moba_in"] = qkv_w.reshape(D, 3 * D)
    mats["moba_out"] = a["moba_w_o_2"][0]
    w = a["dsa_w_in_2"][0]
    heads_w = np.zeros((D, P), np.float32)
    heads_w[:, 0:8] = w[:, 576:584]
    mats["dsa_in"] = np.concatenate([w[:, 0:512], w[:, 512:576], w[:, 512:576], heads_w], 1)
    mats["dsa_q"] = np.concatenate([a["dsa_w_uq_2"][0], a["dsa_w_qi_2"][0]], 1)
    uk = a["dsa_w_uk_2"][0].transpose(2, 0, 1).reshape(2 * P, D)
    uv = a["dsa_w_uv_2"][0].transpose(1, 0, 2).reshape(2 * P, D)
    mats["dsa_kv"] = np.concatenate([uk, uv], 1)
    mats["dsa_out"] = a["dsa_w_o_2"][0]
    weights = {name: blocks(mats[name], name) for name in LIN}

    prm = np.zeros((P, NPARAM), np.float32)

    def put(name, value):
        at, n = PARAM_AT[name]
        prm[:value.shape[0], at:at + n] = value.reshape(value.shape[0], n)

    put("attn_w", by_column(a["attn_norm_w"]))
    put("ffn_w", by_column(a["ffn_norm_w"]))
    put("conv_a", by_column(a["conv_a_w"]))
    put("dn_conv", by_column(a["dn_conv_w"]))
    put("dn_norm", by_column(a["dn_norm_w"]))
    put("q_norm", np.concatenate([a["swa_q_norm_w"][0], a["swa_q_norm_w"][0]])[:, None])
    put("k_norm", np.concatenate([a["swa_k_norm_w"][0], a["swa_k_norm_w"][0]])[:, None])
    put("sinks", np.broadcast_to(a["swa_sinks"][0][SWA_ORDER][None, :], (P, HEADS)))
    put("ffn_conv", by_column(a["ffn_conv_w"]))
    put("ln_attn", by_column(a["ln_attn_2"]))
    put("ln_mlp", by_column(a["ln_mlp_2"]))
    put("g_q", by_column(a["dsa_g_q_2"]))
    put("g_kv", by_column(a["dsa_g_kv_2"]))
    put("final", by_column(a["final_norm_2"]))
    put("a_log", a["dn_a_log"][0][:, None])
    put("dt_bias", a["dn_dt_bias"][0][:, None])
    put("rel", a["rel_bias_2"])
    h0 = np.concatenate([a["meta_tokens"], a["x"][0]], 0)
    x_t = np.ascontiguousarray(h0.T).reshape(KD, P, T)
    return x_t, weights, prm


def kernel(**inputs):
    import concourse.bacc as bacc
    from concourse.bass_utils import run_bass_kernel_spmd

    a = {k: np.asarray(v) for k, v in inputs.items()}
    x_t, weights, prm = lay_out(a)
    nc = bacc.Bacc("TRN2", target_bir_lowering=False, num_devices=1)
    arrays = {"x_t": x_t, "prm": prm, "cst": constants()}
    arrays.update({f"w_{k}": v for k, v in weights.items()})
    ap = {k: nc.dram_tensor(k, v.shape, F32, kind="ExternalInput").ap() for k, v in arrays.items()}
    rel = nc.dram_tensor("rel_scratch", (HEADS, P, VLEN), F32, kind="Internal").ap()
    out = nc.dram_tensor("out", (KD, P, SEQ), F32, kind="ExternalOutput").ap()
    build(nc, ap["x_t"], {k: ap[f"w_{k}"] for k in weights}, ap["prm"], ap["cst"], rel, out)
    r = run_bass_kernel_spmd(nc, [arrays], core_ids=[0])
    return r.results[0]["out"].reshape(D, SEQ).T[None]
```
